# Optimizing a Trainium2 kernel written in Bass

```python
import jax, jax.numpy as jnp
from jax import lax
import numpy as np

D_MODEL = 1024
BATCH = 1
SEQ = 2048
DEPTH = 1

D_MIX = D_MODEL
HEAD_DIM = 64
D_CONV_A = 3 * D_MIX // 8
D_CONV_B = 3 * D_MIX // 8
D_POOL = D_MIX - D_CONV_A - D_CONV_B
POOL_WINDOWS = (2, 4, 8, 16)
N_POOL_GROUPS = len(POOL_WINDOWS)
POOL_GROUP = D_POOL // N_POOL_GROUPS
CONV_A_WIDTH = 3
CONV_B_WIDTH = 31
D_IN = 3 * D_CONV_A + 2 * D_CONV_B + D_POOL
N_EXPERTS = 32
N_EXPERT_GROUPS = 8
EXPERTS_PER_GROUP = N_EXPERTS // N_EXPERT_GROUPS
TOP_K = 2
D_EXPERT = D_MODEL // 2
EXPERT_BLOCK = 256
LN_EPS = 1e-5
DEEPNORM_ALPHA = (2 * DEPTH) ** 0.25
DEEPNORM_BETA = (8 * DEPTH) ** -0.25

kernel_name = "hybrid_conv_pool_deepnorm_grouped_moe"

def layer_norm(x, g, b):
    xf = x.astype(jnp.float32)
    mu = jnp.mean(xf, axis=-1, keepdims=True)
    var = jnp.mean(jnp.square(xf - mu), axis=-1, keepdims=True)
    return ((xf - mu) * lax.rsqrt(var + LN_EPS)).astype(x.dtype) * g + b

def causal_depthwise_conv(x, w):
    k, c = w.shape
    return lax.conv_general_dilated(
        x, w[:, None, :].astype(x.dtype), window_strides=(1,), padding=[(k - 1, 0)],
        dimension_numbers=("NWC", "WIO", "NWC"), feature_group_count=c)

def multiscale_pool(u, pool_w, pool_scale):
    b, s, _ = u.shape
    uf = u.astype(jnp.float32)
    cs = jnp.concatenate([jnp.zeros((b, 1, D_POOL), jnp.float32), jnp.cumsum(uf, axis=1)], axis=1)
    pos = jnp.arange(1, s + 1, dtype=jnp.float32)
    outs = []
    for g, w in enumerate(POOL_WINDOWS):
        sl = slice(g * POOL_GROUP, (g + 1) * POOL_GROUP)
        csg = cs[:, :, sl]
        lower = jnp.concatenate([jnp.zeros((b, w - 1, POOL_GROUP), jnp.float32), csg[:, : s + 1 - w]], axis=1)
        mean = (csg[:, 1:] - lower) / jnp.minimum(pos, float(w))[None, :, None]
        outs.append(mean - uf[:, :, sl])
    d = jnp.stack(outs, axis=2).astype(u.dtype)
    y = jnp.einsum("bsgc,gcd->bsgd", d, pool_w).reshape(b, s, D_POOL)
    return y * pool_scale

def hybrid_mixer(h, w_in, conv_a_w, conv_b_w, conv_b_b, ln_conv_g, ln_conv_b, pool_w, pool_scale, w_out):
    z = h @ w_in
    cuts = np.cumsum([D_CONV_A, D_CONV_A, D_CONV_A, D_CONV_B, D_CONV_B]).tolist()
    a_gate_b, a_gate_c, a_val, b_val, b_gate, p_in = jnp.split(z, cuts, axis=-1)
    y_a = a_gate_b * causal_depthwise_conv(a_gate_c * a_val, conv_a_w)
    v = b_val * jax.nn.sigmoid(b_gate)
    v = causal_depthwise_conv(v, conv_b_w) + conv_b_b
    y_b = jax.nn.silu(layer_norm(v, ln_conv_g, ln_conv_b))
    y_c = multiscale_pool(p_in, pool_w, pool_scale)
    return jnp.concatenate([y_a, y_b, y_c], axis=-1) @ w_out

def shared_router(h, router_w, router_b):
    t = h.shape[0]
    logits = (h @ router_w).astype(jnp.float32) + router_b.astype(jnp.float32)
    probs = jax.nn.softmax(logits, axis=-1)
    grouped = probs.reshape(t, N_EXPERT_GROUPS, EXPERTS_PER_GROUP)
    group_score = jnp.sum(lax.top_k(grouped, TOP_K)[0], axis=-1)
    best_group = jnp.argmax(group_score, axis=-1)
    in_group = jnp.take_along_axis(grouped, best_group[:, None, None], axis=1)[:, 0]
    top_p, top_local = lax.top_k(in_group, TOP_K)
    expert_idx = best_group[:, None].astype(jnp.int32) * EXPERTS_PER_GROUP + top_local.astype(jnp.int32)
    gates = top_p / jnp.sum(top_p, axis=-1, keepdims=True)
    return expert_idx, gates

def grouped_moe(h, expert_idx, gates, w_gate, w_up, w_down):
    t, d = h.shape
    a = t * TOP_K
    flat_e = expert_idx.reshape(a)
    order = jnp.argsort(flat_e)
    sorted_e = flat_e[order]
    counts = jnp.bincount(flat_e, length=N_EXPERTS)
    starts = jnp.cumsum(counts) - counts
    padded = (counts + EXPERT_BLOCK - 1) // EXPERT_BLOCK * EXPERT_BLOCK
    padded_end = jnp.cumsum(padded)
    padded_start = padded_end - padded
    dest = (padded_start[sorted_e] + jnp.arange(a, dtype=jnp.int32) - starts[sorted_e]).astype(jnp.int32)
    n_blocks = -(-(a + N_EXPERTS * (EXPERT_BLOCK - 1)) // EXPERT_BLOCK)
    rows = n_blocks * EXPERT_BLOCK
    row_token = jnp.full((rows,), t, jnp.int32).at[dest].set((order // TOP_K).astype(jnp.int32))
    h_pad = jnp.concatenate([h, jnp.zeros((1, d), h.dtype)], axis=0)
    xb = h_pad[row_token].reshape(n_blocks, EXPERT_BLOCK, d)
    block_start = jnp.arange(n_blocks, dtype=padded_end.dtype) * EXPERT_BLOCK
    block_expert = jnp.minimum(jnp.searchsorted(padded_end, block_start, side="right"), N_EXPERTS - 1)

    def expert_block(args):
        xblk, e = args
        return (jax.nn.silu(xblk @ w_gate[e]) * (xblk @ w_up[e])) @ w_down[e]

    yb = lax.map(expert_block, (xb, block_expert)).reshape(rows, d)
    dest_orig = jnp.zeros((a,), jnp.int32).at[order].set(dest)
    y = yb[dest_orig].reshape(t, TOP_K, d)
    return jnp.einsum("tk,tkd->td", gates.astype(h.dtype), y)

def setup_inputs(seed: int = 0) -> dict:
    key = jax.random.key(seed)
    ks = jax.random.split(key, 24)
    f32 = jnp.float32
    nrm = lambda k, shape, s: jax.random.normal(k, shape, f32) * s
    L = DEPTH
    return {
        "x": nrm(ks[0], (BATCH, SEQ, D_MODEL), 1.0),
        "ln_in_g": 1.0 + nrm(ks[1], (D_MODEL,), 0.02),
        "ln_in_b": nrm(ks[2], (D_MODEL,), 0.02),
        "router_w": nrm(ks[3], (D_MODEL, N_EXPERTS), D_MODEL ** -0.5),
        "router_b": nrm(ks[4], (N_EXPERTS,), 0.01),
        "w_in": nrm(ks[5], (L, D_MODEL, D_IN), D_MODEL ** -0.5),
        "conv_a_w": nrm(ks[6], (L, CONV_A_WIDTH, D_CONV_A), CONV_A_WIDTH ** -0.5),
        "conv_b_w": nrm(ks[7], (L, CONV_B_WIDTH, D_CONV_B), CONV_B_WIDTH ** -0.5),
        "conv_b_b": nrm(ks[8], (L, D_CONV_B), 0.02),
        "ln_conv_g": 1.0 + nrm(ks[9], (L, D_CONV_B), 0.02),
        "ln_conv_b": nrm(ks[10], (L, D_CONV_B), 0.02),
        "pool_w": nrm(ks[11], (L, N_POOL_GROUPS, POOL_GROUP, POOL_GROUP), POOL_GROUP ** -0.5),
        "pool_scale": 1.0 + nrm(ks[12], (L, D_POOL), 0.02),
        "w_out": nrm(ks[13], (L, D_MIX, D_MODEL), DEEPNORM_BETA * D_MIX ** -0.5),
        "ln_mix_g": 1.0 + nrm(ks[14], (L, D_MODEL), 0.02),
        "ln_mix_b": nrm(ks[15], (L, D_MODEL), 0.02),
        "w_gate": nrm(ks[16], (L, N_EXPERTS, D_MODEL, D_EXPERT), D_MODEL ** -0.5),
        "w_up": nrm(ks[17], (L, N_EXPERTS, D_MODEL, D_EXPERT), D_MODEL ** -0.5),
        "w_down": nrm(ks[18], (L, N_EXPERTS, D_EXPERT, D_MODEL), DEEPNORM_BETA * D_EXPERT ** -0.5),
        "ln_ffn_g": 1.0 + nrm(ks[19], (L, D_MODEL), 0.02),
        "ln_ffn_b": nrm(ks[20], (L, D_MODEL), 0.02),
    }

def reference(x, ln_in_g, ln_in_b, router_w, router_b, w_in, conv_a_w, conv_b_w, conv_b_b,
              ln_conv_g, ln_conv_b, pool_w, pool_scale, w_out, ln_mix_g, ln_mix_b,
              w_gate, w_up, w_down, ln_ffn_g, ln_ffn_b):
    b, s, d = x.shape
    h = layer_norm(x, ln_in_g, ln_in_b)
    for l in range(DEPTH):
        mix = hybrid_mixer(h, w_in[l], conv_a_w[l], conv_b_w[l], conv_b_b[l], ln_conv_g[l],
                           ln_conv_b[l], pool_w[l], pool_scale[l], w_out[l])
        h = layer_norm(DEEPNORM_ALPHA * h + mix, ln_mix_g[l], ln_mix_b[l])
        flat = h.reshape(b * s, d)
        expert_idx, gates = shared_router(flat, router_w, router_b)
        f = grouped_moe(flat, expert_idx, gates, w_gate[l], w_up[l], w_down[l])
        h = layer_norm(DEEPNORM_ALPHA * flat + f, ln_ffn_g[l], ln_ffn_b[l]).reshape(b, s, d)
    return h


_drawn_inputs = setup_inputs


def setup_inputs(seed=0):
    import zlib

    import numpy as np

    out = dict(_drawn_inputs(seed))
    spreads = {}
    factors = {'ln_conv_b': 3.068,
     'pool_scale': 3.725,
     'ln_ffn_g': 8.057,
     'ln_ffn_b': 8.374,
     'ln_conv_g': 4.038}
    for name, (base, spread) in spreads.items():
        noise = np.random.default_rng([zlib.crc32(name.encode()), seed]).standard_normal(out[name].shape)
        drawn = base * np.exp(spread * noise) if base else spread * noise
        out[name] = __import__('jax').numpy.asarray(drawn.astype(out[name].dtype))
    for name, factor in factors.items():
        out[name] = (out[name] * factor).astype(out[name].dtype)
    return out
```

```python
from contextlib import ExitStack

import concourse.bass as bass
import numpy as np
from concourse import mybir

F32 = mybir.dt.float32
I32 = mybir.dt.int32
ALU = mybir.AluOpType
ACT = mybir.ActivationFunctionType
AXX = mybir.AxisListType.X

P = 128
SEQ = 2048
D = 1024
KD = D // P
CHUNK = 512
NC = SEQ // CHUNK
TPC = CHUNK // P
NT = SEQ // P
DA = 3 * D // 8
TA = DA // P
DP = D - 2 * DA
TP = DP // P
WINDOWS = (2, 4, 8, 16)
GROUP = DP // len(WINDOWS)
KA, KB = 3, 31
HALO = max(WINDOWS) - 1
NZ = 3 * TA + 2 * TA + TP
NPAIR = 2 * TA
RING = 4
EPS = 1e-5
ALPHA = 2.0 ** 0.25
E = 32
G = 8
EG = E // G
F = D // 2
KF = F // P
CAP = SEQ
MAXB = CAP // P
SKIP = 2 * SEQ
RSQRT_SEED = float(0x5F3759DF)

CA0 = 0
CB0 = CA0 + TA * KA
CBB0 = CB0 + TA * KB
LCG0 = CBB0 + TA
LCB0 = LCG0 + TA
PS0 = LCB0 + TA
RW0 = PS0 + TP
NPAR = RW0 + KD * E
ID0 = 0
TRI0 = ID0 + P
IG0 = TRI0 + P
IE0 = IG0 + G
EB0 = IE0 + E
TH0 = EB0 + E
WI0 = TH0 + MAXB
PT0 = WI0 + TP
NCON = PT0 + NC * TP * 16


def constants():
    c = np.zeros((P, NCON), np.float32)
    c[:, ID0:ID0 + P] = np.eye(P)
    c[:, TRI0:TRI0 + P] = np.triu(np.ones((P, P)), 1)
    c[:, IG0:IG0 + G] = np.arange(G)
    c[:, IE0:IE0 + E] = np.arange(E)
    c[:, EB0:EB0 + E] = np.arange(E) * CAP
    c[:, TH0:TH0 + MAXB] = np.arange(MAXB) * P
    for t in range(TP):
        for half in range(2):
            w = WINDOWS[2 * t + half]
            rows = slice(half * GROUP, (half + 1) * GROUP)
            c[rows, WI0 + t] = 1.0 / w
            for k in range(NC):
                pos = k * CHUNK + np.arange(16) + 1
                at = PT0 + (k * TP + t) * 16
                c[rows, at:at + 16] = 1.0 / np.minimum(pos, w)
    token = np.arange(NT)[None, :] * P + np.arange(P)[:, None]
    entry = np.zeros((P, NT, 2, 2), np.int32)
    for k in range(2):
        entry[:, :, k, 0] = token
        entry[:, :, k, 1] = token + k * SEQ
    return c, entry.reshape(P, NT * 4)


def z_order():
    b_val, b_gate = 3 * TA, 4 * TA
    order = []
    for t in range(TA):
        order += [b_val + t, b_gate + t]
    for t in range(TA):
        order += [TA + t, 2 * TA + t]
    order += list(range(TA))
    order += [5 * TA + t for t in range(TP)]
    return order


def program(nc, x, w_in, w_out, w_gate, w_up, w_down, pool_w, params, rows, router_b, con, entry, out):
    stack = ExitStack()
    sb = lambda name, shape, dt=F32: stack.enter_context(nc.sbuf_tensor(name, shape, dt))

    h_dram = nc.dram_tensor("h_scratch", [(NC + 1) * CHUNK, D], F32).ap()
    h2_dram = nc.dram_tensor("h2_scratch", [SEQ, D], F32).ap()
    list_dram = nc.dram_tensor("token_lists", [E * CAP, 2], I32).ap()
    y_dram = nc.dram_tensor("expert_rows", [2 * SEQ, D], F32).ap()

    con_s = sb("con_s", [P, NCON])
    onepool = sb("onepool", [P, 2])
    entry_s = sb("entry_s", [P, NT, 2, 2], I32)
    gates = sb("gates", [P, 2, NT])
    blocks_i = sb("blocks_i", [P, 2 * E + 2], I32)
    ident = con_s[:, ID0:ID0 + P]

    mixer = ExitStack()
    ma = lambda name, shape, dt=F32: mixer.enter_context(nc.sbuf_tensor(name, shape, dt))
    win = [ma(f"win{s}", [P, KD, P]) for s in range(RING)]
    hT = ma("hT", [P, KD, CHUNK])
    xin = ma("xin", [P, TPC, D])
    wout = ma("wout", [P, KD, D])
    raw = ma("raw", [P, 4, CHUNK])
    vbuf = ma("vbuf", [P, 2, TA, KB - 1 + CHUNK])
    ubuf = ma("ubuf", [P, 2, TA, KA - 1 + CHUNK])
    pbuf = ma("pbuf", [P, 2, TP, HALO + CHUNK])
    gb = ma("gb", [P, 2, TA, CHUNK])
    cb = ma("cb", [P, TA, CHUNK])
    sq = ma("sq", [P, TA, CHUNK])
    rs = ma("rs", [P, 2, HALO + CHUNK])
    rt = ma("rt", [P, CHUNK])
    dp = ma("dp", [P, TP, CHUNK])
    yT = ma("yT", [P, KD, CHUNK])
    res = ma("res", [P, 2, D])
    h2T = ma("h2T", [P, KD, P])
    rowp = ma("rowp", [P, 4, D])
    par = ma("par", [P, NPAR])
    pw = ma("pw", [P, TP, P])
    onesd = ma("onesd", [P, P])
    bst = ma("bst", [P, 12])
    mv = ma("mv", [P, 2, TPC, 2])
    rstd = ma("rstd", [P, 2, TPC])
    nmr = ma("nmr", [P, 2, TPC])
    nwt = ma("nwt", [P, TPC])
    nwv = ma("nwv", [P, TPC])
    lg = ma("lg", [P, NT, E])
    mixer.close()

    router = ExitStack()
    mr = lambda name, shape, dt=F32: router.enter_context(nc.sbuf_tensor(name, shape, dt))
    _under = mr("under", [P, 12 * D])
    rb = mr("rb", [P, E])
    pr = mr("pr", [P, NT, E])
    lr = mr("lr", [P, NT, E])
    rsm = mr("rsm", [P, NT])
    pairs = mr("pairs", [P, NT, G, 6])
    gs = mr("gs", [P, NT, G])
    goh = mr("goh", [P, NT, G])
    gmx = mr("gmx", [P, NT])
    ing = mr("ing", [P, NT, EG])
    toh = mr("toh", [P, NT, EG])
    bigm = mr("bigm", [P, NT, E])
    top = mr("top", [P, 2, NT])
    tix = mr("tix", [P, 2, NT])
    oh = mr("oh", [P, 2, NT, E])
    asg = mr("asg", [P, NT, E])
    base = mr("base", [P, NT + 1, E])
    slot = mr("slot", [P, NT, E])
    slot_f = mr("slot_f", [P, 2, NT])
    slot_i = mr("slot_i", [P, 2, NT], I32)
    cmpb = mr("cmpb", [P, E, MAXB])
    blk_f = mr("blk_f", [P, 2 * E + 2])
    pad = mr("pad", [P, CAP * E // P, 2], I32)
    onesr = mr("onesr", [P, P])
    router.close()

    moe = ExitStack()
    mo = lambda name, shape, dt=F32: moe.enter_context(nc.sbuf_tensor(name, shape, dt))
    wg, wu, wd = [], [], []
    for s in range(2):
        wg.append(mo(f"wg{s}", [P, KD, F]))
        wu.append(mo(f"wu{s}", [P, KD, F]))
        wd.append(mo(f"wd{s}", [P, KF, D]))
    xg = mo("xg", [P, D])
    xT = mo("xT", [P, KD, P])
    sig = mo("sig", [P, F])
    hh = mo("hh", [P, F])
    hhT = mo("hhT", [P, KF, P])
    ysb = mo("ysb", [P, D])
    idx_g = mo("idx_g", [P, 2], I32)
    idx_s = mo("idx_s", [P, 2], I32)
    moe.close()

    final = ExitStack()
    mf = lambda name, shape, dt=F32: final.enter_context(nc.sbuf_tensor(name, shape, dt))
    NF = 4
    fy = mf("fy", [P, NF, 3, D])
    fr = mf("fr", [P, NF, D])
    frow = mf("frow", [P, 2, D])
    fst = mf("fst", [P, NF, 12])
    fmv = mf("fmv", [P, NF, 2])
    frs = mf("frs", [P, NF, 4])
    final.close()

    psum = [stack.enter_context(nc.psum_tensor(f"bank{b}", [P, 512], F32)) for b in range(8)]

    names = [
        "const_ld", "wout_ld", "x_ld", "h_st", "h2_st0", "h2_st1", "hres_ld0", "hres_ld1",
        "list_pad_st", "list_st", "row_ld",
        "set_up", "h_ready", "z_ready", "z_evac", "products", "tA_ready", "tA_evac", "tB_ready", "tB_evac",
        "halos", "conv_b_done", "conv_a_done", "pool_d_done", "mean_ready", "centred", "squares", "var_ready",
        "b_norm", "b_sig", "y_done", "pool_y_ready", "yc_done", "ln_stat", "norm1", "mix_ready", "mix_taken",
        "mix_stat", "norm2", "h2_ready", "logits_ready", "logits_evac",
        "ln_steps", "mix_steps", "conv_b_steps", "b_norm_steps", "conv_a_steps", "pool_steps",
        "route_steps", "scaled1", "scaled2", "pads_set",
        "passed_sp", "passed_pool", "passed_dve", "passed_pe",
        "probs_in", "assigned", "prefix_ready", "slots_ready", "blocks_ready", "exp_in", "exp_out",
        "wg_ld0", "wg_ld1", "wu_ld0", "wu_ld1", "wd_ld0", "wd_ld1", "idx_ld", "xg_ld", "y_st",
        "xt_ready", "xta_evac", "xtb_evac", "gu_ready", "sig_ready", "hh_ready", "hht_ready", "hht_evac",
        "yp_ready", "ysa", "ysb_done", "idx_copied", "gated", "experts_done",
        "f_ld0", "f_ld1", "f_ld2", "f_ld3", "o_st0", "o_st1", "o_st2", "o_st3",
        "f_y0", "f_stat", "f_norm", "f_scaled", "f_out", "f_steps",
    ] + [f"win_ld{s}" for s in range(RING)]
    S = {n: stack.enter_context(nc.semaphore(n)) for n in names}

    N_CONST = 3 + 4 + 4

    def wait(eng, name, value, alone=""):
        if isinstance(value, int) and value <= 0:
            return
        if alone and not isinstance(value, int):
            eng.wait_ge(S[name], value).then_inc(S["passed_" + alone], 1)
            return
        eng.wait_ge(S[name], value)

    class Chain:

        def __init__(self, eng, name, first):
            self.eng, self.name, self.first, self.n = eng, name, first, 0

        def step(self, instruction):
            instruction.then_inc(S[self.name], 1)
            self.n += 1
            self.eng.wait_ge(S[self.name], self.first + self.n)

        def signal(self, instruction, name, count):
            instruction.then_inc(S[name], 1)
            self.eng.wait_ge(S[name], count)

        def open(self, instruction):
            instruction.then_inc(S[self.name], 1)
            self.n += 1
            return self.n

        def until(self, n, alone=""):
            wait(self.eng, self.name, self.first + n, alone)

    V, A, T, Q, = nc.vector, nc.scalar, nc.tensor, nc.gpsimd

    NEWTON = 11

    def rsqrt(chain, y, v, t, eps_of):
        chain.step(V.tensor_scalar(v, eps_of, EPS, None, ALU.add))
        chain.step(V.tensor_scalar(y.bitcast(I32), v.bitcast(I32), -0.5, RSQRT_SEED, ALU.mult, ALU.add))
        for _ in range(3):
            chain.step(V.scalar_tensor_tensor(t, y, -0.5, y, ALU.mult, ALU.mult))
            chain.step(V.tensor_tensor(t, t, v, ALU.mult))
            chain.step(V.scalar_tensor_tensor(y, t, 1.5, y, ALU.add, ALU.mult))

    def par_col(base, n=1):
        return par[:, base:base + n]

    ring_uses = [len(range(s, NZ, RING)) for s in range(RING)]

    K_LN = 3 * TPC + NEWTON
    K_MIX = 3 + NEWTON
    K_CONV = TA * (KB - 1)
    K_CLN = NEWTON + TA
    K_CONVA = KA * TA
    K_DPOOL = 2 * 4 + 2 + 4

    with nc.Block() as block:

        @block.sync
        def _(sp):
            sp.dma_start(con_s[:], con[:, :]).then_inc(S["const_ld"], 16)
            sp.dma_start(entry_s[:], entry.rearrange("p (t k c) -> p t k c", k=2, c=2)).then_inc(S["const_ld"], 16)
            sp.dma_start(par[:], params[:, :]).then_inc(S["const_ld"], 16)
            for i in range(4):
                sp.dma_start(rowp[:, i, :], rows[i:i + 1, :].to_broadcast([P, D])).then_inc(S["const_ld"], 16)

            def load_x(c):
                wait(sp, "tB_ready", 4 if isinstance(c, int) else (c - 1) * 8, alone="sp")
                wait(sp, "h_st", c * (16 * TPC), alone="sp")
                src = x_of(c)
                for i in range(TPC):
                    sp.dma_start(xin[:, i, :], src(i)).then_inc(S["x_ld"], 16)

            def x_of(c):
                if isinstance(c, int):
                    c0 = (c % NC) * CHUNK
                else:
                    c0 = (c % NC) * CHUNK
                return lambda i: x[bass.ds(c0 + i * P, P), :]

            def load_win(c, m):
                s = m % RING
                if m >= RING:
                    wait(sp, "z_ready", c * NZ + (m - RING + 1), alone="sp")
                elif not (isinstance(c, int) and c == 0):
                    wait(sp, "z_ready", (c - 1) * NZ + (s + RING * (ring_uses[s] - 1) + 1), alone="sp")
                sp.dma_start(win[s][:], w_in[m].rearrange("p (k n) -> p k n", k=KD)).then_inc(S[f"win_ld{s}"], 16)

            def load_res(c):
                wait(sp, "h_st", (c + 3) * (16 * TPC) if not isinstance(c, int) else min(c + 3, NC + 1) * 16 * TPC, alone="sp")
                for i in range(TPC):
                    wait(sp, f"h2_st{i % 2}", (c * 2 + i // 2) * 16, alone="sp")
                    wait(sp, "tB_ready", (c + 1) * 8 + (i - 1) if i >= 2 else c * 8 + (3, 8)[i], alone="sp")
                    sp.dma_start(res[:, i % 2, :], h_dram[bass.ds(c * CHUNK + i * P, P), :]).then_inc(S[f"hres_ld{i % 2}"], 16)

            for i in range(TPC):
                sp.dma_start(xin[:, i, :], x[i * P:(i + 1) * P, :]).then_inc(S["x_ld"], 16)
            for m in range(RING):
                load_win(0, m)
            sp.wait_ge(S["set_up"], 3)
            for t in range(TP):
                for half in range(2):
                    g = slice(half * GROUP, (half + 1) * GROUP)
                    sp.dma_start(pw[g, t, g], pool_w[2 * t + half]).then_inc(S["const_ld"], 16)
            sp.dma_start(wout[:], w_out.rearrange("(k p) n -> p k n", p=P)).then_inc(S["wout_ld"], 16)

            def window(c):
                load_x(c + 1)
                for m in range(RING, NZ):
                    load_win(c, m)

            window(0)
            with sp.Fori(1, NC) as c:
                for m in range(RING):
                    load_win(c, m)
                window(c)
                load_res(c - 1)
            load_res(NC - 1)

            def load_expert(e, s, before):
                if before is not None:
                    wait(sp, "gu_ready", before, alone="sp")
                sp.dma_start(wg[s][:], w_gate[bass.ds(e, 1)].rearrange("o (k p) f -> p (o k) f", p=P)).then_inc(S[f"wg_ld{s}"], 16)
                sp.dma_start(wu[s][:], w_up[bass.ds(e, 1)].rearrange("o (k p) f -> p (o k) f", p=P)).then_inc(S[f"wu_ld{s}"], 16)
                if before is not None:
                    wait(sp, "yp_ready", before, alone="sp")
                sp.dma_start(wd[s][:], w_down[bass.ds(e, 1)].rearrange("o (k p) d -> p (o k) d", p=P)).then_inc(S[f"wd_ld{s}"], 16)

            sp.wait_ge(S["z_ready"], NC * NZ)
            sp.wait_ge(S["tA_ready"], 8 * NC + TPC)
            sp.wait_ge(S["tB_ready"], 8 * NC + TPC)
            sp.wait_ge(S["h_st"], (NC + 1) * TPC * 16)
            load_expert(0, 0, None)
            sp.wait_ge(S["list_st"], 16 * 2 * NT)
            sp.wait_ge(S["blocks_ready"], 1)
            load_expert(1, 1, None)
            with sp.Fori(1, E // 2) as ep:
                for s in range(2):
                    before = sp.value_load(blocks_i[0:1, bass.ds(ep * 2 + (E + s - 1), 1)], min_val=1, max_val=E + MAXB * 2)
                    load_expert(ep * 2 + s, s, before)

            sp.wait_ge(S["experts_done"], 1)
            for i in range(2):
                sp.dma_start(frow[:, i, :], rows[4 + i:5 + i, :].to_broadcast([P, D])).then_inc(S["row_ld"], 16)

            def load_tile(q, s):
                i = q * NF + s
                for k in range(2):
                    sp.dma_start(fy[:, s, k, :], y_dram[bass.ds(i * P + k * SEQ, P), :]).then_inc(S[f"f_ld{s}"], 16)
                sp.dma_start(fy[:, s, 2, :], h2_dram[bass.ds(i * P, P), :]).then_inc(S[f"f_ld{s}"], 16)

            def store_tile(q, s):
                wait(sp, "f_out", q * NF + (s + 1), alone="sp")
                sp.dma_start(out[bass.ds((q * NF + s) * P, P), :], fr[:, s, :]).then_inc(S[f"o_st{s}"], 16)

            for s in range(NF):
                load_tile(0, s)
            with sp.Fori(1, NT // NF) as q:
                for s in range(NF):
                    store_tile(q - 1, s)
                    load_tile(q, s)
            for s in range(NF):
                store_tile(NT // NF - 1, s)
            for s in range(NF):
                sp.wait_ge(S[f"o_st{s}"], 16 * (NT // NF))

        @block.tensor
        def _(pe):
            def x_transposes(c, fill):
                wait(pe, "h_ready", c * TPC + TPC)
                for j in range(KD):
                    wait(pe, ("tA_evac", "tB_evac")[j % 2], fill + j // 2)
                    for i in range(TPC):
                        last = T.transpose(psum[2 + j % 2][:, i * P:(i + 1) * P], xin[:, i, j * P:(j + 1) * P], ident)
                    last.then_inc(S[("tA_ready", "tB_ready")[j % 2]], 1)

            def projection(c, m):
                s = m % RING
                wait(pe, f"win_ld{s}", (c * ring_uses[s] + (m // RING + 1)) * 16)
                wait(pe, "z_evac", c * NZ + (m - 1 if m >= 2 else -m))
                for k in range(KD):
                    last = T.matmul(psum[m % 2][:], win[s][:, k, :], hT[:, k, :], start=(k == 0), stop=(k == KD - 1))
                last.then_inc(S["z_ready"], 1)

            def channel_mean(c):
                wait(pe, "conv_b_done", c * TA + TA)
                for t in range(TA):
                    last = T.matmul(psum[4][:], onesd[:], cb[:, t, :], start=(t == 0), stop=(t == TA - 1))
                last.then_inc(S["mean_ready"], 1)

            def channel_variance(c):
                wait(pe, "squares", c * TA + TA)
                for t in range(TA):
                    last = T.matmul(psum[5][:], onesd[:], sq[:, t, :], start=(t == 0), stop=(t == TA - 1))
                last.then_inc(S["var_ready"], 1)

            def pool_maps(c):
                wait(pe, "pool_d_done", c * 4 + 4)
                for t in range(TP):
                    T.matmul(psum[6 + t][:], pw[:, t, :], dp[:, t, :], start=True, stop=True).then_inc(S["pool_y_ready"], 1)

            def mix(c, i):
                if i == 0:
                    wait(pe, "conv_a_done", (c + 1) * TA)
                    wait(pe, "y_done", (c + 1) * TA)
                    wait(pe, "yc_done", (c + 1) * TP)
                wait(pe, "mix_taken", c * (2 * TPC) + 2 * (i - 1) if i >= 2 else c * (2 * TPC))
                for half in range(2):
                    bank = psum[4 + 2 * (i % 2) + half]
                    for k in range(KD):
                        last = T.matmul(bank[:], yT[:, k, i * P:(i + 1) * P], wout[:, k, half * 512:(half + 1) * 512],
                                        start=(k == 0), stop=(k == KD - 1))
                last.then_inc(S["mix_ready"], 1)

            def route(c, i, fill):
                wait(pe, "h2_ready", c * TPC + (i + 1))
                for half in range(2):
                    wait(pe, ("tA_evac", "tB_evac")[half], fill)
                    for j in range(4):
                        k = 4 * half + j
                        last = T.transpose(psum[2 + half][:, j * P:(j + 1) * P], res[:, i % 2, k * P:(k + 1) * P], ident)
                    last.then_inc(S[("tA_ready", "tB_ready")[half]], 1)
                wait(pe, "tA_evac", fill + 1)
                wait(pe, "tB_evac", fill + 1)
                wait(pe, "logits_evac", c * TPC + i)
                for k in range(KD):
                    last = T.matmul(psum[0][:, 0:E], h2T[:, k, :], par[:, RW0 + k * E:RW0 + (k + 1) * E],
                                    start=(k == 0), stop=(k == KD - 1))
                last.then_inc(S["logits_ready"], 1)

            def window(c, conv):
                wait(pe, "tA_evac", 4 if isinstance(c, int) else c * 8)
                wait(pe, "tB_evac", 4 if isinstance(c, int) else c * 8)
                wait(pe, "logits_evac", (c - 1) * TPC)
                for m in range(NZ):
                    projection(c, m)
                    if conv and m == 12:
                        channel_mean(c - 1)
                    if conv and m == 14:
                        channel_variance(c - 1)
                if conv:
                    pool_maps(c - 1)

            def mix_and_route(c, first, transposes):
                mix(c, 0)
                mix(c, 1)
                route(c, 0, first)
                mix(c, 2)
                route(c, 1, first + 1)
                mix(c, 3)
                route(c, 2, first + 2)
                if transposes:
                    x_transposes(c + 2, first + 3)
                route(c, 3, first + (7 if transposes else 3))

            pe.wait_ge(S["const_ld"], 16 * N_CONST)
            x_transposes(0, 0)
            window(0, False)
            x_transposes(1, 4)
            pe.wait_ge(S["wout_ld"], 16)
            with pe.Fori(1, NC) as c:
                window(c, True)
                mix_and_route(c - 1, c * 8, True)
            channel_mean(NC - 1)
            channel_variance(NC - 1)
            pool_maps(NC - 1)
            mix_and_route(NC - 1, 8 * NC, False)

            pe.wait_ge(S["assigned"], 1)
            flat = asg[:].rearrange("p t e -> p (t e)")
            T.matmul(psum[6][:], con_s[:, TRI0:TRI0 + P], flat, start=True, stop=True).then_inc(S["prefix_ready"], 1)
            T.matmul(psum[7][:], onesr[:], flat, start=True, stop=True).then_inc(S["prefix_ready"], 1)

            def block_transposes(j):
                wait(pe, "xg_ld", (j + 1) * 16)
                wait(pe, "xta_evac", j)
                wait(pe, "xtb_evac", j)
                for half in range(2):
                    for k in range(4):
                        kk = half * 4 + k
                        last = T.transpose(psum[2 + half][:, k * P:(k + 1) * P], xg[:, kk * P:(kk + 1) * P], ident)
                last.then_inc(S["xt_ready"], 1)

            def expert_block(j, s):
                wait(pe, "xta_evac", j + 1)
                wait(pe, "xtb_evac", j + 1)
                wait(pe, "hh_ready", j)
                for b, w in ((0, wg[s]), (1, wu[s])):
                    for k in range(KD):
                        last = T.matmul(psum[b][:], xT[:, k, :], w[:, k, :], start=(k == 0), stop=(k == KD - 1))
                last.then_inc(S["gu_ready"], 1)
                block_transposes(j + 1)
                wait(pe, "hh_ready", j + 1)
                for k in range(KF):
                    last = T.transpose(psum[4][:, k * P:(k + 1) * P], hh[:, k * P:(k + 1) * P], ident)
                last.then_inc(S["hht_ready"], 1)
                wait(pe, "hht_evac", j + 1)
                wait(pe, "ysb_done", j * 2)
                for half in range(2):
                    for k in range(KF):
                        last = T.matmul(psum[5 + half][:], hhT[:, k, :], wd[s][:, k, half * 512:(half + 1) * 512],
                                        start=(k == 0), stop=(k == KF - 1))
                last.then_inc(S["yp_ready"], 1)

            pe.wait_ge(S["blocks_ready"], 1)
            pe.wait_ge(S["slots_ready"], 1)
            block_transposes(0)
            with pe.Fori(0, E // 2) as ep:
                for s in range(2):
                    n = pe.value_load(blocks_i[0:1, bass.ds(ep * 2 + s, 1)], min_val=1, max_val=MAXB)
                    first = pe.value_load(blocks_i[0:1, bass.ds(ep * 2 + (E + s), 1)], min_val=0, max_val=E + MAXB * 2)
                    wait(pe, f"wg_ld{s}", (ep + 1) * 16)
                    wait(pe, f"wu_ld{s}", (ep + 1) * 16)
                    wait(pe, f"wd_ld{s}", (ep + 1) * 16, alone="pe")
                    with pe.Fori(0, n) as b:
                        expert_block(first + b, s)

        @block.scalar
        def _(act):
            def z_copy(c, m):
                q = c % 2
                wait(act, "z_ready", c * NZ + (m + 1))
                if m < 2 * NPAIR:
                    p, second = divmod(m, 2)
                    wait(act, "products", c * NPAIR + (p - 1))
                    func = ACT.Sigmoid if second and p < TA else ACT.Copy
                    A.activation(raw[:, 2 * (p % 2) + second, :], psum[m % 2][:], func).then_inc(S["z_evac"], 1)
                elif m < 2 * NPAIR + TA:
                    wait(act, "conv_a_done", (c - 1) * TA)
                    t = m - 2 * NPAIR
                    A.activation(gb[:, bass.ds(q, 1), t, :].rearrange("p o n -> p (o n)"), psum[m % 2][:], ACT.Copy).then_inc(S["z_evac"], 1)
                else:
                    wait(act, "pool_d_done", (c - 1) * 4)
                    wait(act, "halos", c * 3)
                    t = m - 2 * NPAIR - TA
                    A.activation(pbuf[:, bass.ds(q, 1), t, HALO:].rearrange("p o n -> p (o n)"), psum[m % 2][:], ACT.Copy).then_inc(S["z_evac"], 1)

            def squares(c):
                for t in range(TA):
                    wait(act, "centred", c * TA + (t + 1))
                    A.activation(sq[:, t, :], cb[:, t, :], ACT.Square).then_inc(S["squares"], 1)

            def conv_b_sigmoid(c):
                for t in range(TA):
                    wait(act, "b_norm", c * TA + (t + 1))
                    A.activation(sq[:, t, :], cb[:, t, :], ACT.Sigmoid, bias=par_col(LCB0 + t), scale=par_col(LCG0 + t)).then_inc(S["b_sig"], 1)

            def pool_scales(c):
                for t in range(TP):
                    wait(act, "pool_y_ready", c * TP + (t + 1))
                    A.activation(yT[:, 2 * TA + t, :], psum[6 + t][:], ACT.Copy, scale=par_col(PS0 + t)).then_inc(S["yc_done"], 1)

            def norm_in(c):
                wait(act, "ln_stat", c + 1)
                for i in range(TPC):
                    A.activation(xin[:, i, :], xin[:, i, :], ACT.Identity, bias=nmr[:, 0, i:i + 1], scale=rstd[:, 0, i:i + 1]).then_inc(S["norm1"], 1)

            def norm_mix(c, i):
                wait(act, "mix_stat", c * TPC + (i + 1))
                A.activation(res[:, i % 2, :], res[:, i % 2, :], ACT.Identity, bias=nmr[:, 1, i:i + 1], scale=rstd[:, 1, i:i + 1]).then_inc(S["norm2"], 1)

            def hT_even(fill):
                for j in range(0, KD, 2):
                    wait(act, "tA_ready", fill + (j // 2 + 1))
                    A.activation(hT[:, j, :], psum[2][:], ACT.Copy).then_inc(S["tA_evac"], 1)

            def h2T_low(c, i, fill):
                wait(act, "tA_ready", fill + 1)
                wait(act, "logits_ready", c * TPC + i)
                A.activation(h2T[:, 0:4, :], psum[2][:].rearrange("p (k n) -> p k n", k=4), ACT.Copy).then_inc(S["tA_evac"], 1)
                wait(act, "logits_ready", c * TPC + (i + 1))
                A.activation(lg[:, bass.ds(c * TPC + i, 1), :].rearrange("p o n -> p (o n)"), psum[0][:, 0:E], ACT.Copy).then_inc(S["logits_evac"], 1)

            def window(c, conv):
                for m in range(NZ):
                    z_copy(c, m)
                    if conv and m == 13:
                        squares(c - 1)
                if conv:
                    pool_scales(c - 1)
                    conv_b_sigmoid(c - 1)
                norm_in(c + 1)

            def mix_and_route(c, first, transposes):
                norm_mix(c, 0)
                norm_mix(c, 1)
                h2T_low(c, 0, first)
                norm_mix(c, 2)
                h2T_low(c, 1, first + 1)
                norm_mix(c, 3)
                h2T_low(c, 2, first + 2)
                if transposes:
                    hT_even(first + 3)
                h2T_low(c, 3, first + (7 if transposes else 3))

            act.wait_ge(S["const_ld"], 16 * N_CONST)
            norm_in(0)
            hT_even(0)
            window(0, False)
            hT_even(4)
            with act.Fori(1, NC) as c:
                window(c, True)
                mix_and_route(c - 1, c * 8, True)
            squares(NC - 1)
            pool_scales(NC - 1)
            conv_b_sigmoid(NC - 1)
            mix_and_route(NC - 1, 8 * NC, False)

            act.wait_ge(S["exp_in"], 1)
            A.activation(pr[:], lr[:], ACT.Exp).then_inc(S["exp_out"], 1)

            def xT_low(j):
                wait(act, "xt_ready", j + 1)
                wait(act, "gu_ready", j)
                A.activation(xT[:, 0:4, :], psum[2][:].rearrange("p (k n) -> p k n", k=4), ACT.Copy).then_inc(S["xta_evac"], 1)

            act.wait_ge(S["blocks_ready"], 1)
            act.wait_ge(S["slots_ready"], 1)
            total = act.value_load(blocks_i[0:1, 2 * E:2 * E + 1], min_val=E, max_val=E + MAXB * 2)
            xT_low(0)
            with act.Fori(0, total) as j:
                wait(act, "gu_ready", j + 1)
                wait(act, "hh_ready", j)
                A.activation(sig[:], psum[0][:], ACT.Sigmoid).then_inc(S["sig_ready"], 1)
                xT_low(j + 1)
                wait(act, "yp_ready", j + 1)
                wait(act, "y_st", (j + 1) * 16)
                A.activation(ysb[:, 512:1024], psum[6][:], ACT.Copy).then_inc(S["ysb_done"], 1)

            act.wait_ge(S["experts_done"], 1)

            def gate_first(q, s):
                wait(act, f"f_ld{s}", (q + 1) * 48)
                wait(act, f"o_st{s}", q * 16)
                A.activation(fr[:, s, :], fy[:, s, 0, :], ACT.Copy, scale=gates[:, 0, bass.ds(q * NF + s, 1)]).then_inc(S["f_y0"], 1)

            def norm_last(q, s):
                wait(act, "f_stat", q * NF + (s + 1))
                A.activation(fr[:, s, :], fr[:, s, :], ACT.Identity, bias=frs[:, s, 1:2], scale=frs[:, s, 0:1]).then_inc(S["f_norm"], 1)

            with act.Fori(0, NT // NF) as q:
                gate_first(q, 0)
                for s in range(NF):
                    if s + 1 < NF:
                        gate_first(q, s + 1)
                    norm_last(q, s)

        @block.vector
        def _(dve):
            def ln_in_stats(c):
                ch = Chain(dve, "ln_steps", c * K_LN)
                wait(dve, "x_ld", (c + 1) * (16 * TPC))
                wait(dve, "norm1", c * TPC)
                for i in range(TPC):
                    for half in range(2):
                        n = ch.open(V.bn_stats(bst[:, 6 * half:6 * half + 6], xin[:, i, half * 512:(half + 1) * 512]))
                    ch.until(n, alone="dve")
                    ch.step(V.bn_aggr(mv[:, 0, i, :], bst[:]))
                rsqrt(ch, rstd[:, 0, :], nwv[:], nwt[:], mv[:, 0, :, 1])
                assert ch.n == K_LN
                V.scalar_tensor_tensor(nmr[:, 0, :], mv[:, 0, :, 0], -1.0, rstd[:, 0, :], ALU.mult, ALU.mult).then_inc(S["ln_stat"], 1)

            def hT_odd(fill):
                for j in range(1, KD, 2):
                    wait(dve, "tB_ready", fill + (j // 2 + 1))
                    V.tensor_copy(hT[:, j, :], psum[3][:]).then_inc(S["tB_evac"], 1)

            def h2T_high(c, i, fill):
                wait(dve, "tB_ready", fill + 1)
                wait(dve, "logits_ready", c * TPC + i)
                V.tensor_copy(h2T[:, 4:8, :], psum[3][:].rearrange("p (k n) -> p k n", k=4)).then_inc(S["tB_evac"], 1)

            def conv_b(c):
                q = c % 2
                ch = Chain(dve, "conv_b_steps", c * K_CONV)
                wait(dve, "products", c * NPAIR + TA)
                wait(dve, "halos", (c + 1) * 3)
                for j in range(KB):
                    for t in range(TA):
                        src = vbuf[:, bass.ds(q, 1), t, j:j + CHUNK].rearrange("p o n -> p (o n)")
                        w = par_col(CB0 + t * KB + j)
                        if j == 0:
                            ch.open(V.tensor_scalar(cb[:, t, :], src, w, par_col(CBB0 + t), ALU.mult, ALU.add))
                        else:
                            ch.until(ch.n - TA + 1 if j < KB - 1 else ch.n - TA + 1 + t)
                            tap = V.scalar_tensor_tensor(cb[:, t, :], src, w, cb[:, t, :], ALU.mult, ALU.add)
                            if j < KB - 1:
                                ch.open(tap)
                            else:
                                tap.then_inc(S["conv_b_done"], 1)
                assert ch.n == K_CONV

            def conv_a(c):
                q = c % 2
                ch = Chain(dve, "conv_a_steps", c * K_CONVA)
                wait(dve, "products", c * NPAIR + NPAIR)
                wait(dve, "z_evac", c * NZ + 2 * NPAIR + TA)
                for j in range(KA):
                    for t in range(TA):
                        src = ubuf[:, bass.ds(q, 1), t, j:j + CHUNK].rearrange("p o n -> p (o n)")
                        w = par_col(CA0 + t * KA + j)
                        if j == 0:
                            ch.open(V.tensor_scalar(yT[:, t, :], src, w, None, ALU.mult))
                        else:
                            ch.until(ch.n - TA + 1)
                            ch.open(V.scalar_tensor_tensor(yT[:, t, :], src, w, yT[:, t, :], ALU.mult, ALU.add))
                assert ch.n == K_CONVA
                ch.until(ch.n)
                for t in range(TA):
                    V.tensor_tensor(yT[:, t, :], yT[:, t, :], gb[:, bass.ds(q, 1), t, :].rearrange("p o n -> p (o n)"),
                                    ALU.mult).then_inc(S["conv_a_done"], 1)

            def pool_windows(c):
                q = c % 2
                ch = Chain(dve, "pool_steps", c * K_DPOOL)
                wait(dve, "z_evac", c * NZ + NZ)
                W = HALO + CHUNK
                lo, hi = slice(0, GROUP), slice(GROUP, P)
                u = lambda t, rows, a, b: pbuf[rows, bass.ds(q, 1), t, a:b].rearrange("p o n -> p (o n)")
                al = slice(0, P)

                def finish(t, rows, sums):
                    inv = con_s[rows, WI0 + t:WI0 + t + 1]
                    tab = con_s[rows, bass.ds(c * (TP * 16) + (PT0 + t * 16), 16)]
                    ch.open(V.scalar_tensor_tensor(dp[rows, t, 16:], sums[rows, HALO + 16:W], inv, u(t, rows, HALO + 16, W), ALU.mult, ALU.subtract))
                    ch.step(V.tensor_tensor(dp[rows, t, 0:16], sums[rows, HALO:HALO + 16], tab, ALU.mult))
                    V.tensor_tensor(dp[rows, t, 0:16], dp[rows, t, 0:16], u(t, rows, HALO, HALO + 16),
                                    ALU.subtract).then_inc(S["pool_d_done"], 1)

                r0, r1 = rs[:, 0, :], rs[:, 1, :]
                ch.step(V.tensor_tensor(r0[:, 1:W], u(0, al, 1, W), u(0, al, 0, W - 1), ALU.add))
                ch.step(V.tensor_tensor(r1[hi, 3:W], r0[hi, 3:W], r0[hi, 1:W - 2], ALU.add))
                finish(0, lo, r0)
                finish(0, hi, r1)
                ch.step(V.tensor_tensor(r0[:, 1:W], u(1, al, 1, W), u(1, al, 0, W - 1), ALU.add))
                ch.step(V.tensor_tensor(r1[:, 3:W], r0[:, 3:W], r0[:, 1:W - 2], ALU.add))
                ch.step(V.tensor_tensor(r0[:, 7:W], r1[:, 7:W], r1[:, 3:W - 4], ALU.add))
                ch.step(V.tensor_tensor(r1[hi, 15:W], r0[hi, 15:W], r0[hi, 7:W - 8], ALU.add))
                finish(1, lo, r0)
                finish(1, hi, r1)
                assert ch.n == K_DPOOL, ch.n

            def centre(c):
                wait(dve, "mean_ready", c + 1)
                for t in range(TA):
                    V.tensor_tensor(cb[:, t, :], cb[:, t, :], psum[4][:], ALU.subtract).then_inc(S["centred"], 1)

            def conv_b_norm(c):
                ch = Chain(dve, "b_norm_steps", c * K_CLN)
                wait(dve, "var_ready", c + 1)
                rsqrt(ch, rs[:, 0, 0:CHUNK], rs[:, 1, 0:CHUNK], rt[:], psum[5][:])
                wait(dve, "centred", c * TA + TA)
                for t in range(TA):
                    V.tensor_tensor(cb[:, t, :], cb[:, t, :], rs[:, 0, 0:CHUNK], ALU.mult).then_inc(S["b_norm"], 1)
                for t in range(TA):
                    wait(dve, "b_sig", c * TA + (t + 1))
                    ch.open(V.tensor_scalar(cb[:, t, :], cb[:, t, :], par_col(LCG0 + t), par_col(LCB0 + t), ALU.mult, ALU.add))
                assert ch.n == K_CLN, ch.n
                ch.until(ch.n)
                for t in range(TA):
                    V.tensor_tensor(yT[:, TA + t, :], cb[:, t, :], sq[:, t, :], ALU.mult).then_inc(S["y_done"], 1)

            def mix_stats(c, i):
                ch = Chain(dve, "mix_steps", (c * TPC + i) * K_MIX)
                r = res[:, i % 2, :]
                wait(dve, "mix_ready", c * TPC + (i + 1))
                wait(dve, f"hres_ld{i % 2}", (c * 2 + (i // 2 + 1)) * 16)
                for half in range(2):
                    cols = slice(half * 512, (half + 1) * 512)
                    V.scalar_tensor_tensor(r[:, cols], r[:, cols], ALPHA, psum[4 + 2 * (i % 2) + half][:],
                                           ALU.mult, ALU.add).then_inc(S["mix_taken"], 1)
                wait(dve, "mix_taken", (c * TPC + (i + 1)) * 2)
                wait(dve, "norm2", c * TPC)
                for half in range(2):
                    ch.open(V.bn_stats(bst[:, 6 * half:6 * half + 6], r[:, half * 512:(half + 1) * 512]))
                ch.until(ch.n, alone="dve")
                ch.step(V.bn_aggr(mv[:, 1, i, :], bst[:]))
                rsqrt(ch, rstd[:, 1, i:i + 1], nwv[:, 0:1], nwt[:, 0:1], mv[:, 1, i, 1:2])
                assert ch.n == K_MIX
                V.scalar_tensor_tensor(nmr[:, 1, i:i + 1], mv[:, 1, i, 0:1], -1.0, rstd[:, 1, i:i + 1],
                                       ALU.mult, ALU.mult).then_inc(S["mix_stat"], 1)

            def convolutions(c):
                conv_b(c)
                conv_a(c)
                centre(c)
                pool_windows(c)
                conv_b_norm(c)

            def mix_and_route(c, first, transposes):
                mix_stats(c, 0)
                mix_stats(c, 1)
                h2T_high(c, 0, first)
                mix_stats(c, 2)
                h2T_high(c, 1, first + 1)
                mix_stats(c, 3)
                h2T_high(c, 2, first + 2)
                if transposes:
                    hT_odd(first + 3)
                h2T_high(c, 3, first + (7 if transposes else 3))

            V.memset(pw[:], 0.0).then_inc(S["set_up"], 1)
            V.memset(onesd[:], 1.0 / DA).then_inc(S["set_up"], 1)
            dve.wait_ge(S["const_ld"], 16 * N_CONST)
            ln_in_stats(0)
            hT_odd(0)
            ln_in_stats(1)
            hT_odd(4)
            with dve.Fori(1, NC) as c:
                convolutions(c - 1)
                ln_in_stats(c + 1)
                mix_and_route(c - 1, c * 8, True)
            convolutions(NC - 1)
            mix_and_route(NC - 1, 8 * NC, False)

            ch = Chain(dve, "route_steps", 0)
            ie = con_s[:, IE0:IE0 + E].unsqueeze(1).to_broadcast([P, NT, E])
            ig = con_s[:, IG0:IG0 + G].unsqueeze(1).to_broadcast([P, NT, G])
            i4 = con_s[:, IG0:IG0 + EG].unsqueeze(1).to_broadcast([P, NT, EG])
            wide = lambda a, n: a.unsqueeze(2).to_broadcast([P, NT, n])
            dve.wait_ge(S["logits_evac"], NT)
            dve.wait_ge(S["z_ready"], NC * NZ)
            dve.wait_ge(S["h2_ready"], NT)
            dve.wait_ge(S["h2_st0"], NT // 2 * 16)
            dve.wait_ge(S["h2_st1"], NT // 2 * 16)
            dve.wait_ge(S["probs_in"], 16)
            ch.step(V.memset(onesr[:], 1.0))
            ch.step(V.tensor_tensor(lr[:], lg[:], rb[:].unsqueeze(1).to_broadcast([P, NT, E]), ALU.add))
            ch.step(V.tensor_reduce(rsm[:], lr[:], AXX, ALU.max))
            V.tensor_tensor(lr[:], lr[:], wide(rsm[:], E), ALU.subtract).then_inc(S["exp_in"], 1)
            dve.wait_ge(S["exp_out"], 1)
            ch.step(V.tensor_reduce(rsm[:], pr[:], AXX, ALU.add))
            ch.step(V.reciprocal(rsm[:], rsm[:]))
            ch.step(V.tensor_tensor(pr[:], pr[:], wide(rsm[:], E), ALU.mult))
            p4 = pr[:].rearrange("p t (g k) -> p t g k", k=EG)
            for t0 in range(0, NT, 4):
                tt = slice(t0, t0 + 4)
                for n, (a, b) in enumerate(((0, 1), (0, 2), (0, 3), (1, 2), (1, 3), (2, 3))):
                    ch.open(V.tensor_tensor(pairs[:, tt, :, n], p4[:, tt, :, a], p4[:, tt, :, b], ALU.add))
            ch.until(ch.n)
            ch.step(V.tensor_reduce(gs[:], pairs[:], AXX, ALU.max))
            ch.step(V.tensor_reduce(gmx[:], gs[:], AXX, ALU.max))

            def first_index(value, peak, iota, n, out_):
                ch.step(V.tensor_tensor(value, value, wide(peak, n), ALU.is_equal))
                ch.step(V.tensor_scalar(value, value, -float(n), float(n), ALU.mult, ALU.add))
                ch.step(V.tensor_tensor(value, value, iota, ALU.add))
                ch.step(V.tensor_reduce(out_, value, AXX, ALU.min))

            first_index(gs[:], gmx[:], ig, G, gmx[:])
            ch.step(V.tensor_tensor(goh[:], ig, wide(gmx[:], G), ALU.is_equal))
            for k in range(EG):
                ch.open(V.tensor_tensor(bigm[:, :, k * G:(k + 1) * G], p4[:, :, :, k], goh[:], ALU.mult))
            ch.until(ch.n)
            ch.step(V.tensor_reduce(ing[:], bigm[:].rearrange("p t (k g) -> p t k g", g=G), AXX, ALU.add))
            for k in range(2):
                ch.step(V.tensor_reduce(top[:, k, :], ing[:], AXX, ALU.max))
                ch.step(V.tensor_copy(toh[:], ing[:]))
                first_index(toh[:], top[:, k, :], i4, EG, tix[:, k, :])
                if k == 0:
                    ch.step(V.tensor_tensor(toh[:], i4, wide(tix[:, k, :], EG), ALU.is_equal))
                    ch.step(V.scalar_tensor_tensor(ing[:], toh[:], -2.0, ing[:], ALU.mult, ALU.add))
                ch.step(V.scalar_tensor_tensor(tix[:, k, :], gmx[:], float(EG), tix[:, k, :], ALU.mult, ALU.add))
                ch.step(V.tensor_tensor(oh[:, k], ie, wide(tix[:, k, :], E), ALU.is_equal))
            ch.step(V.tensor_tensor(rsm[:], top[:, 0, :], top[:, 1, :], ALU.add))
            ch.step(V.reciprocal(rsm[:], rsm[:]))
            for k in range(2):
                ch.open(V.tensor_tensor(gates[:, k, :], top[:, k, :], rsm[:], ALU.mult))
            ch.step(V.memset(base[:, 0, :], 0.0))
            V.tensor_tensor(asg[:], oh[:, 0], oh[:, 1], ALU.add).then_inc(S["assigned"], 1)
            dve.wait_ge(S["prefix_ready"], 2)
            for t in range(NT):
                ch.step(V.tensor_tensor(base[:, t + 1, :], base[:, t, :], psum[7][:, t * E:(t + 1) * E], ALU.add))
            ch.step(V.tensor_tensor(slot[:], base[:, 0:NT, :], psum[6][:].rearrange("p (t e) -> p t e", e=E), ALU.add))
            ch.step(V.tensor_tensor(slot[:], slot[:], con_s[:, EB0:EB0 + E].unsqueeze(1).to_broadcast([P, NT, E]), ALU.add))
            for k in range(2):
                ch.step(V.tensor_tensor(bigm[:], oh[:, k], slot[:], ALU.mult))
                ch.step(V.tensor_reduce(slot_f[:, k, :], bigm[:], AXX, ALU.add))
            V.tensor_copy(slot_i[:], slot_f[:]).then_inc(S["slots_ready"], 1)
            ch.step(V.tensor_tensor(cmpb[:], base[:, NT, :].unsqueeze(2).to_broadcast([P, E, MAXB]),
                                    con_s[:, TH0:TH0 + MAXB].unsqueeze(1).to_broadcast([P, E, MAXB]), ALU.is_gt))
            ch.step(V.tensor_reduce(blk_f[:, 0:E], cmpb[:], AXX, ALU.add))
            ch.step(V.tensor_scalar(blk_f[:, 0:E], blk_f[:, 0:E], 1.0, None, ALU.max))
            ch.step(V.memset(blk_f[:, E:E + 1], 0.0))
            ch.step(V.tensor_tensor_scan(blk_f[:, E + 1:2 * E + 1], blk_f[:, 0:E], blk_f[:, 0:E], 0.0, ALU.add, ALU.bypass))
            V.tensor_copy(blocks_i[:, 0:2 * E + 1], blk_f[:, 0:2 * E + 1]).then_inc(S["blocks_ready"], 1)

            def xT_high(j):
                wait(dve, "xt_ready", j + 1)
                wait(dve, "gu_ready", j)
                V.tensor_copy(xT[:, 4:8, :], psum[3][:].rearrange("p (k n) -> p k n", k=4)).then_inc(S["xtb_evac"], 1)

            dve.wait_ge(S["list_st"], 16 * 2 * NT)
            dve.wait_ge(S["blocks_ready"], 1)
            total = dve.value_load(blocks_i[0:1, 2 * E:2 * E + 1], min_val=E, max_val=E + MAXB * 2)
            xT_high(0)
            with dve.Fori(0, total) as j:
                wait(dve, "sig_ready", j + 1)
                wait(dve, "hht_ready", j)
                V.tensor_tensor(hh[:], psum[0][:], sig[:], ALU.mult).then_inc(S["gated"], 1)
                wait(dve, "gated", j + 1)
                V.tensor_tensor(hh[:], psum[1][:], hh[:], ALU.mult).then_inc(S["hh_ready"], 1)
                xT_high(j + 1)
                wait(dve, "hht_ready", j + 1)
                wait(dve, "yp_ready", j)
                V.tensor_copy(hhT[:], psum[4][:].rearrange("p (k n) -> p k n", k=KF)).then_inc(S["hht_evac"], 1)
                wait(dve, "yp_ready", j + 1)
                wait(dve, "y_st", (j + 1) * 16)
                V.tensor_copy(ysb[:, 0:512], psum[5][:]).then_inc(S["ysb_done"], 1)

            dve.wait_ge(S["experts_done"], 1)
            K_FIN = 2 + 2 + 1 + NEWTON

            def combine(q, s):
                i = q * NF + s
                ch = Chain(dve, "f_steps", i * K_FIN)
                wait(dve, "f_y0", i + 1)
                wait(dve, "f_norm", q * NF)
                fa = fr[:, s, :]
                ch.step(V.scalar_tensor_tensor(fa, fy[:, s, 1, :], gates[:, 1, bass.ds(i, 1)], fa, ALU.mult, ALU.add))
                ch.step(V.scalar_tensor_tensor(fa, fy[:, s, 2, :], ALPHA, fa, ALU.mult, ALU.add))
                for half in range(2):
                    ch.open(V.bn_stats(fst[:, s, 6 * half:6 * half + 6], fa[:, half * 512:(half + 1) * 512]))
                ch.until(ch.n, alone="dve")
                ch.step(V.bn_aggr(fmv[:, s, :], fst[:, s, :]))
                rsqrt(ch, frs[:, s, 0:1], frs[:, s, 2:3], frs[:, s, 3:4], fmv[:, s, 1:2])
                assert ch.n == K_FIN, ch.n
                V.scalar_tensor_tensor(frs[:, s, 1:2], fmv[:, s, 0:1], -1.0, frs[:, s, 0:1],
                                       ALU.mult, ALU.mult).then_inc(S["f_stat"], 1)

            def scale_last(q, s):
                wait(dve, "f_norm", q * NF + (s + 1))
                wait(dve, "row_ld", 32)
                V.tensor_tensor(fr[:, s, :], fr[:, s, :], frow[:, 0, :], ALU.mult).then_inc(S["f_scaled"], 1)

            with dve.Fori(0, NT // NF) as q:
                combine(q, 0)
                for s in range(NF):
                    if s + 1 < NF:
                        combine(q, s + 1)
                    scale_last(q, s)

        @block.gpsimd
        def _(pool):
            def halo(c):
                q, o = c % 2, (c + 1) % 2
                wait(pool, "conv_b_done", (c - 1) * TA, alone="pool")
                wait(pool, "conv_a_done", (c - 1) * TA, alone="pool")
                wait(pool, "pool_d_done", (c - 1) * 4, alone="pool")
                wait(pool, "z_evac", c * NZ, alone="pool")
                wait(pool, "products", c * NPAIR, alone="pool")
                if isinstance(c, int) and c == 0:
                    for buf, w in ((vbuf, KB - 1), (ubuf, KA - 1), (pbuf, HALO)):
                        Q.memset(buf[:, 0, :, 0:w], 0.0).then_inc(S["halos"], 1)
                else:
                    for buf, w in ((vbuf, KB - 1), (ubuf, KA - 1), (pbuf, HALO)):
                        Q.tensor_copy(buf[:, bass.ds(q, 1), :, 0:w].rearrange("p o t n -> p (o t) n"),
                                      buf[:, bass.ds(o, 1), :, CHUNK:CHUNK + w].rearrange("p o t n -> p (o t) n")).then_inc(S["halos"], 1)

            def product(c, p):
                q = c % 2
                wait(pool, "z_evac", c * NZ + (2 * p + 2), alone="pool")
                buf, w, t = (vbuf, KB - 1, p) if p < TA else (ubuf, KA - 1, p - TA)
                Q.tensor_tensor(buf[:, bass.ds(q, 1), t, w:].rearrange("p o n -> p (o n)"), raw[:, 2 * (p % 2), :],
                                raw[:, 2 * (p % 2) + 1, :], ALU.mult).then_inc(S["products"], 1)

            def affine_in(c):
                for i in range(TPC):
                    wait(pool, "norm1", c * TPC + (i + 1), alone="pool")
                    Q.tensor_tensor(xin[:, i, :], xin[:, i, :], rowp[:, 0, :], ALU.mult).then_inc(S["scaled1"], 1)
                    wait(pool, "scaled1", (c * TPC + (i + 1)), alone="pool")
                    Q.tensor_tensor(xin[:, i, :], xin[:, i, :], rowp[:, 1, :], ALU.add).then_inc(S["h_ready"], 1)
                    wait(pool, "h_ready", c * TPC + (i + 1), alone="pool")
                    Q.dma_start(h_dram[bass.ds(c * CHUNK + i * P, P), :], xin[:, i, :]).then_inc(S["h_st"], 16)

            def affine_mix(c, i):
                wait(pool, "norm2", c * TPC + (i + 1), alone="pool")
                r = res[:, i % 2, :]
                Q.tensor_tensor(r, r, rowp[:, 2, :], ALU.mult).then_inc(S["scaled2"], 1)
                wait(pool, "scaled2", c * TPC + (i + 1), alone="pool")
                Q.tensor_tensor(r, r, rowp[:, 3, :], ALU.add).then_inc(S["h2_ready"], 1)
                wait(pool, "h2_ready", c * TPC + (i + 1), alone="pool")
                Q.dma_start(h2_dram[bass.ds(c * CHUNK + i * P, P), :], r).then_inc(S[f"h2_st{i % 2}"], 16)

            def window(c):
                halo(c)
                for p in range(NPAIR):
                    product(c, p)
                affine_in(c + 1)

            Q.memset(onepool[:], 0.0).then_inc(S["set_up"], 1)
            pool.wait_ge(S["set_up"], 3)
            pool.wait_ge(S["const_ld"], 16 * N_CONST)
            affine_in(0)
            window(0)
            with pool.Fori(1, NC) as c:
                window(c)
                for i in range(TPC):
                    affine_mix(c - 1, i)
            for i in range(TPC):
                affine_mix(NC - 1, i)

            pool.wait_ge(S["logits_evac"], NT)
            pool.wait_ge(S["h2_st0"], NT // 2 * 16)
            pool.wait_ge(S["h2_st1"], NT // 2 * 16)
            Q.dma_start(rb[:], router_b[0:1, :].to_broadcast([P, E])).then_inc(S["probs_in"], 16)
            Q.memset(pad[:, :, 0:1], 0).then_inc(S["pads_set"], 1)
            Q.memset(pad[:, :, 1:2], SKIP).then_inc(S["pads_set"], 1)
            pool.wait_ge(S["pads_set"], 2)
            Q.dma_start(list_dram.rearrange("(p n) c -> p n c", p=P), pad[:]).then_inc(S["list_pad_st"], 16)
            pool.wait_ge(S["list_pad_st"], 16)
            pool.wait_ge(S["slots_ready"], 1)
            for t in range(NT):
                for k in range(2):
                    Q.indirect_dma_start(out=list_dram, out_offset=bass.IndirectOffsetOnAxis(ap=slot_i[:, k, t:t + 1], axis=0),
                                         in_=entry_s[:, t, k, :], in_offset=None).then_inc(S["list_st"], 16)
            pool.wait_ge(S["list_st"], 16 * 2 * NT)

            pool.wait_ge(S["blocks_ready"], 1)
            Q.memset(idx_s[:], SKIP).then_inc(S["idx_copied"], 1)
            Q.memset(ysb[:], 0.0).then_inc(S["idx_copied"], 1)

            def gather(j):
                wait(pool, "xt_ready", j, alone="pool")
                Q.indirect_dma_start(out=xg[:], out_offset=None, in_=h2_dram,
                                     in_offset=bass.IndirectOffsetOnAxis(ap=idx_g[:, 0:1], axis=0)).then_inc(S["xg_ld"], 16)

            def scatter(j):
                wait(pool, "ysb_done", j * 2, alone="pool")
                Q.indirect_dma_start(out=y_dram, out_offset=bass.IndirectOffsetOnAxis(ap=idx_s[:, 1:2], axis=0),
                                     in_=ysb[:], in_offset=None, bounds_check=SKIP - 1, oob_is_err=False).then_inc(S["y_st"], 16)

            pool.wait_ge(S["idx_copied"], 2)
            with pool.Fori(0, E) as e:
                n = pool.value_load(blocks_i[0:1, bass.ds(e, 1)], min_val=1, max_val=MAXB)
                first = pool.value_load(blocks_i[0:1, bass.ds(e + E, 1)], min_val=0, max_val=E + MAXB * 2)
                with pool.Fori(0, n) as b:
                    j = first + b
                    wait(pool, "idx_copied", j + 2, alone="pool")
                    Q.dma_start(idx_g[:], list_dram[bass.ds(e * CAP + b * P, P), :]).then_inc(S["idx_ld"], 16)
                    wait(pool, "idx_ld", (j + 1) * 16, alone="pool")
                    gather(j)
                    scatter(j)
                    wait(pool, "y_st", (j + 1) * 16, alone="pool")
                    wait(pool, "xg_ld", (j + 1) * 16, alone="pool")
                    Q.tensor_copy(idx_s[:], idx_g[:]).then_inc(S["idx_copied"], 1)
            total = pool.value_load(blocks_i[0:1, 2 * E:2 * E + 1], min_val=E, max_val=E + MAXB * 2)
            wait(pool, "idx_copied", total + 2, alone="pool")
            gather(total)
            scatter(total)
            wait(pool, "y_st", (total + 1) * 16, alone="pool")
            wait(pool, "xg_ld", (total + 1) * 16, alone="pool")
            wait(pool, "xta_evac", total + 1, alone="pool")
            wait(pool, "xtb_evac", total + 1, alone="pool")
            Q.memset(onepool[:], 0.0).then_inc(S["experts_done"], 1)

            pool.wait_ge(S["row_ld"], 32)
            with pool.Fori(0, NT // NF) as q:
                for s in range(NF):
                    wait(pool, "f_scaled", q * NF + (s + 1), alone="pool")
                    Q.tensor_tensor(fr[:, s, :], fr[:, s, :], frow[:, 1, :], ALU.add).then_inc(S["f_out"], 1)

    stack.close()


def kernel(x, ln_in_g, ln_in_b, router_w, router_b, w_in, conv_a_w, conv_b_w, conv_b_b, ln_conv_g, ln_conv_b,
           pool_w, pool_scale, w_out, ln_mix_g, ln_mix_b, w_gate, w_up, w_down, ln_ffn_g, ln_ffn_b):
    import concourse.bacc as bacc
    from concourse.bass_utils import run_bass_kernel_spmd

    a = lambda v: np.ascontiguousarray(v)
    con, entry = constants()
    taps = lambda w, n: np.asarray(w)[0].reshape(n, TA, P).transpose(2, 1, 0).reshape(P, TA * n)
    chan = lambda v: np.asarray(v)[0].reshape(-1, P).T
    rw = np.asarray(router_w).reshape(KD, P, E).transpose(1, 0, 2).reshape(P, KD * E)
    params = np.concatenate([taps(conv_a_w, KA), taps(conv_b_w, KB), chan(conv_b_b), chan(ln_conv_g),
                             chan(ln_conv_b), chan(pool_scale), rw], axis=1)
    rows = np.stack([np.asarray(v).reshape(D) for v in (ln_in_g, ln_in_b, ln_mix_g, ln_mix_b, ln_ffn_g, ln_ffn_b)])
    win = np.asarray(w_in)[0].reshape(KD, P, NZ, P).transpose(2, 1, 0, 3).reshape(NZ, P, KD * P)[z_order()]
    ins = {
        "x": a(np.asarray(x)[0]), "w_in": a(win), "w_out": a(np.asarray(w_out)[0]),
        "w_gate": a(np.asarray(w_gate)[0]), "w_up": a(np.asarray(w_up)[0]), "w_down": a(np.asarray(w_down)[0]),
        "pool_w": a(np.asarray(pool_w)[0]), "params": a(params), "rows": a(rows),
        "router_b": a(np.asarray(router_b).reshape(1, E)), "con": a(con), "entry": a(entry),
    }
    nc = bacc.Bacc("TRN2", target_bir_lowering=False, num_devices=1)
    args = {n: nc.dram_tensor(f"in_{n}", v.shape, mybir.dt.from_np(v.dtype), kind="ExternalInput").ap() for n, v in ins.items()}
    out = nc.dram_tensor("out_rows", (SEQ, D), F32, kind="ExternalOutput").ap()
    program(nc, out=out, **args)
    r = run_bass_kernel_spmd(nc, [{f"in_{n}": v for n, v in ins.items()}], core_ids=[0])
    return r.results[0]["out_rows"].reshape(1, SEQ, D)
```

```python
from contextlib import ExitStack

import concourse.bass as bass
import numpy as np
from concourse import mybir

F32 = mybir.dt.float32
I32 = mybir.dt.int32
F32R = mybir.dt.float32r
ALU = mybir.AluOpType
ACT = mybir.ActivationFunctionType
AXX = mybir.AxisListType.X

P = 128
SEQ = 2048
D = 1024
KD = D // P
CHUNK = 512
NC = SEQ // CHUNK
TPC = CHUNK // P
NT = SEQ // P
DA = 3 * D // 8
TA = DA // P
DP = D - 2 * DA
TP = DP // P
WINDOWS = (2, 4, 8, 16)
GROUP = DP // len(WINDOWS)
KA, KB = 3, 31
HALO = max(WINDOWS) - 1
NZ = 3 * TA + 2 * TA + TP
NPAIR = 2 * TA
RING = 4
EPS = 1e-5
ALPHA = 2.0 ** 0.25
E = 32
G = 8
EG = E // G
F = D // 2
KF = F // P
CAP = SEQ
MAXB = CAP // P
PIECES = 6
SKIP = 2 * SEQ
RSQRT_SEED = float(0x5F3759DF)

CA0 = 0
CB0 = CA0 + TA * KA
CBB0 = CB0 + TA * KB
LCG0 = CBB0 + TA
LCB0 = LCG0 + TA
PS0 = LCB0 + TA
RW0 = PS0 + TP
NPAR = RW0 + KD * E
ID0 = 0
TRI0 = ID0 + P
IG0 = TRI0 + P
IE0 = IG0 + G
TH0 = IE0 + E
WI0 = TH0 + MAXB
PT0 = WI0 + TP
NCON = PT0 + NC * TP * 16


def constants():
    c = np.zeros((P, NCON), np.float32)
    c[:, ID0:ID0 + P] = np.eye(P)
    c[:, TRI0:TRI0 + P] = np.triu(np.ones((P, P)), 1)
    c[:, IG0:IG0 + G] = np.arange(G)
    c[:, IE0:IE0 + E] = np.arange(E)
    c[:, TH0:TH0 + MAXB] = np.arange(MAXB) * P
    for t in range(TP):
        for half in range(2):
            w = WINDOWS[2 * t + half]
            rows = slice(half * GROUP, (half + 1) * GROUP)
            c[rows, WI0 + t] = 1.0 / w
            for k in range(NC):
                pos = k * CHUNK + np.arange(16) + 1
                at = PT0 + (k * TP + t) * 16
                c[rows, at:at + 16] = 1.0 / np.minimum(pos, w)
    token = np.arange(NT)[None, :] * P + np.arange(P)[:, None]
    entry = np.zeros((P, NT, 2, 2), np.int32)
    for k in range(2):
        entry[:, :, k, 0] = token
        entry[:, :, k, 1] = token + k * SEQ
    return c, entry.reshape(P, NT * 4)


def z_order():
    b_val, b_gate = 3 * TA, 4 * TA
    order = []
    for t in range(TA):
        order += [b_val + t, b_gate + t]
    for t in range(TA):
        order += [TA + t, 2 * TA + t]
    order += list(range(TA))
    order += [5 * TA + t for t in range(TP)]
    return order


def program(nc, x, w_in, w_out, w_gate, w_up, w_down, pool_w, params, rows, router_b, con, entry, out):
    stack = ExitStack()
    sb = lambda name, shape, dt=F32: stack.enter_context(nc.sbuf_tensor(name, shape, dt))

    h_dram = nc.dram_tensor("h_scratch", [(NC + 1) * CHUNK, D], F32).ap()
    h2_dram = nc.dram_tensor("h2_scratch", [SEQ, D], F32).ap()
    list_dram = nc.dram_tensor("token_lists", [E * CAP, 2], I32).ap()
    y_dram = nc.dram_tensor("expert_rows", [2 * SEQ, D], F32).ap()

    con_s = sb("con_s", [P, NCON])
    onepool = sb("onepool", [P, 2])
    entry_s = sb("entry_s", [P, NT, 2, 2], I32)
    gates = sb("gates", [P, 2, NT])
    blocks_i = sb("blocks_i", [P, 3 * E + 1], I32)
    lg = sb("lg", [P, NT, E])
    ident = con_s[:, ID0:ID0 + P]

    mixer = ExitStack()
    ma = lambda name, shape, dt=F32: mixer.enter_context(nc.sbuf_tensor(name, shape, dt))
    win = [ma(f"win{s}", [P, KD, P]) for s in range(RING)]
    hT = ma("hT", [P, KD, CHUNK])
    xin = ma("xin", [P, TPC, D])
    wout = ma("wout", [P, KD, D])
    raw = ma("raw", [P, 4, CHUNK])
    vbuf = ma("vbuf", [P, 2, TA, KB - 1 + CHUNK])
    ubuf = ma("ubuf", [P, 2, TA, KA - 1 + CHUNK])
    pbuf = ma("pbuf", [P, 2, TP, HALO + CHUNK])
    gb = ma("gb", [P, 2, TA, CHUNK])
    cb = ma("cb", [P, TA, CHUNK])
    sq = ma("sq", [P, TA, CHUNK])
    rs = ma("rs", [P, 2, HALO + CHUNK])
    rt = ma("rt", [P, CHUNK])
    dp = ma("dp", [P, TP, CHUNK])
    yT = ma("yT", [P, KD, CHUNK])
    res = ma("res", [P, 2, D])
    h2T = ma("h2T", [P, KD, P])
    rowp = ma("rowp", [P, 4, D])
    par = ma("par", [P, NPAR])
    pw = ma("pw", [P, TP, P])
    onesd = ma("onesd", [P, P])
    bst = ma("bst", [P, 12])
    mv = ma("mv", [P, 2, TPC, 2])
    rstd = ma("rstd", [P, 2, TPC])
    nmr = ma("nmr", [P, 2, TPC])
    nwt = ma("nwt", [P, TPC])
    nwv = ma("nwv", [P, TPC])
    mixer.close()

    router = ExitStack()
    mr = lambda name, shape, dt=F32: router.enter_context(nc.sbuf_tensor(name, shape, dt))
    _under = mr("under", [P, 36 * D])
    rb = mr("rb", [P, E])
    pr = mr("pr", [P, NT, E])
    lr = mr("lr", [P, NT, E])
    rsm = mr("rsm", [P, NT])
    pairs = mr("pairs", [P, NT, G, 6])
    gs = mr("gs", [P, NT, G])
    goh = mr("goh", [P, NT, G])
    gmx = mr("gmx", [P, NT])
    ing = mr("ing", [P, NT, EG])
    toh = mr("toh", [P, NT, EG])
    bigm = mr("bigm", [P, NT, E])
    top = mr("top", [P, 2, NT])
    tix = mr("tix", [P, 2, NT])
    oh = mr("oh", [P, 2, NT, E])
    asg = mr("asg", [P, NT, E])
    base = mr("base", [P, NT + 1, E])
    slot = mr("slot", [P, NT, E])
    slot_f = mr("slot_f", [P, 2, NT])
    slot_i = mr("slot_i", [P, 2, NT], I32)
    cmpb = mr("cmpb", [P, E, MAXB])
    blk_f = mr("blk_f", [P, 3 * E + 1])
    rank_f = mr("rank_f", [P, 2, NT])
    blk_t = mr("blk_t", [P, 2, NT])
    cmpr = mr("cmpr", [P, NT, MAXB - 1])
    pad = mr("pad", [P, CAP * E // P, 2], I32)
    onesr = mr("onesr", [P, P])
    router.close()

    moe = ExitStack()
    mo = lambda name, shape, dt=F32: moe.enter_context(nc.sbuf_tensor(name, shape, dt))
    piece = [mo(f"piece{p}", [P, 4, F] if p < 4 else [P, 2, D]) for p in range(PIECES)]
    w_hi = [mo(f"w_hi{p}", [P, 4, F] if p < 4 else [P, 2, D], F32R) for p in range(PIECES)]
    w_lo = [mo(f"w_lo{p}", [P, 4, F] if p < 4 else [P, 2, D], F32R) for p in range(PIECES)]
    xg = mo("xg", [P, D])
    xT_hi = mo("xT_hi", [P, KD, P], F32R)
    xT_lo = mo("xT_lo", [P, KD, P], F32R)
    sig = mo("sig", [P, F])
    hh = mo("hh", [P, F])
    hhT_hi = mo("hhT_hi", [P, KF, P], F32R)
    hhT_lo = mo("hhT_lo", [P, KF, P], F32R)
    ysb = mo("ysb", [P, D])
    idx_all = mo("idx_all", [P, E, MAXB, 2], I32)
    idx_g = mo("idx_g", [P, 2], I32)
    idx_h = mo("idx_h", [P, 2, 2], I32)
    idx_s = mo("idx_s", [P, 2], I32)
    moe.close()

    final = ExitStack()
    mf = lambda name, shape, dt=F32: final.enter_context(nc.sbuf_tensor(name, shape, dt))
    NF = 4
    fy = mf("fy", [P, NF, 3, D])
    fr = mf("fr", [P, NF, D])
    frow = mf("frow", [P, 2, D])
    fst = mf("fst", [P, NF, 12])
    fmv = mf("fmv", [P, NF, 2])
    frs = mf("frs", [P, NF, 4])
    final.close()

    psum = [stack.enter_context(nc.psum_tensor(f"bank{b}", [P, 512], F32)) for b in range(8)]

    names = [
        "const_ld", "wout_ld", "x_ld", "h_st", "h2_st0", "h2_st1", "hres_ld0", "hres_ld1",
        "list_pad_st", "list_st", "row_ld",
        "set_up", "h_ready", "z_ready", "z_evac", "products", "tA_ready", "tA_evac", "tB_ready", "tB_evac",
        "halos", "conv_b_done", "conv_a_done", "pool_d_done", "mean_ready", "centred", "squares", "var_ready",
        "b_norm", "b_sig", "y_done", "pool_y_ready", "yc_done", "ln_stat", "norm1", "mix_ready", "mix_taken",
        "mix_stat", "norm2", "h2_ready", "logits_ready", "logits_evac",
        "ln_steps", "mix_steps", "conv_b_steps", "b_norm_steps", "conv_a_steps", "pool_steps",
        "route_steps", "scaled1", "scaled2", "pads_set",
        "passed_sp", "passed_pool", "passed_dve", "passed_pe",
        "probs_in", "assigned", "prefix_ready", "slots_ready", "blocks_ready", "exp_in", "exp_out",
        "idx_ld", "xg_ld", "y_st",
        "w_hi_done", "w_lo_done", "x1_ready", "x2_ready", "xh_done", "xl_done",
        "g_ready", "u_ready", "sig_ready", "hh_ready", "hht_ready", "hhth_done", "hhtl_done",
        "yp_ready", "ysb_done", "idx_copied", "gated", "experts_done",
        "f_ld0", "f_ld1", "f_ld2", "f_ld3", "o_st0", "o_st1", "o_st2", "o_st3",
        "f_y0", "f_stat", "f_norm", "f_scaled", "f_out", "f_steps",
    ] + [f"win_ld{s}" for s in range(RING)] + [f"piece_ld{p}" for p in range(PIECES)]
    S = {n: stack.enter_context(nc.semaphore(n)) for n in names}

    N_CONST = 3 + 4 + 4

    CREDIT = {"hh_ready": 1, "hht_ready": 1, "yp_ready": 1, "x2_ready": 1, "ysb_done": 3}

    def wait(eng, name, value, alone=""):
        value = value + CREDIT.get(name, 0)
        if isinstance(value, int) and value <= 0:
            return
        if alone and not isinstance(value, int):
            eng.wait_ge(S[name], value).then_inc(S["passed_" + alone], 1)
            return
        eng.wait_ge(S[name], value)

    class Chain:

        def __init__(self, eng, name, first):
            self.eng, self.name, self.first, self.n = eng, name, first, 0

        def step(self, instruction):
            instruction.then_inc(S[self.name], 1)
            self.n += 1
            self.eng.wait_ge(S[self.name], self.first + self.n)

        def signal(self, instruction, name, count):
            instruction.then_inc(S[name], 1)
            self.eng.wait_ge(S[name], count)

        def open(self, instruction):
            instruction.then_inc(S[self.name], 1)
            self.n += 1
            return self.n

        def until(self, n, alone=""):
            wait(self.eng, self.name, self.first + n, alone)

    V, A, T, Q, = nc.vector, nc.scalar, nc.tensor, nc.gpsimd

    NEWTON = 11

    def rsqrt(chain, y, v, t, eps_of):
        chain.step(V.tensor_scalar(v, eps_of, EPS, None, ALU.add))
        chain.step(V.tensor_scalar(y.bitcast(I32), v.bitcast(I32), -0.5, RSQRT_SEED, ALU.mult, ALU.add))
        for _ in range(3):
            chain.step(V.scalar_tensor_tensor(t, y, -0.5, y, ALU.mult, ALU.mult))
            chain.step(V.tensor_tensor(t, t, v, ALU.mult))
            chain.step(V.scalar_tensor_tensor(y, t, 1.5, y, ALU.add, ALU.mult))

    def par_col(base, n=1):
        return par[:, base:base + n]

    ring_uses = [len(range(s, NZ, RING)) for s in range(RING)]

    K_LN = 3 * TPC + NEWTON
    K_MIX = 3 + NEWTON
    K_CONV = TA * (KB - 1)
    K_CLN = NEWTON + TA
    K_CONVA = KA * TA
    K_DPOOL = 2 * 4 + 2 + 4

    with nc.Block() as block:

        @block.sync
        def _(sp):
            sp.dma_start(con_s[:], con[:, :]).then_inc(S["const_ld"], 16)
            sp.dma_start(entry_s[:], entry.rearrange("p (t k c) -> p t k c", k=2, c=2)).then_inc(S["const_ld"], 16)
            sp.dma_start(par[:], params[:, :]).then_inc(S["const_ld"], 16)
            for i in range(4):
                sp.dma_start(rowp[:, i, :], rows[i:i + 1, :].to_broadcast([P, D])).then_inc(S["const_ld"], 16)

            def load_x(c):
                wait(sp, "tB_ready", 4 if isinstance(c, int) else (c - 1) * 8, alone="sp")
                wait(sp, "h_st", c * (16 * TPC), alone="sp")
                src = x_of(c)
                for i in range(TPC):
                    sp.dma_start(xin[:, i, :], src(i)).then_inc(S["x_ld"], 16)

            def x_of(c):
                if isinstance(c, int):
                    c0 = (c % NC) * CHUNK
                else:
                    c0 = (c % NC) * CHUNK
                return lambda i: x[bass.ds(c0 + i * P, P), :]

            def load_win(c, m):
                s = m % RING
                if m >= RING:
                    wait(sp, "z_ready", c * NZ + (m - RING + 1), alone="sp")
                elif not (isinstance(c, int) and c == 0):
                    wait(sp, "z_ready", (c - 1) * NZ + (s + RING * (ring_uses[s] - 1) + 1), alone="sp")
                sp.dma_start(win[s][:], w_in[m].rearrange("p (k n) -> p k n", k=KD)).then_inc(S[f"win_ld{s}"], 16)

            def load_res(c):
                wait(sp, "h_st", (c + 3) * (16 * TPC) if not isinstance(c, int) else min(c + 3, NC + 1) * 16 * TPC, alone="sp")
                for i in range(TPC):
                    wait(sp, f"h2_st{i % 2}", (c * 2 + i // 2) * 16, alone="sp")
                    wait(sp, "tB_ready", (c + 1) * 8 + (i - 1) if i >= 2 else c * 8 + (3, 8)[i], alone="sp")
                    sp.dma_start(res[:, i % 2, :], h_dram[bass.ds(c * CHUNK + i * P, P), :]).then_inc(S[f"hres_ld{i % 2}"], 16)

            for i in range(TPC):
                sp.dma_start(xin[:, i, :], x[i * P:(i + 1) * P, :]).then_inc(S["x_ld"], 16)
            for m in range(RING):
                load_win(0, m)
            sp.wait_ge(S["set_up"], 3)
            for t in range(TP):
                for half in range(2):
                    g = slice(half * GROUP, (half + 1) * GROUP)
                    sp.dma_start(pw[g, t, g], pool_w[2 * t + half]).then_inc(S["const_ld"], 16)
            sp.dma_start(wout[:], w_out.rearrange("(k p) n -> p k n", p=P)).then_inc(S["wout_ld"], 16)

            def window(c):
                load_x(c + 1)
                for m in range(RING, NZ):
                    load_win(c, m)

            window(0)
            with sp.Fori(1, NC) as c:
                for m in range(RING):
                    load_win(c, m)
                window(c)
                load_res(c - 1)
            load_res(NC - 1)

            def load_piece(e, p):
                if not isinstance(e, int):
                    wait(sp, "w_lo_done", (e - 1) * PIECES + (p + 1), alone="sp")
                k = 4 * (p % 2) if p < 4 else 2 * (p % 2)
                w = (w_gate, w_up, w_down)[p // 2][bass.ds(e, 1), k * P:(k + (4 if p < 4 else 2)) * P, :]
                sp.dma_start(piece[p][:], w.rearrange("o (k p) f -> p (o k) f", p=P)).then_inc(S[f"piece_ld{p}"], 16)

            sp.wait_ge(S["z_ready"], NC * NZ)
            sp.wait_ge(S["tA_ready"], 8 * NC + TPC)
            sp.wait_ge(S["tB_ready"], 8 * NC + TPC)
            sp.wait_ge(S["h_st"], (NC + 1) * TPC * 16)
            for p in range(PIECES):
                load_piece(0, p)
            with sp.Fori(1, E) as e:
                for p in range(PIECES):
                    load_piece(e, p)

            sp.wait_ge(S["experts_done"], 1)
            for i in range(2):
                sp.dma_start(frow[:, i, :], rows[4 + i:5 + i, :].to_broadcast([P, D])).then_inc(S["row_ld"], 16)

            def load_tile(q, s):
                i = q * NF + s
                for k in range(2):
                    sp.dma_start(fy[:, s, k, :], y_dram[bass.ds(i * P + k * SEQ, P), :]).then_inc(S[f"f_ld{s}"], 16)
                sp.dma_start(fy[:, s, 2, :], h2_dram[bass.ds(i * P, P), :]).then_inc(S[f"f_ld{s}"], 16)

            def store_tile(q, s):
                wait(sp, "f_out", q * NF + (s + 1), alone="sp")
                sp.dma_start(out[bass.ds((q * NF + s) * P, P), :], fr[:, s, :]).then_inc(S[f"o_st{s}"], 16)

            for s in range(NF):
                load_tile(0, s)
            with sp.Fori(1, NT // NF) as q:
                for s in range(NF):
                    store_tile(q - 1, s)
                    load_tile(q, s)
            for s in range(NF):
                store_tile(NT // NF - 1, s)
            for s in range(NF):
                sp.wait_ge(S[f"o_st{s}"], 16 * (NT // NF))

        @block.tensor
        def _(pe):
            def x_transposes(c, fill):
                wait(pe, "h_ready", c * TPC + TPC)
                for j in range(KD):
                    wait(pe, ("tA_evac", "tB_evac")[j % 2], fill + j // 2)
                    for i in range(TPC):
                        last = T.transpose(psum[2 + j % 2][:, i * P:(i + 1) * P], xin[:, i, j * P:(j + 1) * P], ident)
                    last.then_inc(S[("tA_ready", "tB_ready")[j % 2]], 1)

            def projection(c, m):
                s = m % RING
                wait(pe, f"win_ld{s}", (c * ring_uses[s] + (m // RING + 1)) * 16)
                wait(pe, "z_evac", c * NZ + (m - 1 if m >= 2 else -m))
                for k in range(KD):
                    last = T.matmul(psum[m % 2][:], win[s][:, k, :], hT[:, k, :], start=(k == 0), stop=(k == KD - 1))
                last.then_inc(S["z_ready"], 1)

            def channel_mean(c):
                wait(pe, "conv_b_done", c * TA + TA)
                for t in range(TA):
                    last = T.matmul(psum[4][:], onesd[:], cb[:, t, :], start=(t == 0), stop=(t == TA - 1))
                last.then_inc(S["mean_ready"], 1)

            def channel_variance(c):
                wait(pe, "squares", c * TA + TA)
                for t in range(TA):
                    last = T.matmul(psum[5][:], onesd[:], sq[:, t, :], start=(t == 0), stop=(t == TA - 1))
                last.then_inc(S["var_ready"], 1)

            def pool_maps(c):
                wait(pe, "pool_d_done", c * 4 + 4)
                for t in range(TP):
                    T.matmul(psum[6 + t][:], pw[:, t, :], dp[:, t, :], start=True, stop=True).then_inc(S["pool_y_ready"], 1)

            def mix(c, i):
                if i == 0:
                    wait(pe, "conv_a_done", (c + 1) * TA)
                    wait(pe, "y_done", (c + 1) * TA)
                    wait(pe, "yc_done", (c + 1) * TP)
                wait(pe, "mix_taken", c * (2 * TPC) + 2 * (i - 1) if i >= 2 else c * (2 * TPC))
                for half in range(2):
                    bank = psum[4 + 2 * (i % 2) + half]
                    for k in range(KD):
                        last = T.matmul(bank[:], yT[:, k, i * P:(i + 1) * P], wout[:, k, half * 512:(half + 1) * 512],
                                        start=(k == 0), stop=(k == KD - 1))
                last.then_inc(S["mix_ready"], 1)

            def route(c, i, fill):
                wait(pe, "h2_ready", c * TPC + (i + 1))
                for half in range(2):
                    wait(pe, ("tA_evac", "tB_evac")[half], fill)
                    for j in range(4):
                        k = 4 * half + j
                        last = T.transpose(psum[2 + half][:, j * P:(j + 1) * P], res[:, i % 2, k * P:(k + 1) * P], ident)
                    last.then_inc(S[("tA_ready", "tB_ready")[half]], 1)
                wait(pe, "tA_evac", fill + 1)
                wait(pe, "tB_evac", fill + 1)
                wait(pe, "logits_evac", c * TPC + i)
                for k in range(KD):
                    last = T.matmul(psum[0][:, 0:E], h2T[:, k, :], par[:, RW0 + k * E:RW0 + (k + 1) * E],
                                    start=(k == 0), stop=(k == KD - 1))
                last.then_inc(S["logits_ready"], 1)

            def window(c, conv):
                wait(pe, "tA_evac", 4 if isinstance(c, int) else c * 8)
                wait(pe, "tB_evac", 4 if isinstance(c, int) else c * 8)
                wait(pe, "logits_evac", (c - 1) * TPC)
                for m in range(NZ):
                    projection(c, m)
                    if conv and m == 12:
                        channel_mean(c - 1)
                    if conv and m == 14:
                        channel_variance(c - 1)
                if conv:
                    pool_maps(c - 1)

            def mix_and_route(c, first, transposes):
                mix(c, 0)
                mix(c, 1)
                route(c, 0, first)
                mix(c, 2)
                route(c, 1, first + 1)
                mix(c, 3)
                route(c, 2, first + 2)
                if transposes:
                    x_transposes(c + 2, first + 3)
                route(c, 3, first + (7 if transposes else 3))

            pe.wait_ge(S["const_ld"], 16 * N_CONST)
            x_transposes(0, 0)
            window(0, False)
            x_transposes(1, 4)
            pe.wait_ge(S["wout_ld"], 16)
            with pe.Fori(1, NC) as c:
                window(c, True)
                mix_and_route(c - 1, c * 8, True)
            channel_mean(NC - 1)
            channel_variance(NC - 1)
            pool_maps(NC - 1)
            mix_and_route(NC - 1, 8 * NC, False)

            pe.wait_ge(S["assigned"], 1)
            flat = asg[:].rearrange("p t e -> p (t e)")
            T.matmul(psum[6][:], con_s[:, TRI0:TRI0 + P], flat, start=True, stop=True).then_inc(S["prefix_ready"], 1)
            T.matmul(psum[7][:], onesr[:], flat, start=True, stop=True).then_inc(S["prefix_ready"], 1)

            def block_transpose(j, half):
                wait(pe, "xg_ld", (j + 1) * 16)
                wait(pe, "xh_done", 2 * j + half)
                wait(pe, "xl_done", 2 * j + half)
                for k in range(4):
                    kk = half * 4 + k
                    last = T.transpose(psum[2 + half][:, k * P:(k + 1) * P], xg[:, kk * P:(kk + 1) * P], ident)
                last.then_inc(S[("x1_ready", "x2_ready")[half]], 1)

            def split_product(bank, lhs_hi, lhs_lo, rhs_hi, rhs_lo, start, stop):
                T.matmul(bank, lhs_hi, rhs_hi, start=start, stop=False)
                T.matmul(bank, lhs_hi, rhs_lo, start=False, stop=False)
                return T.matmul(bank, lhs_lo, rhs_hi, start=False, stop=stop)

            def piece_split(e, p):
                wait(pe, "w_hi_done", e * PIECES + (p + 1))
                wait(pe, "w_lo_done", e * PIECES + (p + 1))

            def expert_block(j, e):
                wait(pe, "xh_done", 2 * j + 2)
                wait(pe, "xl_done", 2 * j + 2)
                wait(pe, "hh_ready", j)
                for b in range(2):
                    for k in range(KD):
                        p = 2 * b + k // 4
                        if k % 4 == 0:
                            piece_split(e, p)
                        last = split_product(psum[b][:], xT_hi[:, k, :], xT_lo[:, k, :], w_hi[p][:, k % 4, :],
                                             w_lo[p][:, k % 4, :], k == 0, k == KD - 1)
                    last.then_inc(S[("g_ready", "u_ready")[b]], 1)
                block_transpose(j + 1, 0)
                wait(pe, "hh_ready", j + 1)
                for k in range(KF):
                    last = T.transpose(psum[4][:, k * P:(k + 1) * P], hh[:, k * P:(k + 1) * P], ident)
                last.then_inc(S["hht_ready"], 1)
                block_transpose(j + 1, 1)
                wait(pe, "hhth_done", j + 1)
                wait(pe, "hhtl_done", j + 1)
                for half in range(2):
                    cols = slice(half * 512, (half + 1) * 512)
                    wait(pe, "ysb_done", 2 * j + half - 1)
                    for k in range(KF):
                        p = 4 + k // 2
                        if half == 0 and k % 2 == 0:
                            piece_split(e, p)
                        last = split_product(psum[5 + half][:], hhT_hi[:, k, :], hhT_lo[:, k, :], w_hi[p][:, k % 2, cols],
                                             w_lo[p][:, k % 2, cols], k == 0, k == KF - 1)
                    last.then_inc(S["yp_ready"], 1)

            pe.sem_inc(S["x2_ready"], CREDIT["x2_ready"])
            pe.sem_inc(S["hht_ready"], CREDIT["hht_ready"])
            pe.sem_inc(S["yp_ready"], CREDIT["yp_ready"])
            pe.wait_ge(S["list_st"], 16 * 2 * NT)
            block_transpose(0, 0)
            block_transpose(0, 1)
            with pe.Fori(0, E) as e:
                n = pe.value_load(blocks_i[0:1, bass.ds(e, 1)], min_val=1, max_val=MAXB)
                first = pe.value_load(blocks_i[0:1, bass.ds(e + E, 1)], min_val=0, max_val=E + MAXB * 2)
                with pe.Fori(0, n) as b:
                    expert_block(first + b, e)

        @block.scalar
        def _(act):
            def z_copy(c, m):
                q = c % 2
                wait(act, "z_ready", c * NZ + (m + 1))
                if m < 2 * NPAIR:
                    p, second = divmod(m, 2)
                    wait(act, "products", c * NPAIR + (p - 1))
                    func = ACT.Sigmoid if second and p < TA else ACT.Copy
                    A.activation(raw[:, 2 * (p % 2) + second, :], psum[m % 2][:], func).then_inc(S["z_evac"], 1)
                elif m < 2 * NPAIR + TA:
                    wait(act, "conv_a_done", (c - 1) * TA)
                    t = m - 2 * NPAIR
                    A.activation(gb[:, bass.ds(q, 1), t, :].rearrange("p o n -> p (o n)"), psum[m % 2][:], ACT.Copy).then_inc(S["z_evac"], 1)
                else:
                    wait(act, "pool_d_done", (c - 1) * 4)
                    wait(act, "halos", c * 3)
                    t = m - 2 * NPAIR - TA
                    A.activation(pbuf[:, bass.ds(q, 1), t, HALO:].rearrange("p o n -> p (o n)"), psum[m % 2][:], ACT.Copy).then_inc(S["z_evac"], 1)

            def squares(c):
                for t in range(TA):
                    wait(act, "centred", c * TA + (t + 1))
                    A.activation(sq[:, t, :], cb[:, t, :], ACT.Square).then_inc(S["squares"], 1)

            def conv_b_sigmoid(c):
                for t in range(TA):
                    wait(act, "b_norm", c * TA + (t + 1))
                    A.activation(sq[:, t, :], cb[:, t, :], ACT.Sigmoid, bias=par_col(LCB0 + t), scale=par_col(LCG0 + t)).then_inc(S["b_sig"], 1)

            def pool_scales(c):
                for t in range(TP):
                    wait(act, "pool_y_ready", c * TP + (t + 1))
                    A.activation(yT[:, 2 * TA + t, :], psum[6 + t][:], ACT.Copy, scale=par_col(PS0 + t)).then_inc(S["yc_done"], 1)

            def norm_in(c):
                wait(act, "ln_stat", c + 1)
                for i in range(TPC):
                    A.activation(xin[:, i, :], xin[:, i, :], ACT.Identity, bias=nmr[:, 0, i:i + 1], scale=rstd[:, 0, i:i + 1]).then_inc(S["norm1"], 1)

            def norm_mix(c, i):
                wait(act, "mix_stat", c * TPC + (i + 1))
                A.activation(res[:, i % 2, :], res[:, i % 2, :], ACT.Identity, bias=nmr[:, 1, i:i + 1], scale=rstd[:, 1, i:i + 1]).then_inc(S["norm2"], 1)

            def hT_even(fill):
                for j in range(0, KD, 2):
                    wait(act, "tA_ready", fill + (j // 2 + 1))
                    A.activation(hT[:, j, :], psum[2][:], ACT.Copy).then_inc(S["tA_evac"], 1)

            def h2T_low(c, i, fill):
                wait(act, "tA_ready", fill + 1)
                wait(act, "logits_ready", c * TPC + i)
                A.activation(h2T[:, 0:4, :], psum[2][:].rearrange("p (k n) -> p k n", k=4), ACT.Copy).then_inc(S["tA_evac"], 1)
                wait(act, "logits_ready", c * TPC + (i + 1))
                A.activation(lg[:, bass.ds(c * TPC + i, 1), :].rearrange("p o n -> p (o n)"), psum[0][:, 0:E], ACT.Copy).then_inc(S["logits_evac"], 1)

            def window(c, conv):
                for m in range(NZ):
                    z_copy(c, m)
                    if conv and m == 13:
                        squares(c - 1)
                if conv:
                    pool_scales(c - 1)
                    conv_b_sigmoid(c - 1)
                norm_in(c + 1)

            def mix_and_route(c, first, transposes):
                norm_mix(c, 0)
                norm_mix(c, 1)
                h2T_low(c, 0, first)
                norm_mix(c, 2)
                h2T_low(c, 1, first + 1)
                norm_mix(c, 3)
                h2T_low(c, 2, first + 2)
                if transposes:
                    hT_even(first + 3)
                h2T_low(c, 3, first + (7 if transposes else 3))

            act.wait_ge(S["const_ld"], 16 * N_CONST)
            norm_in(0)
            hT_even(0)
            window(0, False)
            hT_even(4)
            with act.Fori(1, NC) as c:
                window(c, True)
                mix_and_route(c - 1, c * 8, True)
            squares(NC - 1)
            pool_scales(NC - 1)
            conv_b_sigmoid(NC - 1)
            mix_and_route(NC - 1, 8 * NC, False)

            act.wait_ge(S["exp_in"], 1)
            A.activation(pr[:], lr[:], ACT.Exp).then_inc(S["exp_out"], 1)

            def split_high(e, p, after):
                wait(act, f"piece_ld{p}", e * 16 + 16)
                if after is not None:
                    wait(act, ("g_ready", "u_ready", "yp_ready")[p // 2], after * 2 if p >= 4 else after)
                A.activation(w_hi[p][:], piece[p][:], ACT.Copy).then_inc(S["w_hi_done"], 1)

            def xT_high(j, half):
                wait(act, ("x1_ready", "x2_ready")[half], j + 1)
                A.activation(xT_hi[:, 4 * half:4 * half + 4, :], psum[2 + half][:].rearrange("p (k n) -> p k n", k=4),
                             ACT.Copy).then_inc(S["xh_done"], 1)

            def result(j, half):
                wait(act, "yp_ready", 2 * j + half + 1)
                wait(act, "y_st", j * 16 + 48)
                A.activation(ysb[:, half * 512:(half + 1) * 512], psum[5 + half][:], ACT.Copy).then_inc(S["ysb_done"], 1)

            def expert_block(j, e):
                wait(act, "g_ready", j + 1)
                wait(act, "hh_ready", j)
                A.activation(sig[:], psum[0][:], ACT.Sigmoid).then_inc(S["sig_ready"], 1)
                if e is not None:
                    split_high(e, 0, j + 1)
                    split_high(e, 1, j + 1)
                wait(act, "u_ready", j + 1)
                xT_high(j + 1, 0)
                wait(act, "hht_ready", j + 1)
                wait(act, "yp_ready", j * 2)
                A.activation(hhT_hi[:], psum[4][:].rearrange("p (k n) -> p k n", k=KF), ACT.Copy).then_inc(S["hhth_done"], 1)
                xT_high(j + 1, 1)
                if e is not None:
                    split_high(e, 2, j + 1)
                result(j, 0)
                if e is not None:
                    split_high(e, 3, j + 1)
                result(j, 1)
                if e is not None:
                    split_high(e, 4, j + 1)
                    split_high(e, 5, j + 1)

            act.sem_inc(S["ysb_done"], CREDIT["ysb_done"])
            for p in range(PIECES):
                split_high(0, p, None)
            act.wait_ge(S["list_st"], 16 * 2 * NT)
            act.wait_ge(S["blocks_ready"], 1)
            xT_high(0, 0)
            xT_high(0, 1)
            with act.Fori(0, E - 1) as e:
                n = act.value_load(blocks_i[0:1, bass.ds(e, 1)], min_val=1, max_val=MAXB)
                first = act.value_load(blocks_i[0:1, bass.ds(e + E, 1)], min_val=0, max_val=E + MAXB * 2)
                with act.If(n > 1):
                    with act.Fori(0, n - 1) as b:
                        expert_block(first + b, None)
                last = act.value_load(blocks_i[0:1, bass.ds(e + (2 * E + 1), 1)], min_val=0, max_val=E + MAXB * 2)
                expert_block(last, e + 1)
            n = act.value_load(blocks_i[0:1, E - 1:E], min_val=1, max_val=MAXB)
            first = act.value_load(blocks_i[0:1, 2 * E - 1:2 * E], min_val=0, max_val=E + MAXB * 2)
            with act.Fori(0, n) as b:
                expert_block(first + b, None)

            act.wait_ge(S["experts_done"], 1)

            def gate_first(q, s):
                wait(act, f"f_ld{s}", (q + 1) * 48)
                wait(act, f"o_st{s}", q * 16)
                A.activation(fr[:, s, :], fy[:, s, 0, :], ACT.Copy, scale=gates[:, 0, bass.ds(q * NF + s, 1)]).then_inc(S["f_y0"], 1)

            def norm_last(q, s):
                wait(act, "f_stat", q * NF + (s + 1))
                A.activation(fr[:, s, :], fr[:, s, :], ACT.Identity, bias=frs[:, s, 1:2], scale=frs[:, s, 0:1]).then_inc(S["f_norm"], 1)

            with act.Fori(0, NT // NF) as q:
                gate_first(q, 0)
                for s in range(NF):
                    if s + 1 < NF:
                        gate_first(q, s + 1)
                    norm_last(q, s)

        @block.vector
        def _(dve):
            def ln_in_stats(c):
                ch = Chain(dve, "ln_steps", c * K_LN)
                wait(dve, "x_ld", (c + 1) * (16 * TPC))
                wait(dve, "norm1", c * TPC)
                for i in range(TPC):
                    for half in range(2):
                        n = ch.open(V.bn_stats(bst[:, 6 * half:6 * half + 6], xin[:, i, half * 512:(half + 1) * 512]))
                    ch.until(n, alone="dve")
                    ch.step(V.bn_aggr(mv[:, 0, i, :], bst[:]))
                rsqrt(ch, rstd[:, 0, :], nwv[:], nwt[:], mv[:, 0, :, 1])
                assert ch.n == K_LN
                V.scalar_tensor_tensor(nmr[:, 0, :], mv[:, 0, :, 0], -1.0, rstd[:, 0, :], ALU.mult, ALU.mult).then_inc(S["ln_stat"], 1)

            def hT_odd(fill):
                for j in range(1, KD, 2):
                    wait(dve, "tB_ready", fill + (j // 2 + 1))
                    V.tensor_copy(hT[:, j, :], psum[3][:]).then_inc(S["tB_evac"], 1)

            def h2T_high(c, i, fill):
                wait(dve, "tB_ready", fill + 1)
                wait(dve, "logits_ready", c * TPC + i)
                V.tensor_copy(h2T[:, 4:8, :], psum[3][:].rearrange("p (k n) -> p k n", k=4)).then_inc(S["tB_evac"], 1)

            def conv_b(c):
                q = c % 2
                ch = Chain(dve, "conv_b_steps", c * K_CONV)
                wait(dve, "products", c * NPAIR + TA)
                wait(dve, "halos", (c + 1) * 3)
                for j in range(KB):
                    for t in range(TA):
                        src = vbuf[:, bass.ds(q, 1), t, j:j + CHUNK].rearrange("p o n -> p (o n)")
                        w = par_col(CB0 + t * KB + j)
                        if j == 0:
                            ch.open(V.tensor_scalar(cb[:, t, :], src, w, par_col(CBB0 + t), ALU.mult, ALU.add))
                        else:
                            ch.until(ch.n - TA + 1 if j < KB - 1 else ch.n - TA + 1 + t)
                            tap = V.scalar_tensor_tensor(cb[:, t, :], src, w, cb[:, t, :], ALU.mult, ALU.add)
                            if j < KB - 1:
                                ch.open(tap)
                            else:
                                tap.then_inc(S["conv_b_done"], 1)
                assert ch.n == K_CONV

            def conv_a(c):
                q = c % 2
                ch = Chain(dve, "conv_a_steps", c * K_CONVA)
                wait(dve, "products", c * NPAIR + NPAIR)
                wait(dve, "z_evac", c * NZ + 2 * NPAIR + TA)
                for j in range(KA):
                    for t in range(TA):
                        src = ubuf[:, bass.ds(q, 1), t, j:j + CHUNK].rearrange("p o n -> p (o n)")
                        w = par_col(CA0 + t * KA + j)
                        if j == 0:
                            ch.open(V.tensor_scalar(yT[:, t, :], src, w, None, ALU.mult))
                        else:
                            ch.until(ch.n - TA + 1)
                            ch.open(V.scalar_tensor_tensor(yT[:, t, :], src, w, yT[:, t, :], ALU.mult, ALU.add))
                assert ch.n == K_CONVA
                ch.until(ch.n)
                for t in range(TA):
                    V.tensor_tensor(yT[:, t, :], yT[:, t, :], gb[:, bass.ds(q, 1), t, :].rearrange("p o n -> p (o n)"),
                                    ALU.mult).then_inc(S["conv_a_done"], 1)

            def pool_windows(c):
                q = c % 2
                ch = Chain(dve, "pool_steps", c * K_DPOOL)
                wait(dve, "z_evac", c * NZ + NZ)
                W = HALO + CHUNK
                lo, hi = slice(0, GROUP), slice(GROUP, P)
                u = lambda t, rows, a, b: pbuf[rows, bass.ds(q, 1), t, a:b].rearrange("p o n -> p (o n)")
                al = slice(0, P)

                def finish(t, rows, sums):
                    inv = con_s[rows, WI0 + t:WI0 + t + 1]
                    tab = con_s[rows, bass.ds(c * (TP * 16) + (PT0 + t * 16), 16)]
                    ch.open(V.scalar_tensor_tensor(dp[rows, t, 16:], sums[rows, HALO + 16:W], inv, u(t, rows, HALO + 16, W), ALU.mult, ALU.subtract))
                    ch.step(V.tensor_tensor(dp[rows, t, 0:16], sums[rows, HALO:HALO + 16], tab, ALU.mult))
                    V.tensor_tensor(dp[rows, t, 0:16], dp[rows, t, 0:16], u(t, rows, HALO, HALO + 16),
                                    ALU.subtract).then_inc(S["pool_d_done"], 1)

                r0, r1 = rs[:, 0, :], rs[:, 1, :]
                ch.step(V.tensor_tensor(r0[:, 1:W], u(0, al, 1, W), u(0, al, 0, W - 1), ALU.add))
                ch.step(V.tensor_tensor(r1[hi, 3:W], r0[hi, 3:W], r0[hi, 1:W - 2], ALU.add))
                finish(0, lo, r0)
                finish(0, hi, r1)
                ch.step(V.tensor_tensor(r0[:, 1:W], u(1, al, 1, W), u(1, al, 0, W - 1), ALU.add))
                ch.step(V.tensor_tensor(r1[:, 3:W], r0[:, 3:W], r0[:, 1:W - 2], ALU.add))
                ch.step(V.tensor_tensor(r0[:, 7:W], r1[:, 7:W], r1[:, 3:W - 4], ALU.add))
                ch.step(V.tensor_tensor(r1[hi, 15:W], r0[hi, 15:W], r0[hi, 7:W - 8], ALU.add))
                finish(1, lo, r0)
                finish(1, hi, r1)
                assert ch.n == K_DPOOL, ch.n

            def centre(c):
                wait(dve, "mean_ready", c + 1)
                for t in range(TA):
                    V.tensor_tensor(cb[:, t, :], cb[:, t, :], psum[4][:], ALU.subtract).then_inc(S["centred"], 1)

            def conv_b_norm(c):
                ch = Chain(dve, "b_norm_steps", c * K_CLN)
                wait(dve, "var_ready", c + 1)
                rsqrt(ch, rs[:, 0, 0:CHUNK], rs[:, 1, 0:CHUNK], rt[:], psum[5][:])
                wait(dve, "centred", c * TA + TA)
                for t in range(TA):
                    V.tensor_tensor(cb[:, t, :], cb[:, t, :], rs[:, 0, 0:CHUNK], ALU.mult).then_inc(S["b_norm"], 1)
                for t in range(TA):
                    wait(dve, "b_sig", c * TA + (t + 1))
                    ch.open(V.tensor_scalar(cb[:, t, :], cb[:, t, :], par_col(LCG0 + t), par_col(LCB0 + t), ALU.mult, ALU.add))
                assert ch.n == K_CLN, ch.n
                ch.until(ch.n)
                for t in range(TA):
                    V.tensor_tensor(yT[:, TA + t, :], cb[:, t, :], sq[:, t, :], ALU.mult).then_inc(S["y_done"], 1)

            def mix_stats(c, i):
                ch = Chain(dve, "mix_steps", (c * TPC + i) * K_MIX)
                r = res[:, i % 2, :]
                wait(dve, "mix_ready", c * TPC + (i + 1))
                wait(dve, f"hres_ld{i % 2}", (c * 2 + (i // 2 + 1)) * 16)
                for half in range(2):
                    cols = slice(half * 512, (half + 1) * 512)
                    V.scalar_tensor_tensor(r[:, cols], r[:, cols], ALPHA, psum[4 + 2 * (i % 2) + half][:],
                                           ALU.mult, ALU.add).then_inc(S["mix_taken"], 1)
                wait(dve, "mix_taken", (c * TPC + (i + 1)) * 2)
                wait(dve, "norm2", c * TPC)
                for half in range(2):
                    ch.open(V.bn_stats(bst[:, 6 * half:6 * half + 6], r[:, half * 512:(half + 1) * 512]))
                ch.until(ch.n, alone="dve")
                ch.step(V.bn_aggr(mv[:, 1, i, :], bst[:]))
                rsqrt(ch, rstd[:, 1, i:i + 1], nwv[:, 0:1], nwt[:, 0:1], mv[:, 1, i, 1:2])
                assert ch.n == K_MIX
                V.scalar_tensor_tensor(nmr[:, 1, i:i + 1], mv[:, 1, i, 0:1], -1.0, rstd[:, 1, i:i + 1],
                                       ALU.mult, ALU.mult).then_inc(S["mix_stat"], 1)

            def convolutions(c):
                conv_b(c)
                conv_a(c)
                centre(c)
                pool_windows(c)
                conv_b_norm(c)

            def mix_and_route(c, first, transposes):
                mix_stats(c, 0)
                mix_stats(c, 1)
                h2T_high(c, 0, first)
                mix_stats(c, 2)
                h2T_high(c, 1, first + 1)
                mix_stats(c, 3)
                h2T_high(c, 2, first + 2)
                if transposes:
                    hT_odd(first + 3)
                h2T_high(c, 3, first + (7 if transposes else 3))

            V.memset(pw[:], 0.0).then_inc(S["set_up"], 1)
            V.memset(onesd[:], 1.0 / DA).then_inc(S["set_up"], 1)
            dve.wait_ge(S["const_ld"], 16 * N_CONST)
            ln_in_stats(0)
            hT_odd(0)
            ln_in_stats(1)
            hT_odd(4)
            with dve.Fori(1, NC) as c:
                convolutions(c - 1)
                ln_in_stats(c + 1)
                mix_and_route(c - 1, c * 8, True)
            convolutions(NC - 1)
            mix_and_route(NC - 1, 8 * NC, False)

            ch = Chain(dve, "route_steps", 0)
            ie = con_s[:, IE0:IE0 + E].unsqueeze(1).to_broadcast([P, NT, E])
            ig = con_s[:, IG0:IG0 + G].unsqueeze(1).to_broadcast([P, NT, G])
            i4 = con_s[:, IG0:IG0 + EG].unsqueeze(1).to_broadcast([P, NT, EG])
            wide = lambda a, n: a.unsqueeze(2).to_broadcast([P, NT, n])
            dve.wait_ge(S["logits_evac"], NT)
            dve.wait_ge(S["z_ready"], NC * NZ)
            dve.wait_ge(S["h2_ready"], NT)
            dve.wait_ge(S["h2_st0"], NT // 2 * 16)
            dve.wait_ge(S["h2_st1"], NT // 2 * 16)
            dve.wait_ge(S["probs_in"], 16)
            ch.step(V.memset(onesr[:], 1.0))
            ch.step(V.tensor_tensor(lr[:], lg[:], rb[:].unsqueeze(1).to_broadcast([P, NT, E]), ALU.add))
            ch.step(V.tensor_reduce(rsm[:], lr[:], AXX, ALU.max))
            V.tensor_tensor(lr[:], lr[:], wide(rsm[:], E), ALU.subtract).then_inc(S["exp_in"], 1)
            dve.wait_ge(S["exp_out"], 1)
            ch.step(V.tensor_reduce(rsm[:], pr[:], AXX, ALU.add))
            ch.step(V.reciprocal(rsm[:], rsm[:]))
            ch.step(V.tensor_tensor(pr[:], pr[:], wide(rsm[:], E), ALU.mult))
            p4 = pr[:].rearrange("p t (g k) -> p t g k", k=EG)
            for t0 in range(0, NT, 4):
                tt = slice(t0, t0 + 4)
                for n, (a, b) in enumerate(((0, 1), (0, 2), (0, 3), (1, 2), (1, 3), (2, 3))):
                    ch.open(V.tensor_tensor(pairs[:, tt, :, n], p4[:, tt, :, a], p4[:, tt, :, b], ALU.add))
            ch.until(ch.n)
            ch.step(V.tensor_reduce(gs[:], pairs[:], AXX, ALU.max))
            ch.step(V.tensor_reduce(gmx[:], gs[:], AXX, ALU.max))

            def first_index(value, peak, iota, n, out_):
                ch.step(V.tensor_tensor(value, value, wide(peak, n), ALU.is_equal))
                ch.step(V.tensor_scalar(value, value, -float(n), float(n), ALU.mult, ALU.add))
                ch.step(V.tensor_tensor(value, value, iota, ALU.add))
                ch.step(V.tensor_reduce(out_, value, AXX, ALU.min))

            first_index(gs[:], gmx[:], ig, G, gmx[:])
            ch.step(V.tensor_tensor(goh[:], ig, wide(gmx[:], G), ALU.is_equal))
            for k in range(EG):
                ch.open(V.tensor_tensor(bigm[:, :, k * G:(k + 1) * G], p4[:, :, :, k], goh[:], ALU.mult))
            ch.until(ch.n)
            ch.step(V.tensor_reduce(ing[:], bigm[:].rearrange("p t (k g) -> p t k g", g=G), AXX, ALU.add))
            for k in range(2):
                ch.step(V.tensor_reduce(top[:, k, :], ing[:], AXX, ALU.max))
                ch.step(V.tensor_copy(toh[:], ing[:]))
                first_index(toh[:], top[:, k, :], i4, EG, tix[:, k, :])
                if k == 0:
                    ch.step(V.tensor_tensor(toh[:], i4, wide(tix[:, k, :], EG), ALU.is_equal))
                    ch.step(V.scalar_tensor_tensor(ing[:], toh[:], -2.0, ing[:], ALU.mult, ALU.add))
                ch.step(V.scalar_tensor_tensor(tix[:, k, :], gmx[:], float(EG), tix[:, k, :], ALU.mult, ALU.add))
                ch.step(V.tensor_tensor(oh[:, k], ie, wide(tix[:, k, :], E), ALU.is_equal))
            ch.step(V.tensor_tensor(rsm[:], top[:, 0, :], top[:, 1, :], ALU.add))
            ch.step(V.reciprocal(rsm[:], rsm[:]))
            for k in range(2):
                ch.open(V.tensor_tensor(gates[:, k, :], top[:, k, :], rsm[:], ALU.mult))
            ch.step(V.memset(base[:, 0, :], 0.0))
            V.tensor_tensor(asg[:], oh[:, 0], oh[:, 1], ALU.add).then_inc(S["assigned"], 1)
            dve.wait_ge(S["prefix_ready"], 2)
            for t in range(NT):
                ch.step(V.tensor_tensor(base[:, t + 1, :], base[:, t, :], psum[7][:, t * E:(t + 1) * E], ALU.add))
            ch.step(V.tensor_tensor(slot[:], base[:, 0:NT, :], psum[6][:].rearrange("p (t e) -> p t e", e=E), ALU.add))
            for k in range(2):
                ch.step(V.tensor_tensor(bigm[:], oh[:, k], slot[:], ALU.mult))
                ch.step(V.tensor_reduce(rank_f[:, k, :], bigm[:], AXX, ALU.add))
                ch.step(V.tensor_tensor(cmpr[:], wide(rank_f[:, k, :], MAXB - 1),
                                        con_s[:, TH0 + 1:TH0 + MAXB].unsqueeze(1).to_broadcast([P, NT, MAXB - 1]), ALU.is_ge))
                ch.step(V.tensor_reduce(blk_t[:, k, :], cmpr[:], AXX, ALU.add))
                ch.step(V.tensor_scalar(slot_f[:, k, :], rank_f[:, k, :], float(E * MAXB), None, ALU.mult))
                ch.step(V.scalar_tensor_tensor(slot_f[:, k, :], tix[:, k, :], float(MAXB), slot_f[:, k, :], ALU.mult, ALU.add))
                ch.step(V.scalar_tensor_tensor(slot_f[:, k, :], blk_t[:, k, :], float(1 - P * E * MAXB), slot_f[:, k, :], ALU.mult, ALU.add))
            V.tensor_copy(slot_i[:], slot_f[:]).then_inc(S["slots_ready"], 1)
            ch.step(V.tensor_tensor(cmpb[:], base[:, NT, :].unsqueeze(2).to_broadcast([P, E, MAXB]),
                                    con_s[:, TH0:TH0 + MAXB].unsqueeze(1).to_broadcast([P, E, MAXB]), ALU.is_gt))
            ch.step(V.tensor_reduce(blk_f[:, 0:E], cmpb[:], AXX, ALU.add))
            ch.step(V.tensor_scalar(blk_f[:, 0:E], blk_f[:, 0:E], 1.0, None, ALU.max))
            ch.step(V.memset(blk_f[:, E:E + 1], 0.0))
            ch.step(V.tensor_tensor_scan(blk_f[:, E + 1:2 * E + 1], blk_f[:, 0:E], blk_f[:, 0:E], 0.0, ALU.add, ALU.bypass))
            ch.step(V.tensor_scalar(blk_f[:, 2 * E + 1:], blk_f[:, E + 1:2 * E + 1], -1.0, None, ALU.add))
            V.tensor_copy(blocks_i[:], blk_f[:]).then_inc(S["blocks_ready"], 1)

            def split_low(e, p):
                wait(dve, "w_hi_done", e * PIECES + (p + 1))
                V.tensor_tensor(w_lo[p][:], piece[p][:], w_hi[p][:].bitcast(F32), ALU.subtract).then_inc(S["w_lo_done"], 1)

            def xT_low(j, half):
                wait(dve, "xh_done", 2 * j + half + 1)
                V.tensor_tensor(xT_lo[:, 4 * half:4 * half + 4, :], psum[2 + half][:].rearrange("p (k n) -> p k n", k=4),
                                xT_hi[:, 4 * half:4 * half + 4, :].bitcast(F32), ALU.subtract).then_inc(S["xl_done"], 1)

            def expert_block(j, e):
                wait(dve, "sig_ready", j + 1)
                wait(dve, "hht_ready", j)
                V.tensor_tensor(hh[:], psum[0][:], sig[:], ALU.mult).then_inc(S["gated"], 1)
                if e is not None:
                    split_low(e, 0)
                wait(dve, "gated", j + 1)
                wait(dve, "u_ready", j + 1)
                V.tensor_tensor(hh[:], psum[1][:], hh[:], ALU.mult).then_inc(S["hh_ready"], 1)
                xT_low(j + 1, 0)
                wait(dve, "hhth_done", j + 1)
                V.tensor_tensor(hhT_lo[:], psum[4][:].rearrange("p (k n) -> p k n", k=KF), hhT_hi[:].bitcast(F32),
                                ALU.subtract).then_inc(S["hhtl_done"], 1)
                xT_low(j + 1, 1)
                if e is not None:
                    for p in range(1, PIECES):
                        split_low(e, p)

            dve.sem_inc(S["hh_ready"], CREDIT["hh_ready"])
            for p in range(PIECES):
                split_low(0, p)
            dve.wait_ge(S["list_st"], 16 * 2 * NT)
            dve.wait_ge(S["blocks_ready"], 1)
            xT_low(0, 0)
            xT_low(0, 1)
            with dve.Fori(0, E - 1) as e:
                n = dve.value_load(blocks_i[0:1, bass.ds(e, 1)], min_val=1, max_val=MAXB)
                first = dve.value_load(blocks_i[0:1, bass.ds(e + E, 1)], min_val=0, max_val=E + MAXB * 2)
                with dve.If(n > 1):
                    with dve.Fori(0, n - 1) as b:
                        expert_block(first + b, None)
                last = dve.value_load(blocks_i[0:1, bass.ds(e + (2 * E + 1), 1)], min_val=0, max_val=E + MAXB * 2)
                expert_block(last, e + 1)
            n = dve.value_load(blocks_i[0:1, E - 1:E], min_val=1, max_val=MAXB)
            first = dve.value_load(blocks_i[0:1, 2 * E - 1:2 * E], min_val=0, max_val=E + MAXB * 2)
            with dve.Fori(0, n) as b:
                expert_block(first + b, None)

            dve.wait_ge(S["experts_done"], 1)
            K_FIN = 2 + 2 + 1 + NEWTON

            def combine(q, s):
                i = q * NF + s
                ch = Chain(dve, "f_steps", i * K_FIN)
                wait(dve, "f_y0", i + 1)
                wait(dve, "f_norm", q * NF)
                fa = fr[:, s, :]
                ch.step(V.scalar_tensor_tensor(fa, fy[:, s, 1, :], gates[:, 1, bass.ds(i, 1)], fa, ALU.mult, ALU.add))
                ch.step(V.scalar_tensor_tensor(fa, fy[:, s, 2, :], ALPHA, fa, ALU.mult, ALU.add))
                for half in range(2):
                    ch.open(V.bn_stats(fst[:, s, 6 * half:6 * half + 6], fa[:, half * 512:(half + 1) * 512]))
                ch.until(ch.n, alone="dve")
                ch.step(V.bn_aggr(fmv[:, s, :], fst[:, s, :]))
                rsqrt(ch, frs[:, s, 0:1], frs[:, s, 2:3], frs[:, s, 3:4], fmv[:, s, 1:2])
                assert ch.n == K_FIN, ch.n
                V.scalar_tensor_tensor(frs[:, s, 1:2], fmv[:, s, 0:1], -1.0, frs[:, s, 0:1],
                                       ALU.mult, ALU.mult).then_inc(S["f_stat"], 1)

            def scale_last(q, s):
                wait(dve, "f_norm", q * NF + (s + 1))
                wait(dve, "row_ld", 32)
                V.tensor_tensor(fr[:, s, :], fr[:, s, :], frow[:, 0, :], ALU.mult).then_inc(S["f_scaled"], 1)

            with dve.Fori(0, NT // NF) as q:
                combine(q, 0)
                for s in range(NF):
                    if s + 1 < NF:
                        combine(q, s + 1)
                    scale_last(q, s)

        @block.gpsimd
        def _(pool):
            def halo(c):
                q, o = c % 2, (c + 1) % 2
                wait(pool, "conv_b_done", (c - 1) * TA, alone="pool")
                wait(pool, "conv_a_done", (c - 1) * TA, alone="pool")
                wait(pool, "pool_d_done", (c - 1) * 4, alone="pool")
                wait(pool, "z_evac", c * NZ, alone="pool")
                wait(pool, "products", c * NPAIR, alone="pool")
                if isinstance(c, int) and c == 0:
                    for buf, w in ((vbuf, KB - 1), (ubuf, KA - 1), (pbuf, HALO)):
                        Q.memset(buf[:, 0, :, 0:w], 0.0).then_inc(S["halos"], 1)
                else:
                    for buf, w in ((vbuf, KB - 1), (ubuf, KA - 1), (pbuf, HALO)):
                        Q.tensor_copy(buf[:, bass.ds(q, 1), :, 0:w].rearrange("p o t n -> p (o t) n"),
                                      buf[:, bass.ds(o, 1), :, CHUNK:CHUNK + w].rearrange("p o t n -> p (o t) n")).then_inc(S["halos"], 1)

            def product(c, p):
                q = c % 2
                wait(pool, "z_evac", c * NZ + (2 * p + 2), alone="pool")
                buf, w, t = (vbuf, KB - 1, p) if p < TA else (ubuf, KA - 1, p - TA)
                Q.tensor_tensor(buf[:, bass.ds(q, 1), t, w:].rearrange("p o n -> p (o n)"), raw[:, 2 * (p % 2), :],
                                raw[:, 2 * (p % 2) + 1, :], ALU.mult).then_inc(S["products"], 1)

            def affine_in(c):
                for i in range(TPC):
                    wait(pool, "norm1", c * TPC + (i + 1), alone="pool")
                    Q.tensor_tensor(xin[:, i, :], xin[:, i, :], rowp[:, 0, :], ALU.mult).then_inc(S["scaled1"], 1)
                    wait(pool, "scaled1", (c * TPC + (i + 1)), alone="pool")
                    Q.tensor_tensor(xin[:, i, :], xin[:, i, :], rowp[:, 1, :], ALU.add).then_inc(S["h_ready"], 1)
                    wait(pool, "h_ready", c * TPC + (i + 1), alone="pool")
                    Q.dma_start(h_dram[bass.ds(c * CHUNK + i * P, P), :], xin[:, i, :]).then_inc(S["h_st"], 16)

            def affine_mix(c, i):
                wait(pool, "norm2", c * TPC + (i + 1), alone="pool")
                r = res[:, i % 2, :]
                Q.tensor_tensor(r, r, rowp[:, 2, :], ALU.mult).then_inc(S["scaled2"], 1)
                wait(pool, "scaled2", c * TPC + (i + 1), alone="pool")
                Q.tensor_tensor(r, r, rowp[:, 3, :], ALU.add).then_inc(S["h2_ready"], 1)
                wait(pool, "h2_ready", c * TPC + (i + 1), alone="pool")
                Q.dma_start(h2_dram[bass.ds(c * CHUNK + i * P, P), :], r).then_inc(S[f"h2_st{i % 2}"], 16)

            def window(c):
                halo(c)
                for p in range(NPAIR):
                    product(c, p)
                affine_in(c + 1)

            Q.memset(onepool[:], 0.0).then_inc(S["set_up"], 1)
            pool.wait_ge(S["set_up"], 3)
            pool.wait_ge(S["const_ld"], 16 * N_CONST)
            affine_in(0)
            window(0)
            with pool.Fori(1, NC) as c:
                window(c)
                for i in range(TPC):
                    affine_mix(c - 1, i)
            for i in range(TPC):
                affine_mix(NC - 1, i)

            pool.wait_ge(S["logits_evac"], NT)
            pool.wait_ge(S["h2_st0"], NT // 2 * 16)
            pool.wait_ge(S["h2_st1"], NT // 2 * 16)
            Q.dma_start(rb[:], router_b[0:1, :].to_broadcast([P, E])).then_inc(S["probs_in"], 16)
            Q.memset(pad[:, :, 0:1], 0).then_inc(S["pads_set"], 1)
            Q.memset(pad[:, :, 1:2], SKIP).then_inc(S["pads_set"], 1)
            pool.wait_ge(S["pads_set"], 2)
            Q.dma_start(list_dram.rearrange("(p n) c -> p n c", p=P), pad[:]).then_inc(S["list_pad_st"], 16)
            pool.wait_ge(S["list_pad_st"], 16)
            pool.wait_ge(S["slots_ready"], 1)
            for t in range(NT):
                for k in range(2):
                    Q.indirect_dma_start(out=list_dram, out_offset=bass.IndirectOffsetOnAxis(ap=slot_i[:, k, t:t + 1], axis=0),
                                         in_=entry_s[:, t, k, :], in_offset=None).then_inc(S["list_st"], 16)
            pool.wait_ge(S["list_st"], 16 * 2 * NT)

            def gather(j, source):
                wait(pool, "x2_ready", j, alone="pool")
                if source is not None:
                    wait(pool, "idx_copied", j * 4 + 4, alone="pool")
                    Q.tensor_copy(idx_g[:], source).then_inc(S["idx_copied"], 1)
                    wait(pool, "idx_copied", j * 4 + 5, alone="pool")
                Q.indirect_dma_start(out=xg[:], out_offset=None, in_=h2_dram,
                                     in_offset=bass.IndirectOffsetOnAxis(ap=idx_g[:, 0:1], axis=0)).then_inc(S["xg_ld"], 16)

            def rows_out():
                Q.indirect_dma_start(out=y_dram, out_offset=bass.IndirectOffsetOnAxis(ap=idx_s[:, 1:2], axis=0),
                                     in_=ysb[:], in_offset=None, bounds_check=SKIP - 1, oob_is_err=False).then_inc(S["y_st"], 16)

            def shift(j, n):
                wait(pool, "y_st", (j + 1) * 16, alone="pool")
                Q.tensor_copy(idx_s[:], idx_h[:, 1, :]).then_inc(S["idx_copied"], 1)
                wait(pool, "idx_copied", n + 1, alone="pool")
                Q.tensor_copy(idx_h[:, 1, :], idx_h[:, 0, :]).then_inc(S["idx_copied"], 1)
                wait(pool, "idx_copied", n + 2, alone="pool")

            def scatter(j):
                wait(pool, "ysb_done", 2 * (j - 1), alone="pool")
                rows_out()

            pool.wait_ge(S["blocks_ready"], 1)
            Q.dma_start(idx_all[:], list_dram.rearrange("(p e b) c -> p e b c", p=P, e=E)).then_inc(S["idx_ld"], 16)
            Q.memset(idx_s[:], SKIP).then_inc(S["idx_copied"], 1)
            Q.memset(idx_h[:], SKIP).then_inc(S["idx_copied"], 1)
            Q.memset(ysb[:], 0.0).then_inc(S["idx_copied"], 1)
            pool.wait_ge(S["idx_copied"], 3)
            rows_out()
            pool.wait_ge(S["idx_ld"], 16)
            Q.tensor_copy(idx_g[:], idx_all[:, 0, 0, :]).then_inc(S["idx_copied"], 1)
            pool.wait_ge(S["idx_copied"], 4)
            with pool.Fori(0, E) as e:
                n = pool.value_load(blocks_i[0:1, bass.ds(e, 1)], min_val=1, max_val=MAXB)
                first = pool.value_load(blocks_i[0:1, bass.ds(e + E, 1)], min_val=0, max_val=E + MAXB * 2)
                with pool.Fori(0, n) as b:
                    j = first + b
                    gather(j, idx_all[:, bass.ds(e, 1), bass.ds(b, 1), :].rearrange("p o q c -> p (o q c)"))
                    shift(j, j * 4 + 5)
                    Q.tensor_copy(idx_h[:, 0, :], idx_g[:]).then_inc(S["idx_copied"], 1)
                    scatter(j)
            total = pool.value_load(blocks_i[0:1, 2 * E:2 * E + 1], min_val=E, max_val=E + MAXB * 2)
            gather(total, None)
            shift(total, total * 4 + 4)
            scatter(total)
            shift(total + 1, total * 4 + 6)
            scatter(total + 1)
            wait(pool, "y_st", total * 16 + 48, alone="pool")
            wait(pool, "xg_ld", total * 16 + 16, alone="pool")
            wait(pool, "xh_done", total * 2 + 2, alone="pool")
            wait(pool, "xl_done", total * 2 + 2, alone="pool")
            Q.memset(onepool[:], 0.0).then_inc(S["experts_done"], 1)

            pool.wait_ge(S["row_ld"], 32)
            with pool.Fori(0, NT // NF) as q:
                for s in range(NF):
                    wait(pool, "f_scaled", q * NF + (s + 1), alone="pool")
                    Q.tensor_tensor(fr[:, s, :], fr[:, s, :], frow[:, 1, :], ALU.add).then_inc(S["f_out"], 1)

    stack.close()


def kernel(x, ln_in_g, ln_in_b, router_w, router_b, w_in, conv_a_w, conv_b_w, conv_b_b, ln_conv_g, ln_conv_b,
           pool_w, pool_scale, w_out, ln_mix_g, ln_mix_b, w_gate, w_up, w_down, ln_ffn_g, ln_ffn_b):
    import concourse.bacc as bacc
    from concourse.bass_utils import run_bass_kernel_spmd

    a = lambda v: np.ascontiguousarray(v)
    con, entry = constants()
    taps = lambda w, n: np.asarray(w)[0].reshape(n, TA, P).transpose(2, 1, 0).reshape(P, TA * n)
    chan = lambda v: np.asarray(v)[0].reshape(-1, P).T
    rw = np.asarray(router_w).reshape(KD, P, E).transpose(1, 0, 2).reshape(P, KD * E)
    params = np.concatenate([taps(conv_a_w, KA), taps(conv_b_w, KB), chan(conv_b_b), chan(ln_conv_g),
                             chan(ln_conv_b), chan(pool_scale), rw], axis=1)
    rows = np.stack([np.asarray(v).reshape(D) for v in (ln_in_g, ln_in_b, ln_mix_g, ln_mix_b, ln_ffn_g, ln_ffn_b)])
    win = np.asarray(w_in)[0].reshape(KD, P, NZ, P).transpose(2, 1, 0, 3).reshape(NZ, P, KD * P)[z_order()]
    ins = {
        "x": a(np.asarray(x)[0]), "w_in": a(win), "w_out": a(np.asarray(w_out)[0]),
        "w_gate": a(np.asarray(w_gate)[0]), "w_up": a(np.asarray(w_up)[0]), "w_down": a(np.asarray(w_down)[0]),
        "pool_w": a(np.asarray(pool_w)[0]), "params": a(params), "rows": a(rows),
        "router_b": a(np.asarray(router_b).reshape(1, E)), "con": a(con), "entry": a(entry),
    }
    nc = bacc.Bacc("TRN2", target_bir_lowering=False, num_devices=1)
    args = {n: nc.dram_tensor(f"in_{n}", v.shape, mybir.dt.from_np(v.dtype), kind="ExternalInput").ap() for n, v in ins.items()}
    out = nc.dram_tensor("out_rows", (SEQ, D), F32, kind="ExternalOutput").ap()
    program(nc, out=out, **args)
    r = run_bass_kernel_spmd(nc, [{f"in_{n}": v for n, v in ins.items()}], core_ids=[0])
    return r.results[0]["out_rows"].reshape(1, SEQ, D)
```

```python
from contextlib import ExitStack

import concourse.bass as bass
import numpy as np
from concourse import mybir

F32 = mybir.dt.float32
I32 = mybir.dt.int32
F32R = mybir.dt.float32r
ALU = mybir.AluOpType
ACT = mybir.ActivationFunctionType
AXX = mybir.AxisListType.X

P = 128
SEQ = 2048
D = 1024
KD = D // P
CHUNK = 512
NC = SEQ // CHUNK
TPC = CHUNK // P
NT = SEQ // P
DA = 3 * D // 8
TA = DA // P
DP = D - 2 * DA
TP = DP // P
WINDOWS = (2, 4, 8, 16)
GROUP = DP // len(WINDOWS)
KA, KB = 3, 31
HALO = max(WINDOWS) - 1
NZ = 3 * TA + 2 * TA + TP
NPAIR = 2 * TA
RING = 3
KS = 7
KS_EVEN, KS_ODD = (KS + 1) // 2, KS // 2
NORM_AT = 5
EARLY_AT = (0, 21, 24, 27, 30)
EARLY = EARLY_AT[-1]
EPS = 1e-5
ALPHA = 2.0 ** 0.25
E = 32
G = 8
EG = E // G
F = D // 2
KF = F // P
CAP = SEQ
MAXB = CAP // P
PIECES = 6
PADS = 8 * P
SKIP = 2 * SEQ
RSQRT_SEED = float(0x5F3759DF)

CA0 = 0
CB0 = CA0 + TA * KA
CBB0 = CB0 + TA * KB
LCG0 = CBB0 + TA
LCB0 = LCG0 + TA
PS0 = LCB0 + TA
RW0 = PS0 + TP
NPAR = RW0 + KD * E
ID0 = 0
TRI0 = ID0 + P
IG0 = TRI0 + P
IE0 = IG0 + G
TH0 = IE0 + E
WI0 = TH0 + MAXB
PT0 = WI0 + TP
NCON = PT0 + NC * TP * 16


def constants():
    c = np.zeros((P, NCON), np.float32)
    c[:, ID0:ID0 + P] = np.eye(P)
    c[:, TRI0:TRI0 + P] = np.triu(np.ones((P, P)), 1)
    c[:, IG0:IG0 + G] = np.arange(G)
    c[:, IE0:IE0 + E] = np.arange(E)
    c[:, TH0:TH0 + MAXB] = np.arange(MAXB) * P
    for t in range(TP):
        for half in range(2):
            w = WINDOWS[2 * t + half]
            rows = slice(half * GROUP, (half + 1) * GROUP)
            c[rows, WI0 + t] = 1.0 / w
            for k in range(NC):
                pos = k * CHUNK + np.arange(16) + 1
                at = PT0 + (k * TP + t) * 16
                c[rows, at:at + 16] = 1.0 / np.minimum(pos, w)
    token = np.arange(NT)[None, :] * P + np.arange(P)[:, None]
    entry = np.zeros((P, NT, 2, 2), np.int32)
    for k in range(2):
        entry[:, :, k, 0] = token
        entry[:, :, k, 1] = token + k * SEQ
    return c, entry.reshape(P, NT * 4)


def z_order():
    b_val, b_gate = 3 * TA, 4 * TA
    order = []
    for t in range(TA):
        order += [b_val + t, b_gate + t]
    for t in range(TA):
        order += [TA + t, 2 * TA + t]
    order += list(range(TA))
    order += [5 * TA + t for t in range(TP)]
    return order


def program(nc, x, w_in, w_out, w_gate, w_up, w_down, pool_w, params, rows, router_b, con, entry, out):
    stack = ExitStack()
    sb = lambda name, shape, dt=F32: stack.enter_context(nc.sbuf_tensor(name, shape, dt))

    h_dram = nc.dram_tensor("h_scratch", [(NC + 1) * CHUNK, D], F32).ap()
    h2_dram = nc.dram_tensor("h2_scratch", [SEQ, D], F32).ap()
    list_dram = nc.dram_tensor("token_lists", [E * CAP, 2], I32).ap()
    credit_dram = nc.dram_tensor("credit_scratch", [TPC, D], F32).ap()
    y_dram = nc.dram_tensor("expert_rows", [2 * SEQ, D], F32).ap()

    con_s = sb("con_s", [P, NCON])
    onepool = sb("onepool", [P, 2])
    entry_s = sb("entry_s", [P, NT, 2, 2], I32)
    gates = sb("gates", [P, 2, NT])
    blocks_i = sb("blocks_i", [P, 3 * E + 1], I32)
    lg = sb("lg", [P, NT, E])
    rb = sb("rb", [P, E])
    pad = sb("pad", [P, CAP * E // PADS, 2], I32)
    ident = con_s[:, ID0:ID0 + P]

    mixer = ExitStack()
    ma = lambda name, shape, dt=F32: mixer.enter_context(nc.sbuf_tensor(name, shape, dt))
    win = [ma(f"win{s}", [P, KD, P]) for s in range(RING)]
    hT_hi = ma("hT_hi", [P, KS, CHUNK], F32R)
    hT_lo = ma("hT_lo", [P, KS, CHUNK], F32R)
    hT = ma("hT", [P, KD - KS, CHUNK])
    win_hi = ma("win_hi", [P, 2, KS, P], F32R)
    win_lo = ma("win_lo", [P, 2, KS, P], F32R)
    xin = ma("xin", [P, TPC, D])
    wout = ma("wout", [P, KD, D])
    raw = ma("raw", [P, 4, CHUNK])
    vbuf = ma("vbuf", [P, TA, KB - 1 + CHUNK])
    ubuf = ma("ubuf", [P, TA, KA - 1 + CHUNK])
    pbuf = ma("pbuf", [P, TP, HALO + CHUNK])
    gb = ma("gb", [P, TA, CHUNK])
    cb = ma("cb", [P, TA, CHUNK])
    rs = ma("rs", [P, 2, HALO + CHUNK])
    dp = ma("dp", [P, TP, CHUNK])
    yT = ma("yT", [P, KD, CHUNK])
    sq = yT[:, TA:2 * TA, :]
    rt = yT[:, 2 * TA, :]
    h2T = raw[:, 0:2, :].rearrange("p a (k n) -> p (a k) n", n=P)
    res = ma("res", [P, TPC, D])
    rowp = ma("rowp", [P, 4, D])
    par = ma("par", [P, NPAR])
    pw = ma("pw", [P, TP, P])
    onesd = ma("onesd", [P, P])
    bst = ma("bst", [P, 12])
    mv = ma("mv", [P, 2, TPC, 2])
    rstd = ma("rstd", [P, 2, TPC])
    nmr = ma("nmr", [P, 2, TPC])
    nwt = ma("nwt", [P, TPC])
    nwv = ma("nwv", [P, TPC])
    mixer.close()

    router = ExitStack()
    mr = lambda name, shape, dt=F32: router.enter_context(nc.sbuf_tensor(name, shape, dt))
    _under = mr("under", [P, 36 * D])
    pr = mr("pr", [P, NT, E])
    lr = mr("lr", [P, NT, E])
    rsm = mr("rsm", [P, NT])
    pairs = mr("pairs", [P, NT, G, 6])
    gs = mr("gs", [P, NT, G])
    goh = mr("goh", [P, NT, G])
    gmx = mr("gmx", [P, NT])
    ing = mr("ing", [P, NT, EG])
    toh = mr("toh", [P, NT, EG])
    bigm = mr("bigm", [P, NT, E])
    top = mr("top", [P, 2, NT])
    tix = mr("tix", [P, 2, NT])
    oh = mr("oh", [P, 2, NT, E])
    asg = mr("asg", [P, NT, E])
    base = mr("base", [P, NT + 1, E])
    slot = mr("slot", [P, NT, E])
    slot_f = mr("slot_f", [P, 2, NT])
    slot_i = mr("slot_i", [P, 2, NT], I32)
    cmpb = mr("cmpb", [P, E, MAXB])
    blk_f = mr("blk_f", [P, 3 * E + 1])
    rank_f = mr("rank_f", [P, 2, NT])
    blk_t = mr("blk_t", [P, 2, NT])
    cmpr = mr("cmpr", [P, NT, MAXB - 1])
    onesr = mr("onesr", [P, P])
    router.close()

    moe = ExitStack()
    mo = lambda name, shape, dt=F32: moe.enter_context(nc.sbuf_tensor(name, shape, dt))
    piece = [mo(f"piece{p}", [P, 4, F] if p < 4 else [P, 2, D]) for p in range(PIECES)]
    w_hi = [mo(f"w_hi{p}", [P, 4, F] if p < 4 else [P, 2, D], F32R) for p in range(PIECES)]
    w_lo = [mo(f"w_lo{p}", [P, 4, F] if p < 4 else [P, 2, D], F32R) for p in range(PIECES)]
    xg = mo("xg", [P, D])
    xT_hi = mo("xT_hi", [P, KD, P], F32R)
    xT_lo = mo("xT_lo", [P, KD, P], F32R)
    sig = mo("sig", [P, F])
    hh = mo("hh", [P, F])
    hhT_hi = mo("hhT_hi", [P, KF, P], F32R)
    hhT_lo = mo("hhT_lo", [P, KF, P], F32R)
    ysb = mo("ysb", [P, D])
    idx_all = mo("idx_all", [P, E, MAXB, 2], I32)
    idx_g = mo("idx_g", [P, 2], I32)
    idx_h = mo("idx_h", [P, 2, 2], I32)
    idx_s = mo("idx_s", [P, 2], I32)
    moe.close()

    final = ExitStack()
    mf = lambda name, shape, dt=F32: final.enter_context(nc.sbuf_tensor(name, shape, dt))
    NF = 8
    fres = mf("fres", [P, NF, D])
    frow = mf("frow", [P, 2, D])
    _over = mf("over", [P, 2 * D])
    fy = mf("fy", [P, NF, 2, D])
    fr = mf("fr", [P, NF, D])
    dg = mf("dg", [P, 4, 2, P])
    alpha_d = mf("alpha_d", [P, P])
    fst = mf("fst", [P, NF, 12])
    fmv = mf("fmv", [P, NF, 2])
    frs = mf("frs", [P, 4, NF])
    final.close()

    psum = [stack.enter_context(nc.psum_tensor(f"bank{b}", [P, 512], F32)) for b in range(8)]

    names = [
        "first_ld", "const_ld", "wout_ld", "x_ld", "h_st", 
        "list_pad_st", "list_st", "row_ld",
        "set_up", "h_ready", "z_ready", "z_evac", "products", "tA_ready", "tA_evac", "tB_ready", "tB_evac",
        "halos", "conv_b_done", "conv_a_done", "pool_d_done", "mean_ready", "centred", "squares", "var_ready",
        "b_norm", "b_sig", "y_done", "pool_y_ready", "yc_done", "ln_stat", "norm1", "mix_ready", "mix_taken",
        "mix_stat", "norm2", "h2_ready", "logits_ready", "logits_evac",
        "ln_steps", "mix_steps", "conv_b_steps", "b_norm_steps", "conv_a_steps", "pool_steps",
        "route_steps", "scaled1", "scaled2", "pads_set",
        "win_hi_done", "win_lo_done", "tA_low", "tB_high",
        "passed_sp", "passed_pool", "passed_dve", "passed_pe", "passed_act",
        "assigned", "prefix_ready", "slots_ready", "blocks_ready", "exp_in", "exp_out",
        "idx_ld", "xg_ld", "y_st",
        "w_hi_done", "w_lo_done", "x1_ready", "x2_ready", "xh_done", "xl_done",
        "g_ready", "u_ready", "sig_ready", "hh_ready", "hht_ready", "hhth_done", "hhtl_done",
        "yp_ready", "ysb_done", "idx_copied", "gated", "experts_done",
        "f_diag", "f_alpha", "f_sum", "f_stat", "f_norm", "f_scaled", "f_out", "f_steps",
    ] + [f"win_ld{s}" for s in range(RING)] + [f"piece_ld{p}" for p in range(PIECES)] + [
        f"{n}{s}" for n in ("f_ld", "o_st") for s in range(8)] + [
        f"{n}{i}" for n in ("hres_ld", "h2_st") for i in range(TPC)]
    S = {n: stack.enter_context(nc.semaphore(n)) for n in names}

    N_FIRST = 3
    N_CONST = 5 + 2 * TP

    CREDIT = {"hh_ready": 1, "hht_ready": 1, "yp_ready": 1, "x2_ready": 1, "ysb_done": 3, "conv_a_done": 1,
              "conv_b_done": 1, "pool_d_done": 1, "logits_ready": 1, "f_norm": 16, "f_sum": 4, "b_norm": 1, "norm2": 1, "logits_evac": 1,
              "mix_taken": 1, **{f"h2_st{i}": 16 for i in range(TPC)}}

    def wait(eng, name, value, alone=""):
        value = value + CREDIT.get(name, 0)
        if isinstance(value, int) and value <= 0:
            return
        if alone and not isinstance(value, int):
            eng.wait_ge(S[name], value).then_inc(S["passed_" + alone], 1)
            return
        eng.wait_ge(S[name], value)

    class Chain:

        def __init__(self, eng, name, first):
            self.eng, self.name, self.first, self.n = eng, name, first, 0

        def step(self, instruction):
            instruction.then_inc(S[self.name], 1)
            self.n += 1
            self.eng.wait_ge(S[self.name], self.first + self.n)

        def signal(self, instruction, name, count):
            instruction.then_inc(S[name], 1)
            self.eng.wait_ge(S[name], count)

        def open(self, instruction):
            instruction.then_inc(S[self.name], 1)
            self.n += 1
            return self.n

        def until(self, n, alone=""):
            wait(self.eng, self.name, self.first + n, alone)

    V, A, T, Q, = nc.vector, nc.scalar, nc.tensor, nc.gpsimd

    NEWTON = 11

    def rsqrt(chain, y, v, t, eps_of):
        chain.step(V.tensor_scalar(v, eps_of, EPS, None, ALU.add))
        chain.step(V.tensor_scalar(y.bitcast(I32), v.bitcast(I32), -0.5, RSQRT_SEED, ALU.mult, ALU.add))
        for _ in range(3):
            chain.step(V.scalar_tensor_tensor(t, y, -0.5, y, ALU.mult, ALU.mult))
            chain.step(V.tensor_tensor(t, t, v, ALU.mult))
            chain.step(V.scalar_tensor_tensor(y, t, 1.5, y, ALU.add, ALU.mult))

    def par_col(base, n=1):
        return par[:, base:base + n]

    ring_uses = [len(range(s, NZ, RING)) for s in range(RING)]

    K_LN = 3 * TPC + NEWTON
    K_MIX = 3 + NEWTON
    K_CONV = TA * (KB - 1)
    K_CLN = NEWTON + TA
    K_CONVA = KA * TA
    K_DPOOL0 = 2 * 2 + 2
    K_DPOOL = K_DPOOL0 + 2 * 2 + 4

    with nc.Block() as block:

        @block.sync
        def _(sp):
            for i in range(TPC):
                sp.dma_start(xin[:, i, :], x[i * P:(i + 1) * P, :]).then_inc(S["x_ld"], 16)
            for i in range(2):
                sp.dma_start(rowp[:, i, :], rows[i:i + 1, :].to_broadcast([P, D])).then_inc(S["first_ld"], 16)
            sp.dma_start(con_s[:], con[:, :]).then_inc(S["first_ld"], 16)

            def load_x(c):
                wait(sp, "tB_ready", 4 if isinstance(c, int) else (c - 1) * 8, alone="sp")
                wait(sp, "h_st", c * (16 * TPC), alone="sp")
                src = x_of(c)
                for i in range(TPC):
                    sp.dma_start(xin[:, i, :], src(i)).then_inc(S["x_ld"], 16)

            def x_of(c):
                if isinstance(c, int):
                    c0 = (c % NC) * CHUNK
                else:
                    c0 = (c % NC) * CHUNK
                return lambda i: x[bass.ds(c0 + i * P, P), :]

            def load_win(c, m):
                s = m % RING
                if m >= RING:
                    wait(sp, "z_ready", c * NZ + (m - RING + 1), alone="sp")
                elif not (isinstance(c, int) and c == 0):
                    wait(sp, "z_ready", (c - 1) * NZ + (s + RING * (ring_uses[s] - 1) + 1), alone="sp")
                sp.dma_start(win[s][:], w_in[m].rearrange("p (k n) -> p k n", k=KD)).then_inc(S[f"win_ld{s}"], 16)

            def load_res(c):
                wait(sp, "h_st", (c + 3) * (16 * TPC) if not isinstance(c, int) else min(c + 3, NC + 1) * 16 * TPC, alone="sp")
                wait(sp, "tB_ready", c * 8 + 8, alone="sp")
                for i in range(TPC):
                    wait(sp, f"h2_st{i}", c * 16, alone="sp")
                    sp.dma_start(res[:, i, :], h_dram[bass.ds(c * CHUNK + i * P, P), :]).then_inc(S[f"hres_ld{i}"], 16)

            for m in range(RING):
                load_win(0, m)
            sp.dma_start(par[:], params[:, :]).then_inc(S["const_ld"], 16)
            sp.dma_start(entry_s[:], entry.rearrange("p (t k c) -> p t k c", k=2, c=2)).then_inc(S["const_ld"], 16)
            for i in range(2, 4):
                sp.dma_start(rowp[:, i, :], rows[i:i + 1, :].to_broadcast([P, D])).then_inc(S["const_ld"], 16)
            sp.dma_start(rb[:], router_b[0:1, :].to_broadcast([P, E])).then_inc(S["const_ld"], 16)
            sp.wait_ge(S["set_up"], 2)
            for t in range(TP):
                for half in range(2):
                    g = slice(half * GROUP, (half + 1) * GROUP)
                    sp.dma_start(pw[g, t, g], pool_w[2 * t + half]).then_inc(S["const_ld"], 16)
            sp.dma_start(wout[:], w_out.rearrange("(k p) n -> p k n", p=P)).then_inc(S["wout_ld"], 16)
            sp.wait_ge(S["pads_set"], 2)
            n = CAP * E // PADS
            for i in range(PADS // P):
                sp.dma_start(list_dram[i * P * n:(i + 1) * P * n, :].rearrange("(p n) c -> p n c", p=P), pad[:]).then_inc(S["list_pad_st"], 16)

            def window(c):
                load_x(c + 1)
                for m in range(RING, NZ):
                    load_win(c, m)

            window(0)
            with sp.Fori(1, NC) as c:
                for m in range(RING):
                    load_win(c, m)
                window(c)
                load_res(c - 1)
            load_res(NC - 1)

            def load_piece(e, p):
                if not isinstance(e, int):
                    wait(sp, "w_lo_done", (e - 1) * PIECES + (p + 1), alone="sp")
                k = 4 * (p % 2) if p < 4 else 2 * (p % 2)
                w = (w_gate, w_up, w_down)[p // 2][bass.ds(e, 1), k * P:(k + (4 if p < 4 else 2)) * P, :]
                sp.dma_start(piece[p][:], w.rearrange("o (k p) f -> p (o k) f", p=P)).then_inc(S[f"piece_ld{p}"], 16)

            sp.wait_ge(S["z_ready"], NC * NZ)
            sp.wait_ge(S["tA_ready"], 8 * NC + TPC)
            sp.wait_ge(S["tB_ready"], 8 * NC + TPC)
            sp.wait_ge(S["h_st"], (NC + 1) * TPC * 16)
            for p in range(PIECES):
                load_piece(0, p)
            with sp.Fori(1, E) as e:
                for p in range(PIECES):
                    load_piece(e, p)

            def load_residual(q, s):
                sp.dma_start(fres[:, s, :], h2_dram[bass.ds((q * NF + s) * P, P), :]).then_inc(S[f"f_ld{s}"], 16)

            def load_rows(q, s):
                for k in range(2):
                    sp.dma_start(fy[:, s, k, :], y_dram[bass.ds((q * NF + s) * P + k * SEQ, P), :]).then_inc(S[f"f_ld{s}"], 16)

            sp.wait_ge(S["w_lo_done"], E * PIECES)
            for i in range(2):
                sp.dma_start(frow[:, i, :], rows[4 + i:5 + i, :].to_broadcast([P, D])).then_inc(S["row_ld"], 16)
            for s in range(NF):
                load_residual(0, s)
            sp.wait_ge(S["experts_done"], 1)

            def store_tile(q, s):
                wait(sp, "f_out", q * NF + (s + 1), alone="sp")
                sp.dma_start(out[bass.ds((q * NF + s) * P, P), :], fr[:, s, :]).then_inc(S[f"o_st{s}"], 16)

            for s in range(NF):
                load_rows(0, s)
            with sp.Fori(1, NT // NF) as q:
                for s in range(NF):
                    store_tile(q - 1, s)
                    load_residual(q, s)
                    load_rows(q, s)
            for s in range(NF):
                store_tile(NT // NF - 1, s)
            for s in range(NF):
                sp.wait_ge(S[f"o_st{s}"], 16 * (NT // NF))

        @block.tensor
        def _(pe):
            def x_transposes(c, fill):
                wait(pe, "h_ready", c * TPC + TPC)
                for j in range(KD):
                    wait(pe, ("tA_evac", "tB_evac")[j % 2], fill + j // 2)
                    if j % 2 == 0:
                        wait(pe, "tA_low", c * KS_EVEN + min(j // 2, KS_EVEN))
                    for i in range(TPC):
                        last = T.transpose(psum[2 + j % 2][:, i * P:(i + 1) * P], xin[:, i, j * P:(j + 1) * P], ident)
                    last.then_inc(S[("tA_ready", "tB_ready")[j % 2]], 1)

            def projection(c, m):
                s = m % RING
                wait(pe, f"win_ld{s}", (c * ring_uses[s] + (m // RING + 1)) * 16)
                wait(pe, "z_evac", c * NZ + (m - 1 if m >= 2 else -m))
                for k in range(KS, KD):
                    T.matmul(psum[m % 2][:], win[s][:, k, :], hT[:, k - KS, :], start=(k == KS), stop=False)
                wait(pe, "win_lo_done", c * NZ + m + 1)
                hi, lo = win_hi[:, m % 2], win_lo[:, m % 2]
                for k in range(KS):
                    T.matmul(psum[m % 2][:], hi[:, k, :], hT_hi[:, k, :], start=False, stop=False)
                    T.matmul(psum[m % 2][:], hi[:, k, :], hT_lo[:, k, :], start=False, stop=False)
                    last = T.matmul(psum[m % 2][:], lo[:, k, :], hT_hi[:, k, :], start=False, stop=(k == KS - 1))
                last.then_inc(S["z_ready"], 1)

            def channel_mean(c):
                wait(pe, "conv_b_done", c * TA + TA)
                for t in range(TA):
                    last = T.matmul(psum[4][:], onesd[:], cb[:, t, :], start=(t == 0), stop=(t == TA - 1))
                last.then_inc(S["mean_ready"], 1)

            def channel_variance(c):
                wait(pe, "squares", c * TA + TA)
                for t in range(TA):
                    last = T.matmul(psum[5][:], onesd[:], sq[:, t, :], start=(t == 0), stop=(t == TA - 1))
                last.then_inc(S["var_ready"], 1)

            def pool_maps(c):
                wait(pe, "pool_d_done", c * 4 + 4)
                for t in range(TP):
                    T.matmul(psum[6 + t][:], pw[:, t, :], dp[:, t, :], start=True, stop=True).then_inc(S["pool_y_ready"], 1)

            def mix(c, i):
                if i == 0:
                    wait(pe, "conv_a_done", (c + 1) * TA)
                    wait(pe, "y_done", (c + 1) * TA)
                    wait(pe, "yc_done", (c + 1) * TP)
                wait(pe, "mix_taken", c * (2 * TPC) + 2 * (i - 1) if i >= 2 else c * (2 * TPC))
                for half in range(2):
                    bank = psum[4 + 2 * (i % 2) + half]
                    for k in range(KD):
                        last = T.matmul(bank[:], yT[:, k, i * P:(i + 1) * P], wout[:, k, half * 512:(half + 1) * 512],
                                        start=(k == 0), stop=(k == KD - 1))
                last.then_inc(S["mix_ready"], 1)

            def route(c, i, fill):
                wait(pe, "h2_ready", c * TPC + (i + 1))
                wait(pe, "tA_low", (NC + 1) * KS_EVEN if isinstance(c, int) else (c + (2 if i < 2 else 3)) * KS_EVEN)
                for half in range(2):
                    wait(pe, ("tA_evac", "tB_evac")[half], fill)
                    for j in range(4):
                        k = 4 * half + j
                        last = T.transpose(psum[2 + half][:, j * P:(j + 1) * P], res[:, i, k * P:(k + 1) * P], ident)
                    last.then_inc(S[("tA_ready", "tB_ready")[half]], 1)
                wait(pe, "tA_evac", fill + 1)
                wait(pe, "tB_evac", fill + 1)
                wait(pe, "logits_evac", c * TPC + i)
                for k in range(KD):
                    last = T.matmul(psum[0][:, 0:E], h2T[:, k, :], par[:, RW0 + k * E:RW0 + (k + 1) * E],
                                    start=(k == 0), stop=(k == KD - 1))
                last.then_inc(S["logits_ready"], 1)

            def window(c, conv):
                wait(pe, "tA_evac", 4 if isinstance(c, int) else c * 8)
                wait(pe, "tB_evac", 4 if isinstance(c, int) else c * 8)
                wait(pe, "tA_low", (c + 1) * KS_EVEN)
                wait(pe, "logits_evac", (c - 1) * TPC)
                for m in range(NZ):
                    projection(c, m)
                    if conv and m == 4:
                        channel_mean(c - 1)
                    if conv and m == 7:
                        channel_variance(c - 1)
                    if conv and m == 11:
                        pool_maps(c - 1)

            def mix_and_route(c, first, transposes):
                mix(c, 0)
                mix(c, 1)
                mix(c, 2)
                route(c, 0, first)
                mix(c, 3)
                route(c, 1, first + 1)
                if transposes:
                    x_transposes(c + 2, first + 2)
                after = first + (6 if transposes else 2)
                route(c, 2, after)
                route(c, 3, after + 1)

            pe.sem_inc(S["logits_ready"], CREDIT["logits_ready"])
            pe.wait_ge(S["first_ld"], 16 * N_FIRST)
            x_transposes(0, 0)
            window(0, False)
            x_transposes(1, 4)
            pe.wait_ge(S["const_ld"], 16 * N_CONST)
            pe.wait_ge(S["set_up"], 2)
            pe.wait_ge(S["wout_ld"], 16)
            with pe.Fori(1, NC) as c:
                window(c, True)
                mix_and_route(c - 1, c * 8, True)
            channel_mean(NC - 1)
            channel_variance(NC - 1)
            pool_maps(NC - 1)
            mix_and_route(NC - 1, 8 * NC, False)

            pe.wait_ge(S["assigned"], 1)
            flat = asg[:].rearrange("p t e -> p (t e)")
            T.matmul(psum[6][:], con_s[:, TRI0:TRI0 + P], flat, start=True, stop=True).then_inc(S["prefix_ready"], 1)
            T.matmul(psum[7][:], onesr[:], flat, start=True, stop=True).then_inc(S["prefix_ready"], 1)

            def block_transpose(j, half):
                wait(pe, "xg_ld", (j + 1) * 16)
                wait(pe, "xh_done", 2 * j)
                wait(pe, "xl_done", 2 * j)
                for k in range(4):
                    kk = half * 4 + k
                    last = T.transpose(psum[2 + half][:, k * P:(k + 1) * P], xg[:, kk * P:(kk + 1) * P], ident)
                last.then_inc(S[("x1_ready", "x2_ready")[half]], 1)

            def split_product(bank, lhs_hi, lhs_lo, rhs_hi, rhs_lo, start, stop):
                T.matmul(bank, lhs_hi, rhs_hi, start=start, stop=False)
                T.matmul(bank, lhs_hi, rhs_lo, start=False, stop=False)
                return T.matmul(bank, lhs_lo, rhs_hi, start=False, stop=stop)

            def piece_split(e, p):
                wait(pe, "w_hi_done", e * PIECES + (p + 1))
                wait(pe, "w_lo_done", e * PIECES + (p + 1))

            def expert_block(j, e):
                wait(pe, "xh_done", 2 * j + 2)
                wait(pe, "xl_done", 2 * j + 2)
                wait(pe, "hh_ready", 2 * j)
                for b in range(2):
                    for k in range(KD):
                        p = 2 * b + k // 4
                        if k % 4 == 0:
                            piece_split(e, p)
                        last = split_product(psum[b][:], xT_hi[:, k, :], xT_lo[:, k, :], w_hi[p][:, k % 4, :],
                                             w_lo[p][:, k % 4, :], k == 0, k == KD - 1)
                    last.then_inc(S[("g_ready", "u_ready")[b]], 1)
                block_transpose(j + 1, 0)
                for half in range(2):
                    wait(pe, "hh_ready", 2 * j + (half + 1))
                    for k in range(2 * half, 2 * half + 2):
                        last = T.transpose(psum[4 if half == 0 else 7][:, k * P:(k + 1) * P], hh[:, k * P:(k + 1) * P], ident)
                    last.then_inc(S["hht_ready"], 1)
                block_transpose(j + 1, 1)
                for half in range(2):
                    cols = slice(half * 512, (half + 1) * 512)
                    bank = psum[5 + half][:]
                    wait(pe, "ysb_done", 2 * j + half - 1)
                    for k in range(KF):
                        p = 4 + k // 2
                        if half == 0 and k % 2 == 0:
                            wait(pe, "hhth_done", 2 * j + (k // 2 + 1))
                            piece_split(e, p)
                        T.matmul(bank, hhT_hi[:, k, :], w_hi[p][:, k % 2, cols], start=(k == 0), stop=False)
                        T.matmul(bank, hhT_hi[:, k, :], w_lo[p][:, k % 2, cols], start=False, stop=False)
                    if half == 0:
                        wait(pe, "hhtl_done", 2 * j + 2)
                    for k in range(KF):
                        last = T.matmul(bank, hhT_lo[:, k, :], w_hi[4 + k // 2][:, k % 2, cols], start=False, stop=(k == KF - 1))
                    last.then_inc(S["yp_ready"], 1)

            pe.sem_inc(S["x2_ready"], CREDIT["x2_ready"])
            pe.sem_inc(S["hht_ready"], CREDIT["hht_ready"])
            pe.sem_inc(S["yp_ready"], CREDIT["yp_ready"])
            pe.wait_ge(S["list_st"], 16 * 2 * NT)
            block_transpose(0, 0)
            block_transpose(0, 1)
            with pe.Fori(0, E) as e:
                n = pe.value_load(blocks_i[0:1, bass.ds(e, 1)], min_val=1, max_val=MAXB)
                first = pe.value_load(blocks_i[0:1, bass.ds(e + E, 1)], min_val=0, max_val=E + MAXB * 2)
                with pe.Fori(0, n) as b:
                    expert_block(first + b, e)

            pe.sem_inc(S["f_sum"], CREDIT["f_sum"])
            pe.wait_ge(S["experts_done"], 1)
            pe.wait_ge(S["f_alpha"], 1)
            with pe.Fori(0, NT // NF) as q:
                for s in range(NF):
                    wait(pe, f"f_ld{s}", q * 48 + 48)
                    wait(pe, "f_diag", (q * NF + s) * 2 + 2)
                    wait(pe, "f_norm", (q * NF + s - 3) * 2)
                    for half in range(2):
                        cols = slice(half * 512, (half + 1) * 512)
                        bank = psum[2 * (s % 4) + half][:]
                        T.matmul(bank, dg[:, s % 4, 0, :], fy[:, s, 0, cols], start=True, stop=False)
                        T.matmul(bank, dg[:, s % 4, 1, :], fy[:, s, 1, cols], start=False, stop=False)
                        last = T.matmul(bank, alpha_d[:], fres[:, s, cols], start=False, stop=True)
                    last.then_inc(S["f_sum"], 1)

        @block.scalar
        def _(act):
            def z_copy(c, m):
                wait(act, "z_ready", c * NZ + (m + 1))
                if m < 2 * NPAIR:
                    p, second = divmod(m, 2)
                    wait(act, "products", c * NPAIR + (p - 1))
                    func = ACT.Sigmoid if second and p < TA else ACT.Copy
                    A.activation(raw[:, 2 * (p % 2) + second, :], psum[m % 2][:], func).then_inc(S["z_evac"], 1)
                elif m < 2 * NPAIR + TA:
                    wait(act, "conv_a_done", c * TA)
                    t = m - 2 * NPAIR
                    A.activation(gb[:, t, :], psum[m % 2][:], ACT.Copy).then_inc(S["z_evac"], 1)
                else:
                    wait(act, "halos", c * 3 + 3)
                    t = m - 2 * NPAIR - TA
                    A.activation(pbuf[:, t, HALO:], psum[m % 2][:], ACT.Copy).then_inc(S["z_evac"], 1)

            def squares(c):
                for t in range(TA):
                    wait(act, "centred", c * TA + (t + 1))
                    A.activation(sq[:, t, :], cb[:, t, :], ACT.Square).then_inc(S["squares"], 1)

            def conv_b_sigmoid(c):
                for t in range(TA):
                    wait(act, "b_norm", c * TA + (t + 1))
                    A.activation(sq[:, t, :], cb[:, t, :], ACT.Sigmoid, bias=par_col(LCB0 + t), scale=par_col(LCG0 + t)).then_inc(S["b_sig"], 1)

            def pool_scales(c):
                for t in range(TP):
                    wait(act, "pool_y_ready", c * TP + (t + 1))
                    A.activation(yT[:, 2 * TA + t, :], psum[6 + t][:], ACT.Copy, scale=par_col(PS0 + t)).then_inc(S["yc_done"], 1)

            def norm_in(c, tiles=range(TPC)):
                for i in tiles:
                    wait(act, "ln_stat", c + 1)
                    A.activation(xin[:, i, :], xin[:, i, :], ACT.Identity, bias=nmr[:, 0, i:i + 1], scale=rstd[:, 0, i:i + 1]).then_inc(S["norm1"], 1)

            def store_h(c):
                for i in range(TPC):
                    wait(act, "h_ready", c * TPC + (i + 1), alone="act")
                    A.dma_start(h_dram[bass.ds(c * CHUNK + i * P, P), :], xin[:, i, :]).then_inc(S["h_st"], 16)

            def store_h2(c, i):
                wait(act, "h2_ready", c * TPC + (i + 1), alone="act")
                A.dma_start(h2_dram[bass.ds(c * CHUNK + i * P, P), :], res[:, i, :]).then_inc(S[f"h2_st{i}"], 16)

            def norm_mix(c, i):
                wait(act, "mix_stat", c * TPC + (i + 1))
                A.activation(res[:, i, :], res[:, i, :], ACT.Identity, bias=nmr[:, 1, i:i + 1], scale=rstd[:, 1, i:i + 1]).then_inc(S["norm2"], 1)

            def hT_evac(c, fill):
                for j in range(KD):
                    if j % 2 == 0:
                        wait(act, "tA_ready", fill + (j // 2 + 1))
                        A.activation(hT_hi[:, j, :] if j < KS else hT[:, j - KS, :], psum[2][:], ACT.Copy).then_inc(S["tA_evac"], 1)
                    elif j < KS:
                        wait(act, "tB_ready", fill + (j // 2 + 1))
                        A.activation(hT_hi[:, j, :], psum[3][:], ACT.Copy).then_inc(S["tB_high"], 1)

            def split_win(c, m):
                wait(act, f"win_ld{m % RING}", (c * ring_uses[m % RING] + (m // RING + 1)) * 16)
                wait(act, "z_ready", c * NZ + (m - 1 if m >= 2 else -m))
                A.activation(win_hi[:, m % 2], win[m % RING][:, 0:KS, :], ACT.Copy).then_inc(S["win_hi_done"], 1)

            def h2T_low(c, i, fill):
                store_h2(c, i)
                wait(act, "products", NC * NPAIR if isinstance(c, int) else (c + 2) * NPAIR)
                wait(act, "tA_ready", fill + 1)
                wait(act, "logits_ready", c * TPC + i)
                A.activation(h2T[:, 0:4, :], psum[2][:].rearrange("p (k n) -> p k n", k=4), ACT.Copy).then_inc(S["tA_evac"], 1)
                wait(act, "logits_ready", c * TPC + (i + 1))
                A.activation(lg[:, bass.ds(c * TPC + i, 1), :].rearrange("p o n -> p (o n)"), psum[0][:, 0:E], ACT.Copy).then_inc(S["logits_evac"], 1)

            def window(c, conv):
                split_win(c, 0)
                split_win(c, 1)
                for m in range(NZ):
                    z_copy(c, m)
                    if m + 2 < NZ:
                        split_win(c, m + 2)
                    if NORM_AT <= m < NORM_AT + TPC:
                        norm_in(c + 1, [m - NORM_AT])
                    if conv and m == 6:
                        squares(c - 1)
                    if conv and m == 9:
                        conv_b_sigmoid(c - 1)
                    if conv and m == 12:
                        pool_scales(c - 1)
                store_h(c + 1)

            def mix_and_route(c, first, transposes):
                norm_mix(c, 0)
                norm_mix(c, 1)
                h2T_low(c, 0, first)
                norm_mix(c, 2)
                h2T_low(c, 1, first + 1)
                norm_mix(c, 3)
                if transposes:
                    hT_evac(c + 2, first + 2)
                after = first + (6 if transposes else 2)
                h2T_low(c, 2, after)
                h2T_low(c, 3, after + 1)

            for i in range(TPC):
                A.dma_start(credit_dram[i:i + 1, :], rows[i:i + 1, :]).then_inc(S[f"h2_st{i}"], CREDIT[f"h2_st{i}"])
            act.sem_inc(S["f_norm"], CREDIT["f_norm"])
            act.sem_inc(S["norm2"], CREDIT["norm2"])
            act.sem_inc(S["logits_evac"], CREDIT["logits_evac"])
            norm_in(0)
            hT_evac(0, 0)
            store_h(0)
            window(0, False)
            hT_evac(1, 4)
            act.wait_ge(S["const_ld"], 16 * N_CONST)
            with act.Fori(1, NC) as c:
                window(c, True)
                mix_and_route(c - 1, c * 8, True)
            squares(NC - 1)
            conv_b_sigmoid(NC - 1)
            pool_scales(NC - 1)
            mix_and_route(NC - 1, 8 * NC, False)

            act.wait_ge(S["exp_in"], 1)
            A.activation(pr[:], lr[:], ACT.Exp).then_inc(S["exp_out"], 1)

            def split_high(e, p, after):
                wait(act, f"piece_ld{p}", e * 16 + 16)
                if after is not None:
                    wait(act, ("g_ready", "u_ready", "yp_ready")[p // 2], after * 2 if p >= 4 else after)
                A.activation(w_hi[p][:], piece[p][:], ACT.Copy).then_inc(S["w_hi_done"], 1)

            def xT_high(j, half):
                wait(act, ("x1_ready", "x2_ready")[half], j + 1)
                A.activation(xT_hi[:, 4 * half:4 * half + 4, :], psum[2 + half][:].rearrange("p (k n) -> p k n", k=4),
                             ACT.Copy).then_inc(S["xh_done"], 1)

            def result(j, half):
                wait(act, "yp_ready", 2 * j + half + 1)
                wait(act, "y_st", j * 16 + 48)
                A.activation(ysb[:, half * 512:(half + 1) * 512], psum[5 + half][:], ACT.Copy).then_inc(S["ysb_done"], 1)

            def expert_block(j, e):
                wait(act, "g_ready", j + 1)
                wait(act, "hh_ready", 2 * j)
                A.activation(sig[:], psum[0][:], ACT.Sigmoid).then_inc(S["sig_ready"], 1)
                if e is not None:
                    split_high(e, 0, j + 1)
                    split_high(e, 1, j + 1)
                wait(act, "u_ready", j + 1)
                xT_high(j + 1, 0)
                wait(act, "yp_ready", j * 2)
                for half in range(2):
                    wait(act, "hht_ready", 2 * j + (half + 1))
                    A.activation(hhT_hi[:, 2 * half:2 * half + 2, :],
                                 psum[4 if half == 0 else 7][:, half * 256:half * 256 + 256].rearrange("p (k n) -> p k n", k=2),
                                 ACT.Copy).then_inc(S["hhth_done"], 1)
                xT_high(j + 1, 1)
                if e is not None:
                    split_high(e, 2, j + 1)
                result(j, 0)
                if e is not None:
                    split_high(e, 3, j + 1)
                result(j, 1)
                if e is not None:
                    split_high(e, 4, j + 1)
                    split_high(e, 5, j + 1)

            act.sem_inc(S["ysb_done"], CREDIT["ysb_done"])
            for p in range(PIECES):
                split_high(0, p, None)
            act.wait_ge(S["list_st"], 16 * 2 * NT)
            act.wait_ge(S["blocks_ready"], 1)
            xT_high(0, 0)
            xT_high(0, 1)
            with act.Fori(0, E - 1) as e:
                n = act.value_load(blocks_i[0:1, bass.ds(e, 1)], min_val=1, max_val=MAXB)
                first = act.value_load(blocks_i[0:1, bass.ds(e + E, 1)], min_val=0, max_val=E + MAXB * 2)
                with act.If(n > 1):
                    with act.Fori(0, n - 1) as b:
                        expert_block(first + b, None)
                last = act.value_load(blocks_i[0:1, bass.ds(e + (2 * E + 1), 1)], min_val=0, max_val=E + MAXB * 2)
                expert_block(last, e + 1)
            n = act.value_load(blocks_i[0:1, E - 1:E], min_val=1, max_val=MAXB)
            first = act.value_load(blocks_i[0:1, 2 * E - 1:2 * E], min_val=0, max_val=E + MAXB * 2)
            with act.Fori(0, n) as b:
                expert_block(first + b, None)

            act.wait_ge(S["experts_done"], 1)

            A.activation(alpha_d[:], ident, ACT.Copy, scale=ALPHA).then_inc(S["f_alpha"], 1)

            def diagonals(i):
                wait(act, "f_sum", i - 3)
                for k in range(2):
                    A.activation(dg[:, i % 4, k, :], ident, ACT.Copy, scale=gates[:, k, i:i + 1]).then_inc(S["f_diag"], 1)

            def norm_last(i):
                s = i % NF
                wait(act, "f_stat", i // 2 + 1)
                wait(act, "f_sum", i + 1)
                if i >= NF:
                    act.wait_ge(S[f"o_st{s}"], i // NF * 16)
                for half in range(2):
                    A.activation(fr[:, s, half * 512:(half + 1) * 512], psum[2 * (s % 4) + half][:], ACT.Identity,
                                 bias=frs[:, 1, s:s + 1], scale=frs[:, 0, s:s + 1]).then_inc(S["f_norm"], 1)

            for i in range(4):
                diagonals(i)
            for i in range(NT):
                norm_last(i)
                if i + 4 < NT:
                    diagonals(i + 4)

        @block.vector
        def _(dve):
            def ln_in_stats(c):
                ch = Chain(dve, "ln_steps", c * K_LN)
                wait(dve, "x_ld", (c + 1) * (16 * TPC))
                wait(dve, "norm1", c * TPC)
                for i in range(TPC):
                    for half in range(2):
                        n = ch.open(V.bn_stats(bst[:, 6 * half:6 * half + 6], xin[:, i, half * 512:(half + 1) * 512]))
                    ch.until(n, alone="dve")
                    ch.step(V.bn_aggr(mv[:, 0, i, :], bst[:]))
                rsqrt(ch, rstd[:, 0, :], nwv[:], nwt[:], mv[:, 0, :, 1])
                assert ch.n == K_LN
                V.scalar_tensor_tensor(nmr[:, 0, :], mv[:, 0, :, 0], -1.0, rstd[:, 0, :], ALU.mult, ALU.mult).then_inc(S["ln_stat"], 1)

            def gain_in(c):
                for i in range(TPC):
                    wait(dve, "norm1", c * TPC + (i + 1))
                    V.tensor_tensor(xin[:, i, :], xin[:, i, :], rowp[:, 0, :], ALU.mult).then_inc(S["scaled1"], 1)

            def hT_evac(c, fill):
                for j in range(KD):
                    if j < KS:
                        if j % 2 == 0:
                            wait(dve, "tA_evac", fill + (j // 2 + 1))
                        else:
                            wait(dve, "tB_high", c * KS_ODD + (j // 2 + 1))
                        V.tensor_tensor(hT_lo[:, j, :], psum[2 + j % 2][:], hT_hi[:, j, :].bitcast(F32),
                                        ALU.subtract).then_inc(S[("tA_low", "tB_evac")[j % 2]], 1)
                    elif j % 2 == 1:
                        wait(dve, "tB_ready", fill + (j // 2 + 1))
                        V.tensor_copy(hT[:, j - KS, :], psum[3][:]).then_inc(S["tB_evac"], 1)

            def h2T_high(c, i, fill):
                wait(dve, "tB_ready", fill + 1)
                wait(dve, "logits_ready", c * TPC + i)
                wait(dve, "products", NC * NPAIR if isinstance(c, int) else (c + 2) * NPAIR)
                V.tensor_copy(h2T[:, 4:8, :], psum[3][:].rearrange("p (k n) -> p k n", k=4)).then_inc(S["tB_evac"], 1)

            def conv_b(c, taps):
                ch = Chain(dve, "conv_b_steps", c * K_CONV)
                ch.n = taps[0] * TA
                if taps[0] == 0:
                    wait(dve, "products", c * NPAIR + TA)
                    wait(dve, "halos", c * 3 + 1)
                    wait(dve, "y_done", c * TA)
                for j in taps:
                    for t in range(TA):
                        src = vbuf[:, t, j:j + CHUNK]
                        w = par_col(CB0 + t * KB + j)
                        if j == 0:
                            ch.open(V.tensor_scalar(cb[:, t, :], src, w, par_col(CBB0 + t), ALU.mult, ALU.add))
                        else:
                            ch.until(ch.n - TA + 1 if j < KB - 1 else ch.n - TA + 1 + t)
                            tap = V.scalar_tensor_tensor(cb[:, t, :], src, w, cb[:, t, :], ALU.mult, ALU.add)
                            if j < KB - 1:
                                ch.open(tap)
                            else:
                                tap.then_inc(S["conv_b_done"], 1)

            def conv_a(c):
                ch = Chain(dve, "conv_a_steps", c * K_CONVA)
                wait(dve, "products", c * NPAIR + NPAIR)
                wait(dve, "z_evac", c * NZ + 2 * NPAIR + TA)
                for j in range(KA):
                    for t in range(TA):
                        src = ubuf[:, t, j:j + CHUNK]
                        w = par_col(CA0 + t * KA + j)
                        if j == 0:
                            ch.open(V.tensor_scalar(yT[:, t, :], src, w, None, ALU.mult))
                        else:
                            ch.until(ch.n - TA + 1)
                            ch.open(V.scalar_tensor_tensor(yT[:, t, :], src, w, yT[:, t, :], ALU.mult, ALU.add))
                assert ch.n == K_CONVA
                ch.until(ch.n)
                for t in range(TA):
                    V.tensor_tensor(yT[:, t, :], yT[:, t, :], gb[:, t, :], ALU.mult).then_inc(S["conv_a_done"], 1)

            def pool_windows(c, t):
                ch = Chain(dve, "pool_steps", c * K_DPOOL)
                ch.n = t * K_DPOOL0
                wait(dve, "z_evac", c * NZ + NZ)
                wait(dve, "halos", c * 3 + 3)
                W = HALO + CHUNK
                lo, hi = slice(0, GROUP), slice(GROUP, P)
                u = lambda t, rows, a, b: pbuf[rows, t, a:b]
                al = slice(0, P)

                def finish(t, rows, sums):
                    inv = con_s[rows, WI0 + t:WI0 + t + 1]
                    tab = con_s[rows, bass.ds(c * (TP * 16) + (PT0 + t * 16), 16)]
                    ch.open(V.scalar_tensor_tensor(dp[rows, t, 16:], sums[rows, HALO + 16:W], inv, u(t, rows, HALO + 16, W), ALU.mult, ALU.subtract))
                    ch.step(V.tensor_tensor(dp[rows, t, 0:16], sums[rows, HALO:HALO + 16], tab, ALU.mult))
                    V.tensor_tensor(dp[rows, t, 0:16], dp[rows, t, 0:16], u(t, rows, HALO, HALO + 16),
                                    ALU.subtract).then_inc(S["pool_d_done"], 1)

                r0, r1 = rs[:, 0, :], rs[:, 1, :]
                ch.step(V.tensor_tensor(r0[:, 1:W], u(t, al, 1, W), u(t, al, 0, W - 1), ALU.add))
                if t == 0:
                    ch.step(V.tensor_tensor(r1[hi, 3:W], r0[hi, 3:W], r0[hi, 1:W - 2], ALU.add))
                else:
                    ch.step(V.tensor_tensor(r1[:, 3:W], r0[:, 3:W], r0[:, 1:W - 2], ALU.add))
                    ch.step(V.tensor_tensor(r0[:, 7:W], r1[:, 7:W], r1[:, 3:W - 4], ALU.add))
                    ch.step(V.tensor_tensor(r1[hi, 15:W], r0[hi, 15:W], r0[hi, 7:W - 8], ALU.add))
                finish(t, lo, r0)
                finish(t, hi, r1)
                wait(dve, "pool_d_done", c * 4 + 2 * t + 2)
                assert ch.n == (K_DPOOL0, K_DPOOL)[t], ch.n

            def centre(c):
                wait(dve, "mean_ready", c + 1)
                for t in range(TA):
                    V.tensor_tensor(cb[:, t, :], cb[:, t, :], psum[4][:], ALU.subtract).then_inc(S["centred"], 1)

            def conv_b_norm(c):
                ch = Chain(dve, "b_norm_steps", c * K_CLN)
                wait(dve, "var_ready", c + 1)
                rsqrt(ch, rs[:, 0, 0:CHUNK], rs[:, 1, 0:CHUNK], rt, psum[5][:])
                wait(dve, "centred", c * TA + TA)
                for t in range(TA):
                    V.tensor_tensor(cb[:, t, :], cb[:, t, :], rs[:, 0, 0:CHUNK], ALU.mult).then_inc(S["b_norm"], 1)
                for t in range(TA):
                    wait(dve, "b_sig", c * TA + (t + 1))
                    ch.open(V.tensor_scalar(cb[:, t, :], cb[:, t, :], par_col(LCG0 + t), par_col(LCB0 + t), ALU.mult, ALU.add))
                assert ch.n == K_CLN, ch.n
                ch.until(ch.n)
                for t in range(TA):
                    V.tensor_tensor(yT[:, TA + t, :], cb[:, t, :], sq[:, t, :], ALU.mult).then_inc(S["y_done"], 1)

            def mix_stats(c, i):
                ch = Chain(dve, "mix_steps", (c * TPC + i) * K_MIX)
                r = res[:, i, :]
                wait(dve, "mix_ready", c * TPC + (i + 1))
                wait(dve, f"hres_ld{i}", c * 16 + 16)
                for half in range(2):
                    cols = slice(half * 512, (half + 1) * 512)
                    V.scalar_tensor_tensor(r[:, cols], r[:, cols], ALPHA, psum[4 + 2 * (i % 2) + half][:],
                                           ALU.mult, ALU.add).then_inc(S["mix_taken"], 1)
                wait(dve, "mix_taken", (c * TPC + (i + 1)) * 2)
                wait(dve, "norm2", c * TPC)
                for half in range(2):
                    ch.open(V.bn_stats(bst[:, 6 * half:6 * half + 6], r[:, half * 512:(half + 1) * 512]))
                ch.until(ch.n, alone="dve")
                ch.step(V.bn_aggr(mv[:, 1, i, :], bst[:]))
                rsqrt(ch, rstd[:, 1, i:i + 1], nwv[:, 0:1], nwt[:, 0:1], mv[:, 1, i, 1:2])
                assert ch.n == K_MIX
                V.scalar_tensor_tensor(nmr[:, 1, i:i + 1], mv[:, 1, i, 0:1], -1.0, rstd[:, 1, i:i + 1],
                                       ALU.mult, ALU.mult).then_inc(S["mix_stat"], 1)

            def convolutions(c):
                wait(dve, "b_norm", c * TA)
                pool_windows(c, 0)
                centre(c)
                pool_windows(c, 1)
                conv_b_norm(c)

            def mix_and_route(c, first, transposes):
                def early(i):
                    if transposes:
                        conv_b(c + 1, range(EARLY_AT[i], EARLY_AT[i + 1]))

                early(0)
                mix_stats(c, 0)
                early(1)
                mix_stats(c, 1)
                early(2)
                h2T_high(c, 0, first)
                mix_stats(c, 2)
                early(3)
                h2T_high(c, 1, first + 1)
                mix_stats(c, 3)
                if transposes:
                    hT_evac(c + 2, first + 2)
                after = first + (6 if transposes else 2)
                h2T_high(c, 2, after)
                h2T_high(c, 3, after + 1)

            dve.sem_inc(S["conv_a_done"], CREDIT["conv_a_done"])
            dve.sem_inc(S["conv_b_done"], CREDIT["conv_b_done"])
            dve.sem_inc(S["pool_d_done"], CREDIT["pool_d_done"])
            dve.sem_inc(S["mix_taken"], CREDIT["mix_taken"])
            dve.sem_inc(S["b_norm"], CREDIT["b_norm"])
            V.memset(pw[:], 0.0).then_inc(S["set_up"], 1)
            V.memset(onesd[:], 1.0 / DA).then_inc(S["set_up"], 1)
            ln_in_stats(0)
            dve.wait_ge(S["first_ld"], 16 * N_FIRST)
            gain_in(0)
            hT_evac(0, 0)
            ln_in_stats(1)
            gain_in(1)
            dve.wait_ge(S["first_ld"], 16 * N_FIRST)
            dve.wait_ge(S["const_ld"], 16 * N_CONST)
            conv_b(0, range(20))
            hT_evac(1, 4)
            conv_b(0, range(20, EARLY))
            with dve.Fori(1, NC) as c:
                conv_b(c - 1, range(EARLY, KB))
                conv_a(c - 1)
                ln_in_stats(c + 1)
                convolutions(c - 1)
                gain_in(c + 1)
                mix_and_route(c - 1, c * 8, True)
            conv_b(NC - 1, range(EARLY, KB))
            conv_a(NC - 1)
            convolutions(NC - 1)
            mix_and_route(NC - 1, 8 * NC, False)

            ch = Chain(dve, "route_steps", 0)
            ie = con_s[:, IE0:IE0 + E].unsqueeze(1).to_broadcast([P, NT, E])
            ig = con_s[:, IG0:IG0 + G].unsqueeze(1).to_broadcast([P, NT, G])
            i4 = con_s[:, IG0:IG0 + EG].unsqueeze(1).to_broadcast([P, NT, EG])
            wide = lambda a, n: a.unsqueeze(2).to_broadcast([P, NT, n])
            dve.wait_ge(S["logits_evac"], NT + CREDIT["logits_evac"])
            dve.wait_ge(S["z_ready"], NC * NZ)
            dve.wait_ge(S["h2_ready"], NT)
            for i in range(TPC):
                wait(dve, f"h2_st{i}", NC * 16)
            ch.step(V.memset(onesr[:], 1.0))
            ch.step(V.tensor_tensor(lr[:], lg[:], rb[:].unsqueeze(1).to_broadcast([P, NT, E]), ALU.add))
            ch.step(V.tensor_reduce(rsm[:], lr[:], AXX, ALU.max))
            V.tensor_tensor(lr[:], lr[:], wide(rsm[:], E), ALU.subtract).then_inc(S["exp_in"], 1)
            dve.wait_ge(S["exp_out"], 1)
            ch.step(V.tensor_reduce(rsm[:], pr[:], AXX, ALU.add))
            ch.step(V.reciprocal(rsm[:], rsm[:]))
            ch.step(V.tensor_tensor(pr[:], pr[:], wide(rsm[:], E), ALU.mult))
            p4 = pr[:].rearrange("p t (g k) -> p t g k", k=EG)
            for t0 in range(0, NT, 4):
                tt = slice(t0, t0 + 4)
                for n, (a, b) in enumerate(((0, 1), (0, 2), (0, 3), (1, 2), (1, 3), (2, 3))):
                    ch.open(V.tensor_tensor(pairs[:, tt, :, n], p4[:, tt, :, a], p4[:, tt, :, b], ALU.add))
            ch.until(ch.n)
            ch.step(V.tensor_reduce(gs[:], pairs[:], AXX, ALU.max))
            ch.step(V.tensor_reduce(gmx[:], gs[:], AXX, ALU.max))

            def first_index(value, peak, iota, n, out_):
                ch.step(V.tensor_tensor(value, value, wide(peak, n), ALU.is_equal))
                ch.step(V.tensor_scalar(value, value, -float(n), float(n), ALU.mult, ALU.add))
                ch.step(V.tensor_tensor(value, value, iota, ALU.add))
                ch.step(V.tensor_reduce(out_, value, AXX, ALU.min))

            first_index(gs[:], gmx[:], ig, G, gmx[:])
            ch.step(V.tensor_tensor(goh[:], ig, wide(gmx[:], G), ALU.is_equal))
            for k in range(EG):
                ch.open(V.tensor_tensor(bigm[:, :, k * G:(k + 1) * G], p4[:, :, :, k], goh[:], ALU.mult))
            ch.until(ch.n)
            ch.step(V.tensor_reduce(ing[:], bigm[:].rearrange("p t (k g) -> p t k g", g=G), AXX, ALU.add))
            for k in range(2):
                ch.step(V.tensor_reduce(top[:, k, :], ing[:], AXX, ALU.max))
                ch.step(V.tensor_copy(toh[:], ing[:]))
                first_index(toh[:], top[:, k, :], i4, EG, tix[:, k, :])
                if k == 0:
                    ch.step(V.tensor_tensor(toh[:], i4, wide(tix[:, k, :], EG), ALU.is_equal))
                    ch.step(V.scalar_tensor_tensor(ing[:], toh[:], -2.0, ing[:], ALU.mult, ALU.add))
                ch.step(V.scalar_tensor_tensor(tix[:, k, :], gmx[:], float(EG), tix[:, k, :], ALU.mult, ALU.add))
                ch.step(V.tensor_tensor(oh[:, k], ie, wide(tix[:, k, :], E), ALU.is_equal))
            ch.step(V.tensor_tensor(rsm[:], top[:, 0, :], top[:, 1, :], ALU.add))
            ch.step(V.reciprocal(rsm[:], rsm[:]))
            for k in range(2):
                ch.open(V.tensor_tensor(gates[:, k, :], top[:, k, :], rsm[:], ALU.mult))
            ch.step(V.memset(base[:, 0, :], 0.0))
            V.tensor_tensor(asg[:], oh[:, 0], oh[:, 1], ALU.add).then_inc(S["assigned"], 1)
            dve.wait_ge(S["prefix_ready"], 2)
            for t in range(NT):
                ch.step(V.tensor_tensor(base[:, t + 1, :], base[:, t, :], psum[7][:, t * E:(t + 1) * E], ALU.add))
            ch.step(V.tensor_tensor(slot[:], base[:, 0:NT, :], psum[6][:].rearrange("p (t e) -> p t e", e=E), ALU.add))
            for k in range(2):
                ch.step(V.tensor_tensor(bigm[:], oh[:, k], slot[:], ALU.mult))
                ch.step(V.tensor_reduce(rank_f[:, k, :], bigm[:], AXX, ALU.add))
                ch.step(V.tensor_tensor(cmpr[:], wide(rank_f[:, k, :], MAXB - 1),
                                        con_s[:, TH0 + 1:TH0 + MAXB].unsqueeze(1).to_broadcast([P, NT, MAXB - 1]), ALU.is_ge))
                ch.step(V.tensor_reduce(blk_t[:, k, :], cmpr[:], AXX, ALU.add))
                ch.step(V.tensor_scalar(slot_f[:, k, :], rank_f[:, k, :], float(E * MAXB), None, ALU.mult))
                ch.step(V.scalar_tensor_tensor(slot_f[:, k, :], tix[:, k, :], float(MAXB), slot_f[:, k, :], ALU.mult, ALU.add))
                ch.step(V.scalar_tensor_tensor(slot_f[:, k, :], blk_t[:, k, :], float(1 - P * E * MAXB), slot_f[:, k, :], ALU.mult, ALU.add))
                V.tensor_copy(slot_i[:, k, :], slot_f[:, k, :]).then_inc(S["slots_ready"], 1)
            ch.step(V.tensor_tensor(cmpb[:], base[:, NT, :].unsqueeze(2).to_broadcast([P, E, MAXB]),
                                    con_s[:, TH0:TH0 + MAXB].unsqueeze(1).to_broadcast([P, E, MAXB]), ALU.is_gt))
            ch.step(V.tensor_reduce(blk_f[:, 0:E], cmpb[:], AXX, ALU.add))
            ch.step(V.tensor_scalar(blk_f[:, 0:E], blk_f[:, 0:E], 1.0, None, ALU.max))
            ch.step(V.memset(blk_f[:, E:E + 1], 0.0))
            ch.step(V.tensor_tensor_scan(blk_f[:, E + 1:2 * E + 1], blk_f[:, 0:E], blk_f[:, 0:E], 0.0, ALU.add, ALU.bypass))
            ch.step(V.tensor_scalar(blk_f[:, 2 * E + 1:], blk_f[:, E + 1:2 * E + 1], -1.0, None, ALU.add))
            V.tensor_copy(blocks_i[:], blk_f[:]).then_inc(S["blocks_ready"], 1)

            def split_low(e, p):
                wait(dve, "w_hi_done", e * PIECES + (p + 1))
                V.tensor_tensor(w_lo[p][:], piece[p][:], w_hi[p][:].bitcast(F32), ALU.subtract).then_inc(S["w_lo_done"], 1)

            def xT_low(j, half):
                wait(dve, "xh_done", 2 * j + half + 1)
                V.tensor_tensor(xT_lo[:, 4 * half:4 * half + 4, :], psum[2 + half][:].rearrange("p (k n) -> p k n", k=4),
                                xT_hi[:, 4 * half:4 * half + 4, :].bitcast(F32), ALU.subtract).then_inc(S["xl_done"], 1)

            def expert_block(j, e):
                wait(dve, "sig_ready", j + 1)
                wait(dve, "hht_ready", 2 * j)
                V.tensor_tensor(hh[:], psum[0][:], sig[:], ALU.mult).then_inc(S["gated"], 1)
                wait(dve, "gated", j + 1)
                wait(dve, "u_ready", j + 1)
                for half in range(2):
                    cols = slice(half * 256, half * 256 + 256)
                    V.tensor_tensor(hh[:, cols], psum[1][:, cols], hh[:, cols], ALU.mult).then_inc(S["hh_ready"], 1)
                xT_low(j + 1, 0)
                for half in range(2):
                    ks = slice(2 * half, 2 * half + 2)
                    wait(dve, "hhth_done", 2 * j + (half + 1))
                    V.tensor_tensor(hhT_lo[:, ks, :], psum[4 if half == 0 else 7][:, half * 256:half * 256 + 256].rearrange("p (k n) -> p k n", k=2),
                                    hhT_hi[:, ks, :].bitcast(F32), ALU.subtract).then_inc(S["hhtl_done"], 1)
                xT_low(j + 1, 1)
                if e is not None:
                    for p in range(PIECES):
                        split_low(e, p)

            dve.sem_inc(S["hh_ready"], CREDIT["hh_ready"])
            for p in range(PIECES):
                split_low(0, p)
            dve.wait_ge(S["list_st"], 16 * 2 * NT)
            dve.wait_ge(S["blocks_ready"], 1)
            xT_low(0, 0)
            xT_low(0, 1)
            with dve.Fori(0, E - 1) as e:
                n = dve.value_load(blocks_i[0:1, bass.ds(e, 1)], min_val=1, max_val=MAXB)
                first = dve.value_load(blocks_i[0:1, bass.ds(e + E, 1)], min_val=0, max_val=E + MAXB * 2)
                with dve.If(n > 1):
                    with dve.Fori(0, n - 1) as b:
                        expert_block(first + b, None)
                last = dve.value_load(blocks_i[0:1, bass.ds(e + (2 * E + 1), 1)], min_val=0, max_val=E + MAXB * 2)
                expert_block(last, e + 1)
            n = dve.value_load(blocks_i[0:1, E - 1:E], min_val=1, max_val=MAXB)
            first = dve.value_load(blocks_i[0:1, 2 * E - 1:2 * E], min_val=0, max_val=E + MAXB * 2)
            with dve.Fori(0, n) as b:
                expert_block(first + b, None)

            dve.wait_ge(S["experts_done"], 1)
            K_FIN = 2 * (2 + 1) + NEWTON

            def combine(q, s):
                i = q * NF + s
                ch = Chain(dve, "f_steps", (q * (NF // 2) + s // 2) * K_FIN)
                wait(dve, "f_norm", ((q - 1) * NF + (s + 2)) * 2)
                for n in range(2):
                    wait(dve, "f_sum", i + (n + 1))
                    for half in range(2):
                        ch.open(V.bn_stats(fst[:, s + n, 6 * half:6 * half + 6], psum[2 * ((s + n) % 4) + half][:]))
                    ch.until(ch.n, alone="dve")
                    ch.step(V.bn_aggr(fmv[:, s + n, :], fst[:, s + n, :]))
                two = slice(s, s + 2)
                rsqrt(ch, frs[:, 0, two], frs[:, 2, two], frs[:, 3, two], fmv[:, two, 1])
                assert ch.n == K_FIN, ch.n
                V.scalar_tensor_tensor(frs[:, 1, two], fmv[:, two, 0], -1.0, frs[:, 0, two],
                                       ALU.mult, ALU.mult).then_inc(S["f_stat"], 1)

            def gain_last(q, s):
                for n in range(2):
                    wait(dve, "f_norm", (q * NF + (s + n + 1)) * 2)
                    wait(dve, "row_ld", 32)
                    V.tensor_tensor(fr[:, s + n, :], fr[:, s + n, :], frow[:, 0, :], ALU.mult).then_inc(S["f_scaled"], 1)

            with dve.Fori(0, NT // NF) as q:
                combine(q, 0)
                for s in range(0, NF, 2):
                    if s + 2 < NF:
                        combine(q, s + 2)
                    gain_last(q, s)

        @block.gpsimd
        def _(pool):
            def halo(buf, w, c, readers, done, n):
                if isinstance(c, int) and c == 0:
                    Q.memset(buf[:, :, 0:w], 0.0).then_inc(S["halos"], 1)
                else:
                    wait(pool, readers, done, alone="pool")
                    Q.tensor_copy(buf[:, :, 0:w], buf[:, :, CHUNK:CHUNK + w]).then_inc(S["halos"], 1)
                    wait(pool, "halos", c * 3 + n, alone="pool")

            def product(c, p):
                wait(pool, "z_evac", c * NZ + (2 * p + 2), alone="pool")
                if p < TA:
                    to = vbuf[:, p, KB - 1:]
                else:
                    to = ubuf[:, p - TA, KA - 1:]
                Q.tensor_tensor(to, raw[:, 2 * (p % 2), :], raw[:, 2 * (p % 2) + 1, :], ALU.mult).then_inc(S["products"], 1)

            def affine_in(c, tiles=range(TPC)):
                for i in tiles:
                    wait(pool, "scaled1", c * TPC + (i + 1), alone="pool")
                    Q.tensor_tensor(xin[:, i, :], xin[:, i, :], rowp[:, 1, :], ALU.add).then_inc(S["h_ready"], 1)

            def affine_mix(c, i):
                wait(pool, "norm2", c * TPC + (i + 1), alone="pool")
                r = res[:, i, :]
                Q.tensor_tensor(r, r, rowp[:, 2, :], ALU.mult).then_inc(S["scaled2"], 1)
                wait(pool, "scaled2", c * TPC + (i + 1), alone="pool")
                Q.tensor_tensor(r, r, rowp[:, 3, :], ALU.add).then_inc(S["h2_ready"], 1)

            def split_win(c, m):
                wait(pool, "win_hi_done", c * NZ + (m + 1), alone="pool")
                Q.tensor_tensor(win_lo[:, m % 2], win[m % RING][:, 0:KS, :], win_hi[:, m % 2].bitcast(F32),
                                ALU.subtract).then_inc(S["win_lo_done"], 1)

            def window(c):
                split_win(c, 0)
                split_win(c, 1)
                halo(vbuf, KB - 1, c, "conv_b_done", c * TA, 1)
                for m in range(NZ - 2):
                    split_win(c, m + 2)
                    if m % 2 == 1 and m // 2 < NPAIR:
                        if m // 2 == TA:
                            halo(ubuf, KA - 1, c, "conv_a_done", c * TA, 2)
                        product(c, m // 2)
                    if m == 2 * TA + 4:
                        halo(pbuf, HALO, c, "pool_d_done", c * 4, 3)
                    if m >= NZ - 2 - TPC:
                        affine_in(c + 1, [m - (NZ - 2 - TPC)])

            Q.memset(pad[:, :, 0:1], 0).then_inc(S["pads_set"], 1)
            Q.memset(pad[:, :, 1:2], SKIP).then_inc(S["pads_set"], 1)
            pool.wait_ge(S["first_ld"], 16 * N_FIRST)
            affine_in(0)
            window(0)
            pool.wait_ge(S["const_ld"], 16 * N_CONST)
            with pool.Fori(1, NC) as c:
                window(c)
                for i in range(TPC):
                    affine_mix(c - 1, i)
            for i in range(TPC):
                affine_mix(NC - 1, i)

            pool.wait_ge(S["list_pad_st"], 16 * (PADS // P))
            for k in range(2):
                pool.wait_ge(S["slots_ready"], k + 1)
                for t in range(NT):
                    Q.indirect_dma_start(out=list_dram, out_offset=bass.IndirectOffsetOnAxis(ap=slot_i[:, k, t:t + 1], axis=0),
                                         in_=entry_s[:, t, k, :], in_offset=None).then_inc(S["list_st"], 16)
            pool.wait_ge(S["list_st"], 16 * 2 * NT)

            def gather(j, source):
                wait(pool, "x2_ready", j, alone="pool")
                if source is not None:
                    wait(pool, "idx_copied", j * 4 + 4, alone="pool")
                    Q.tensor_copy(idx_g[:], source).then_inc(S["idx_copied"], 1)
                    wait(pool, "idx_copied", j * 4 + 5, alone="pool")
                Q.indirect_dma_start(out=xg[:], out_offset=None, in_=h2_dram,
                                     in_offset=bass.IndirectOffsetOnAxis(ap=idx_g[:, 0:1], axis=0)).then_inc(S["xg_ld"], 16)

            def rows_out():
                Q.indirect_dma_start(out=y_dram, out_offset=bass.IndirectOffsetOnAxis(ap=idx_s[:, 1:2], axis=0),
                                     in_=ysb[:], in_offset=None, bounds_check=SKIP - 1, oob_is_err=False).then_inc(S["y_st"], 16)

            def shift(j, n):
                wait(pool, "y_st", (j + 1) * 16, alone="pool")
                Q.tensor_copy(idx_s[:], idx_h[:, 1, :]).then_inc(S["idx_copied"], 1)
                wait(pool, "idx_copied", n + 1, alone="pool")
                Q.tensor_copy(idx_h[:, 1, :], idx_h[:, 0, :]).then_inc(S["idx_copied"], 1)
                wait(pool, "idx_copied", n + 2, alone="pool")

            def scatter(j):
                wait(pool, "ysb_done", 2 * (j - 1), alone="pool")
                rows_out()

            pool.wait_ge(S["blocks_ready"], 1)
            Q.dma_start(idx_all[:], list_dram.rearrange("(p e b) c -> p e b c", p=P, e=E)).then_inc(S["idx_ld"], 16)
            Q.memset(idx_s[:], SKIP).then_inc(S["idx_copied"], 1)
            Q.memset(idx_h[:], SKIP).then_inc(S["idx_copied"], 1)
            Q.memset(ysb[:], 0.0).then_inc(S["idx_copied"], 1)
            pool.wait_ge(S["idx_copied"], 3)
            rows_out()
            pool.wait_ge(S["idx_ld"], 16)
            Q.tensor_copy(idx_g[:], idx_all[:, 0, 0, :]).then_inc(S["idx_copied"], 1)
            pool.wait_ge(S["idx_copied"], 4)
            with pool.Fori(0, E) as e:
                n = pool.value_load(blocks_i[0:1, bass.ds(e, 1)], min_val=1, max_val=MAXB)
                first = pool.value_load(blocks_i[0:1, bass.ds(e + E, 1)], min_val=0, max_val=E + MAXB * 2)
                with pool.Fori(0, n) as b:
                    j = first + b
                    gather(j, idx_all[:, bass.ds(e, 1), bass.ds(b, 1), :].rearrange("p o q c -> p (o q c)"))
                    shift(j, j * 4 + 5)
                    Q.tensor_copy(idx_h[:, 0, :], idx_g[:]).then_inc(S["idx_copied"], 1)
                    scatter(j)
            total = pool.value_load(blocks_i[0:1, 2 * E:2 * E + 1], min_val=E, max_val=E + MAXB * 2)
            gather(total, None)
            shift(total, total * 4 + 4)
            scatter(total)
            shift(total + 1, total * 4 + 6)
            scatter(total + 1)
            wait(pool, "y_st", total * 16 + 48, alone="pool")
            wait(pool, "xg_ld", total * 16 + 16, alone="pool")
            wait(pool, "xh_done", total * 2 + 2, alone="pool")
            wait(pool, "xl_done", total * 2 + 2, alone="pool")
            Q.memset(onepool[:], 0.0).then_inc(S["experts_done"], 1)

            pool.wait_ge(S["row_ld"], 32)
            with pool.Fori(0, NT // NF) as q:
                for s in range(NF):
                    wait(pool, "f_scaled", q * NF + (s + 1), alone="pool")
                    Q.tensor_tensor(fr[:, s, :], fr[:, s, :], frow[:, 1, :], ALU.add).then_inc(S["f_out"], 1)

    stack.close()


def kernel(x, ln_in_g, ln_in_b, router_w, router_b, w_in, conv_a_w, conv_b_w, conv_b_b, ln_conv_g, ln_conv_b,
           pool_w, pool_scale, w_out, ln_mix_g, ln_mix_b, w_gate, w_up, w_down, ln_ffn_g, ln_ffn_b):
    import concourse.bacc as bacc
    from concourse.bass_utils import run_bass_kernel_spmd

    a = lambda v: np.ascontiguousarray(v)
    con, entry = constants()
    taps = lambda w, n: np.asarray(w)[0].reshape(n, TA, P).transpose(2, 1, 0).reshape(P, TA * n)
    chan = lambda v: np.asarray(v)[0].reshape(-1, P).T
    rw = np.asarray(router_w).reshape(KD, P, E).transpose(1, 0, 2).reshape(P, KD * E)
    params = np.concatenate([taps(conv_a_w, KA), taps(conv_b_w, KB), chan(conv_b_b), chan(ln_conv_g),
                             chan(ln_conv_b), chan(pool_scale), rw], axis=1)
    rows = np.stack([np.asarray(v).reshape(D) for v in (ln_in_g, ln_in_b, ln_mix_g, ln_mix_b, ln_ffn_g, ln_ffn_b)])
    win = np.asarray(w_in)[0].reshape(KD, P, NZ, P).transpose(2, 1, 0, 3).reshape(NZ, P, KD * P)[z_order()]
    ins = {
        "x": a(np.asarray(x)[0]), "w_in": a(win), "w_out": a(np.asarray(w_out)[0]),
        "w_gate": a(np.asarray(w_gate)[0]), "w_up": a(np.asarray(w_up)[0]), "w_down": a(np.asarray(w_down)[0]),
        "pool_w": a(np.asarray(pool_w)[0]), "params": a(params), "rows": a(rows),
        "router_b": a(np.asarray(router_b).reshape(1, E)), "con": a(con), "entry": a(entry),
    }
    nc = bacc.Bacc("TRN2", target_bir_lowering=False, num_devices=1)
    args = {n: nc.dram_tensor(f"in_{n}", v.shape, mybir.dt.from_np(v.dtype), kind="ExternalInput").ap() for n, v in ins.items()}
    out = nc.dram_tensor("out_rows", (SEQ, D), F32, kind="ExternalOutput").ap()
    program(nc, out=out, **args)
    r = run_bass_kernel_spmd(nc, [{f"in_{n}": v for n, v in ins.items()}], core_ids=[0])
    return r.results[0]["out_rows"].reshape(1, SEQ, D)
```
